# Optimizing a Trainium2 kernel written in Bass

```python
import math
import jax, jax.numpy as jnp
from jax import lax
import numpy as np

D_MODEL = 1024
BATCH = 1
SEQ = 256
DEPTH = 2

N_META = 16
MLA_HEADS = 8
Q_LORA = 384
KV_LORA = 256
QK_NOPE = 64
QK_ROPE = 32
V_HEAD = 64
ROPE_THETA = 10000.0
Q_BLOCK = 128
HG_HEADS = 4
HG_KDIM = 128
HG_VDIM = 128
HG_CHUNK = 64
D_FF = 2816
EPS = 1e-6
NEG_BIG = -1e30
F_MIN = 1e-20

MLA_WIDTH = MLA_HEADS * V_HEAD
HG_FWIDTH = HG_HEADS * HG_KDIM
HG_WIDTH = HG_HEADS * HG_VDIM
IN_SPLITS = (Q_LORA, KV_LORA, QK_ROPE, HG_FWIDTH, HG_FWIDTH, HG_WIDTH, HG_WIDTH, D_MODEL, D_MODEL)
D_IN = sum(IN_SPLITS)


def rms_norm(x, w):
    xf = x.astype(jnp.float32)
    y = xf * lax.rsqrt(jnp.mean(xf * xf, axis=-1, keepdims=True) + EPS)
    return (y * w.astype(jnp.float32)).astype(x.dtype)

def split_cols(z, sizes):
    outs, start = [], 0
    for s in sizes:
        outs.append(z[..., start:start + s])
        start += s
    return outs

def swiglu(x, w_gu, w_down):
    gate, up = jnp.split(x @ w_gu, 2, axis=-1)
    return (jax.nn.silu(gate) * up) @ w_down

def rope(x, pos):
    half = x.shape[-1] // 2
    inv = ROPE_THETA ** (-jnp.arange(half, dtype=jnp.float32) / half)
    ang = pos.astype(jnp.float32)[:, None] * inv[None, :]
    cos = jnp.cos(ang)[:, None, :]
    sin = jnp.sin(ang)[:, None, :]
    x1 = x[..., :half].astype(jnp.float32)
    x2 = x[..., half:].astype(jnp.float32)
    return jnp.concatenate([x1 * cos - x2 * sin, x2 * cos + x1 * sin], axis=-1).astype(x.dtype)

def mla(c_q, c_kv, k_pe, pos, q_norm_w, kv_norm_w, w_uq, w_ukv):
    B, L, _ = c_q.shape
    H, DQK = MLA_HEADS, QK_NOPE + QK_ROPE
    q = (rms_norm(c_q, q_norm_w) @ w_uq).reshape(B, L, H, DQK)
    q = jnp.concatenate([q[..., :QK_NOPE], rope(q[..., QK_NOPE:], pos)], axis=-1)
    kv = (rms_norm(c_kv, kv_norm_w) @ w_ukv).reshape(B, L, H, QK_NOPE + V_HEAD)
    v = kv[..., QK_NOPE:]
    k_rot = rope(k_pe[:, :, None, :], pos)
    k = jnp.concatenate([kv[..., :QK_NOPE], jnp.broadcast_to(k_rot, (B, L, H, QK_ROPE))], axis=-1)
    scale = DQK ** -0.5
    n_blocks = -(-L // Q_BLOCK)
    pad = n_blocks * Q_BLOCK - L
    qb = jnp.pad(q, ((0, 0), (0, pad), (0, 0), (0, 0)))
    qb = qb.reshape(B, n_blocks, Q_BLOCK, H, DQK).transpose(1, 0, 2, 3, 4)
    k_pos = jnp.arange(L)

    def block(args):
        qi, blk = args
        s = jnp.einsum('bqhd,bkhd->bhqk', qi, k).astype(jnp.float32) * scale
        q_pos = blk * Q_BLOCK + jnp.arange(Q_BLOCK)
        s = jnp.where(k_pos[None, :] <= q_pos[:, None], s, NEG_BIG)
        p = jax.nn.softmax(s, axis=-1).astype(v.dtype)
        return jnp.einsum('bhqk,bkhd->bqhd', p, v)

    o = lax.map(block, (qb, jnp.arange(n_blocks)))
    o = o.transpose(1, 0, 2, 3, 4).reshape(B, n_blocks * Q_BLOCK, H * V_HEAD)
    return o[:, :L]

def hgrn2(q_in, f_in, i_in, g_in, lb, norm_w):
    B, L, _ = q_in.shape
    dt = q_in.dtype
    f32 = jnp.float32
    q = jax.nn.silu(q_in.astype(f32)).reshape(B, L, HG_HEADS, HG_KDIM)
    z = f_in.astype(f32).reshape(B, L, HG_HEADS, HG_KDIM)
    lbf = lb.astype(f32).reshape(HG_HEADS, HG_KDIM)
    f = lbf + (1.0 - lbf) * jax.nn.sigmoid(z)
    log_f = jnp.log(jnp.maximum(f, F_MIN))
    k = (1.0 - lbf) * jax.nn.sigmoid(-z)
    v = i_in.astype(f32).reshape(B, L, HG_HEADS, HG_VDIM)
    front = (-N_META) % HG_CHUNK

    def to_chunks(t):
        t = jnp.pad(t, ((0, 0), (front, 0), (0, 0), (0, 0)))
        n = t.shape[1] // HG_CHUNK
        return t.reshape(B, n, HG_CHUNK, HG_HEADS, t.shape[-1]).transpose(1, 0, 3, 2, 4)

    qc, kc, vc, gc = to_chunks(q), to_chunks(k), to_chunks(v), to_chunks(log_f)
    scale = HG_KDIM ** -0.5
    causal = jnp.tril(jnp.ones((HG_CHUNK, HG_CHUNK), dtype=bool))

    def step(S, inp):
        qt, kt, vt, gt = inp
        b = jnp.cumsum(gt, axis=2)
        diff = b[:, :, :, None, :] - b[:, :, None, :, :]
        decay = jnp.exp(jnp.where(causal[:, :, None], diff, NEG_BIG))
        attn = jnp.einsum('bhtk,bhtsk,bhsk->bhts', qt, decay, kt) * scale
        o = jnp.einsum('bhts,bhsv->bhtv', attn, vt) + \
            jnp.einsum('bhtk,bhkv->bhtv', qt * jnp.exp(b) * scale, S)
        b_last = b[:, :, -1:, :]
        S = jnp.exp(b_last[:, :, 0, :])[..., None] * S + \
            jnp.einsum('bhsk,bhsv->bhkv', kt * jnp.exp(b_last - b), vt)
        return S, o

    S0 = jnp.zeros((B, HG_HEADS, HG_KDIM, HG_VDIM), f32)
    _, o = lax.scan(step, S0, (qc, kc, vc, gc))
    n = o.shape[0]
    o = o.transpose(1, 0, 3, 2, 4).reshape(B, n * HG_CHUNK, HG_HEADS, HG_VDIM)[:, front:]
    o = o * lax.rsqrt(jnp.mean(o * o, axis=-1, keepdims=True) + EPS) * norm_w.astype(f32)
    gate = jax.nn.silu(g_in.astype(f32)).reshape(B, L, HG_HEADS, HG_VDIM)
    return (o * gate).reshape(B, L, HG_WIDTH).astype(dt)

def first_inputs(seed: int = 0) -> dict:
    key = jax.random.key(seed)
    ks = jax.random.split(key, 24)
    f32 = jnp.float32

    def nrm(k, shape, fan_in):
        return jax.random.normal(k, shape, f32) * (fan_in ** -0.5)

    def gain(k, shape):
        return 1.0 + 0.02 * jax.random.normal(k, shape, f32)

    return {
        "x": jax.random.normal(ks[0], (BATCH, SEQ, D_MODEL), f32),
        "meta_tokens": jax.random.normal(ks[1], (N_META, D_MODEL), f32),
        "ffn1_norm": gain(ks[2], (DEPTH, D_MODEL)),
        "ffn1_w_gu": nrm(ks[3], (DEPTH, D_MODEL, 2 * D_FF), D_MODEL),
        "ffn1_w_down": nrm(ks[4], (DEPTH, D_FF, D_MODEL), D_FF),
        "mix_norm": gain(ks[5], (DEPTH, D_MODEL)),
        "w_in": nrm(ks[6], (DEPTH, D_MODEL, D_IN), D_MODEL),
        "q_norm": gain(ks[7], (DEPTH, Q_LORA)),
        "kv_norm": gain(ks[8], (DEPTH, KV_LORA)),
        "w_uq": nrm(ks[9], (DEPTH, Q_LORA, MLA_HEADS * (QK_NOPE + QK_ROPE)), Q_LORA),
        "w_ukv": nrm(ks[10], (DEPTH, KV_LORA, MLA_HEADS * (QK_NOPE + V_HEAD)), KV_LORA),
        "hg_lb_raw": 0.5 * jax.random.normal(ks[11], (DEPTH, HG_FWIDTH), f32),
        "hg_norm": gain(ks[12], (DEPTH, HG_VDIM)),
        "w_proj_attn": nrm(ks[13], (DEPTH, MLA_WIDTH, D_MODEL), MLA_WIDTH),
        "w_proj_rec": nrm(ks[14], (DEPTH, HG_WIDTH, D_MODEL), HG_WIDTH),
        "w_out": nrm(ks[15], (DEPTH, D_MODEL, D_MODEL), D_MODEL),
        "ffn2_norm": gain(ks[16], (DEPTH, D_MODEL)),
        "ffn2_w_gu": nrm(ks[17], (DEPTH, D_MODEL, 2 * D_FF), D_MODEL),
        "ffn2_w_down": nrm(ks[18], (DEPTH, D_FF, D_MODEL), D_FF),
        "final_norm": gain(ks[19], (D_MODEL,)),
    }

def first_block(x, meta_tokens, ffn1_norm, ffn1_w_gu, ffn1_w_down, mix_norm, w_in, q_norm, kv_norm,
              w_uq, w_ukv, hg_lb_raw, hg_norm, w_proj_attn, w_proj_rec, w_out,
              ffn2_norm, ffn2_w_gu, ffn2_w_down, final_norm):
    B = x.shape[0]
    meta = jnp.broadcast_to(meta_tokens.astype(x.dtype)[None], (B, N_META, D_MODEL))
    h = jnp.concatenate([meta, x], axis=1)
    L = h.shape[1]
    pos = jnp.arange(L)
    p_lb = jax.nn.softmax(hg_lb_raw.astype(jnp.float32), axis=0)
    lbs = jnp.cumsum(p_lb, axis=0) - p_lb[0:1]
    for l in range(DEPTH):
        h = h + 0.5 * swiglu(rms_norm(h, ffn1_norm[l]), ffn1_w_gu[l], ffn1_w_down[l])
        u = rms_norm(h, mix_norm[l])
        c_q, c_kv, k_pe, hq, hf, hi, hg, ga, gb = split_cols(u @ w_in[l], IN_SPLITS)
        y_a = mla(c_q, c_kv, k_pe, pos, q_norm[l], kv_norm[l], w_uq[l], w_ukv[l]) @ w_proj_attn[l]
        y_b = hgrn2(hq, hf, hi, hg, lbs[l], hg_norm[l]) @ w_proj_rec[l]
        merged = jax.nn.sigmoid(ga) * y_a + jax.nn.sigmoid(gb) * y_b
        h = h + merged @ w_out[l]
        h = h + 0.5 * swiglu(rms_norm(h, ffn2_norm[l]), ffn2_w_gu[l], ffn2_w_down[l])
    return rms_norm(h, final_norm)[:, N_META:]


N_A_LAYERS = DEPTH // 2
N_B_LAYERS = DEPTH - N_A_LAYERS
MACARON_WEIGHT = 0.5
D_RNN = D_MODEL
LRU_HEADS = 4
LRU_BLOCK = D_RNN // LRU_HEADS
CONV_WIDTH = 4
LRU_C = 8.0
N_HEADS = 8
HEAD_DIM = D_MODEL // N_HEADS
MOBA_BLOCK = 256
MOBA_TOPK = 3
Q_CHUNK = 16
N_BUCKETS = 32
MAX_DISTANCE = 128
RMS_EPS = 1e-6


def rms_norm_2(x, g):
    xf = x.astype(jnp.float32)
    y = xf * lax.rsqrt(jnp.mean(xf * xf, axis=-1, keepdims=True) + RMS_EPS)
    return (y * g.astype(jnp.float32)).astype(x.dtype)

def swiglu_2(x, w_gate, w_up, w_down):
    return (jax.nn.silu(x @ w_gate) * (x @ w_up)) @ w_down

def macaron_ffn(x, pre_g, post_g, w_gate, w_up, w_down):
    h = swiglu_2(rms_norm_2(x, pre_g), w_gate, w_up, w_down)
    return x + MACARON_WEIGHT * rms_norm_2(h, post_g)

def causal_dwconv(x, w, b):
    c = x.shape[-1]
    out = lax.conv_general_dilated(
        x, w[:, None, :].astype(x.dtype), window_strides=(1,),
        padding=[(CONV_WIDTH - 1, 0)], dimension_numbers=('NWC', 'WIO', 'NWC'),
        feature_group_count=c)
    return out + b

def rg_lru(x, w_r, b_r, w_i, b_i, lam):
    bn, s, c = x.shape
    xh = x.reshape(bn, s, LRU_HEADS, LRU_BLOCK)
    r = jax.nn.sigmoid(jnp.einsum('bshi,hij->bshj', xh, w_r).reshape(bn, s, c) + b_r)
    i = jax.nn.sigmoid(jnp.einsum('bshi,hij->bshj', xh, w_i).reshape(bn, s, c) + b_i)
    log_a = -LRU_C * r.astype(jnp.float32) * jax.nn.softplus(-lam.astype(jnp.float32))
    a = jnp.exp(log_a)
    mult = jnp.sqrt(-jnp.expm1(2.0 * log_a))
    u = mult * (i * x).astype(jnp.float32)

    def combine(left, right):
        a_l, b_l = left
        a_r, b_r2 = right
        return a_l * a_r, a_r * b_l + b_r2

    _, h = lax.associative_scan(combine, (a, u), axis=1)
    return h.astype(x.dtype)

def recurrent_block(xn, w_in, b_in, conv_w, conv_b, w_r, b_r, w_i, b_i, lam, w_out, b_out):
    proj = xn @ w_in + b_in
    xb, yb = jnp.split(proj, 2, axis=-1)
    xb = causal_dwconv(xb, conv_w, conv_b)
    h = rg_lru(xb, w_r, b_r, w_i, b_i, lam)
    return (h * jax.nn.gelu(yb)) @ w_out + b_out

def t5_bucket(dist):
    n = jnp.maximum(dist, 0)
    max_exact = N_BUCKETS // 2
    nf = jnp.maximum(n, 1).astype(jnp.float32)
    large = max_exact + (jnp.log(nf / max_exact) / math.log(MAX_DISTANCE / max_exact)
                         * (N_BUCKETS - max_exact)).astype(jnp.int32)
    large = jnp.minimum(large, N_BUCKETS - 1)
    return jnp.where(n < max_exact, n, large)

def shared_kv(x, kv_norm_g, w_kv):
    bn, s, _ = x.shape
    nblk = -(-s // MOBA_BLOCK)
    kv = rms_norm_2(x, kv_norm_g) @ w_kv
    k, v = jnp.split(kv, 2, axis=-1)
    pad = nblk * MOBA_BLOCK - s
    k = jnp.pad(k, ((0, 0), (0, pad), (0, 0)))
    v = jnp.pad(v, ((0, 0), (0, pad), (0, 0)))
    k_blk = k.reshape(bn, nblk, MOBA_BLOCK, N_HEADS, HEAD_DIM).transpose(0, 3, 1, 2, 4)
    v_blk = v.reshape(bn, nblk, MOBA_BLOCK, N_HEADS, HEAD_DIM).transpose(0, 3, 1, 2, 4)
    k_mean = jnp.mean(k_blk, axis=3)
    return k_blk, v_blk, k_mean

def moba_attention(q, k_blk, v_blk, k_mean, rel_bias):
    bn, s = q.shape[0], q.shape[1]
    nblk = k_blk.shape[2]
    topk = min(MOBA_TOPK, max(nblk - 1, 1))
    pos = jnp.arange(s)
    cur = pos // MOBA_BLOCK
    gate = jnp.einsum('bshd,bhnd->bhsn', q, k_mean).astype(jnp.float32)
    past = jnp.arange(nblk)[None, :] < cur[:, None]
    gate = jnp.where(past, gate, -jnp.inf)
    _, idx = lax.top_k(gate, topk)
    valid = idx < cur[None, None, :, None]

    nc = s // Q_CHUNK
    q_c = q.transpose(0, 2, 1, 3).reshape(bn, N_HEADS, nc, Q_CHUNK, HEAD_DIM).transpose(2, 0, 1, 3, 4)
    idx_c = idx.reshape(bn, N_HEADS, nc, Q_CHUNK, topk).transpose(2, 0, 1, 3, 4)
    valid_c = valid.reshape(bn, N_HEADS, nc, Q_CHUNK, topk).transpose(2, 0, 1, 3, 4)
    starts = jnp.arange(nc) * Q_CHUNK
    b_ix = jnp.arange(bn)[:, None, None, None]
    h_ix = jnp.arange(N_HEADS)[None, :, None, None]
    offs = jnp.arange(MOBA_BLOCK)
    scale = HEAD_DIM ** -0.5
    n_sel = topk * MOBA_BLOCK

    def chunk(args):
        qc, ic, vc, start = args
        t = start + jnp.arange(Q_CHUNK)
        ks = k_blk[b_ix, h_ix, ic]
        vs = v_blk[b_ix, h_ix, ic]
        kpos = ic[..., None] * MOBA_BLOCK + offs
        bias_s = rel_bias[h_ix[..., None], t5_bucket(t[:, None, None] - kpos)]
        s_sel = jnp.einsum('bhqd,bhqkjd->bhqkj', qc, ks).astype(jnp.float32) * scale + bias_s
        s_sel = jnp.where(vc[..., None], s_sel, -jnp.inf)
        cb = start // MOBA_BLOCK
        k_own = lax.dynamic_index_in_dim(k_blk, cb, axis=2, keepdims=False)
        v_own = lax.dynamic_index_in_dim(v_blk, cb, axis=2, keepdims=False)
        d_own = t[:, None] - (cb * MOBA_BLOCK + offs)[None, :]
        bias_o = rel_bias[:, t5_bucket(d_own)]
        s_own = jnp.einsum('bhqd,bhjd->bhqj', qc, k_own).astype(jnp.float32) * scale + bias_o
        s_own = jnp.where(d_own >= 0, s_own, -jnp.inf)
        logits = jnp.concatenate([s_sel.reshape(bn, N_HEADS, Q_CHUNK, n_sel), s_own], axis=-1)
        p = jax.nn.softmax(logits, axis=-1)
        p_sel = p[..., :n_sel].reshape(bn, N_HEADS, Q_CHUNK, topk, MOBA_BLOCK).astype(vs.dtype)
        p_own = p[..., n_sel:].astype(v_own.dtype)
        return (jnp.einsum('bhqkj,bhqkjd->bhqd', p_sel, vs)
                + jnp.einsum('bhqj,bhjd->bhqd', p_own, v_own))

    out = lax.map(chunk, (q_c, idx_c, valid_c, starts))
    return out.transpose(1, 0, 3, 2, 4).reshape(bn, s, N_HEADS * HEAD_DIM)

def second_inputs(seed: int = 0) -> dict:
    key = jax.random.key(seed)
    ks = iter(jax.random.split(key, 64))

    def nrm(shape, scale):
        return jax.random.normal(next(ks), shape, jnp.float32) * scale

    def gain(shape):
        return 1.0 + nrm(shape, 0.05)

    d, f = D_MODEL, D_FF
    u = jax.random.uniform(next(ks), (N_A_LAYERS, D_RNN), jnp.float32, 0.9, 0.999)
    return {
        "x": nrm((BATCH, SEQ, d), 1.0),
        "ffn1_pre_g": gain((DEPTH, d)),
        "ffn1_post_g": gain((DEPTH, d)),
        "ffn1_w_gate": nrm((DEPTH, d, f), d ** -0.5),
        "ffn1_w_up": nrm((DEPTH, d, f), d ** -0.5),
        "ffn1_w_down": nrm((DEPTH, f, d), f ** -0.5),
        "ffn2_pre_g": gain((DEPTH, d)),
        "ffn2_post_g": gain((DEPTH, d)),
        "ffn2_w_gate": nrm((DEPTH, d, f), d ** -0.5),
        "ffn2_w_up": nrm((DEPTH, d, f), d ** -0.5),
        "ffn2_w_down": nrm((DEPTH, f, d), f ** -0.5),
        "mix_pre_g": gain((DEPTH, d)),
        "mix_post_g": gain((DEPTH, d)),
        "lru_w_in": nrm((N_A_LAYERS, d, 2 * D_RNN), d ** -0.5),
        "lru_b_in": nrm((N_A_LAYERS, 2 * D_RNN), 0.02),
        "lru_conv_w": nrm((N_A_LAYERS, CONV_WIDTH, D_RNN), CONV_WIDTH ** -0.5),
        "lru_conv_b": nrm((N_A_LAYERS, D_RNN), 0.02),
        "lru_w_r": nrm((N_A_LAYERS, LRU_HEADS, LRU_BLOCK, LRU_BLOCK), LRU_BLOCK ** -0.5),
        "lru_b_r": nrm((N_A_LAYERS, D_RNN), 0.02),
        "lru_w_i": nrm((N_A_LAYERS, LRU_HEADS, LRU_BLOCK, LRU_BLOCK), LRU_BLOCK ** -0.5),
        "lru_b_i": nrm((N_A_LAYERS, D_RNN), 0.02),
        "lru_lambda": jnp.log(u / (1.0 - u)),
        "lru_w_out": nrm((N_A_LAYERS, D_RNN, d), D_RNN ** -0.5),
        "lru_b_out": nrm((N_A_LAYERS, d), 0.02),
        "kv_norm_g": gain((d,)),
        "w_kv": nrm((d, 2 * N_HEADS * HEAD_DIM), d ** -0.5),
        "attn_w_q": nrm((N_B_LAYERS, d, N_HEADS * HEAD_DIM), d ** -0.5),
        "attn_w_o": nrm((N_B_LAYERS, N_HEADS * HEAD_DIM, d), (N_HEADS * HEAD_DIM) ** -0.5),
        "rel_bias": nrm((N_HEADS, N_BUCKETS), 0.5),
    }

def second_block(x, ffn1_pre_g, ffn1_post_g, ffn1_w_gate, ffn1_w_up, ffn1_w_down,
              ffn2_pre_g, ffn2_post_g, ffn2_w_gate, ffn2_w_up, ffn2_w_down,
              mix_pre_g, mix_post_g,
              lru_w_in, lru_b_in, lru_conv_w, lru_conv_b, lru_w_r, lru_b_r, lru_w_i, lru_b_i,
              lru_lambda, lru_w_out, lru_b_out,
              kv_norm_g, w_kv, attn_w_q, attn_w_o, rel_bias):
    bn, s, _ = x.shape
    k_blk = v_blk = k_mean = None
    for l in range(DEPTH):
        x = macaron_ffn(x, ffn1_pre_g[l], ffn1_post_g[l], ffn1_w_gate[l], ffn1_w_up[l], ffn1_w_down[l])
        xn = rms_norm_2(x, mix_pre_g[l])
        if l < N_A_LAYERS:
            m = recurrent_block(xn, lru_w_in[l], lru_b_in[l], lru_conv_w[l], lru_conv_b[l],
                                lru_w_r[l], lru_b_r[l], lru_w_i[l], lru_b_i[l], lru_lambda[l],
                                lru_w_out[l], lru_b_out[l])
        else:
            j = l - N_A_LAYERS
            q = (xn @ attn_w_q[j]).reshape(bn, s, N_HEADS, HEAD_DIM)
            m = moba_attention(q, k_blk, v_blk, k_mean, rel_bias) @ attn_w_o[j]
        x = x + rms_norm_2(m, mix_post_g[l])
        x = macaron_ffn(x, ffn2_pre_g[l], ffn2_post_g[l], ffn2_w_gate[l], ffn2_w_up[l], ffn2_w_down[l])
        if l == N_A_LAYERS - 1:
            k_blk, v_blk, k_mean = shared_kv(x, kv_norm_g, w_kv)
    return x


def setup_inputs(seed=0):
    out = dict(first_inputs(seed))
    for name, value in second_inputs(seed + 1).items():
        if name != "x":
            out[name + "_2"] = value
    return out


def reference(
    x, meta_tokens, ffn1_norm, ffn1_w_gu, ffn1_w_down, mix_norm, w_in, q_norm, kv_norm, w_uq,
    w_ukv, hg_lb_raw, hg_norm, w_proj_attn, w_proj_rec, w_out, ffn2_norm, ffn2_w_gu,
    ffn2_w_down, final_norm, ffn1_pre_g_2, ffn1_post_g_2, ffn1_w_gate_2, ffn1_w_up_2,
    ffn1_w_down_2, ffn2_pre_g_2, ffn2_post_g_2, ffn2_w_gate_2, ffn2_w_up_2, ffn2_w_down_2,
    mix_pre_g_2, mix_post_g_2, lru_w_in_2, lru_b_in_2, lru_conv_w_2, lru_conv_b_2, lru_w_r_2,
    lru_b_r_2, lru_w_i_2, lru_b_i_2, lru_lambda_2, lru_w_out_2, lru_b_out_2, kv_norm_g_2,
    w_kv_2, attn_w_q_2, attn_w_o_2, rel_bias_2,
):
    x = first_block(
        x, meta_tokens, ffn1_norm, ffn1_w_gu, ffn1_w_down, mix_norm, w_in, q_norm, kv_norm,
        w_uq, w_ukv, hg_lb_raw, hg_norm, w_proj_attn, w_proj_rec, w_out, ffn2_norm, ffn2_w_gu,
        ffn2_w_down, final_norm,
    )
    return second_block(
        x, ffn1_pre_g_2, ffn1_post_g_2, ffn1_w_gate_2, ffn1_w_up_2, ffn1_w_down_2, ffn2_pre_g_2,
        ffn2_post_g_2, ffn2_w_gate_2, ffn2_w_up_2, ffn2_w_down_2, mix_pre_g_2, mix_post_g_2,
        lru_w_in_2, lru_b_in_2, lru_conv_w_2, lru_conv_b_2, lru_w_r_2, lru_b_r_2, lru_w_i_2,
        lru_b_i_2, lru_lambda_2, lru_w_out_2, lru_b_out_2, kv_norm_g_2, w_kv_2, attn_w_q_2,
        attn_w_o_2, rel_bias_2,
    )


_drawn_inputs = setup_inputs


def setup_inputs(seed=0):
    import zlib

    import numpy as np

    out = dict(_drawn_inputs(seed))
    spreads = {}
    factors = {'q_norm': 8.0,
     'kv_norm': 6.875,
     'hg_norm': 3.972,
     'ffn2_norm': 3.125,
     'lru_b_r_2': 8.0,
     'lru_b_i_2': 8.0,
     'hg_lb_raw': 2.874}
    for name, (base, spread) in spreads.items():
        noise = np.random.default_rng([zlib.crc32(name.encode()), seed]).standard_normal(out[name].shape)
        drawn = base * np.exp(spread * noise) if base else spread * noise
        out[name] = __import__('jax').numpy.asarray(drawn.astype(out[name].dtype))
    for name, factor in factors.items():
        out[name] = (out[name] * factor).astype(out[name].dtype)
    return out
```

```python
from contextlib import ExitStack

import numpy as np
import concourse.bass as bass
from concourse import mybir

P = 128
D_MODEL, SEQ, N_META, D_FF, DEPTH = 1024, 256, 16, 2816, 2
T = SEQ + N_META
KD = D_MODEL // P
KF = D_FF // P
HEADS, NOPE, ROPE, V_HEAD = 8, 64, 32, 64
Q_LORA, KV_LORA = 384, 256
QK_SCALE = float((NOPE + ROPE) ** -0.5)
HG_HEADS, HG_DIM = 4, 128
HG_SCALE = float(HG_DIM ** -0.5)
HEAD_DIM = 128
MOBA_SCALE = float(HEAD_DIM ** -0.5)
N_BUCKETS, MAX_DISTANCE = 32, 128
EPS = 1e-6
F_MIN = 1e-20
NEG_BIG = -1e30
LRU_C = 8.0
LN_SPLIT = 2.0 ** -32
LN_SHIFT = float(32 * np.log(2.0))
TINY = 1e-30

F32, F32R, U8 = mybir.dt.float32, mybir.dt.float32r, mybir.dt.uint8
ACT = mybir.ActivationFunctionType
ALU = mybir.AluOpType
AX_X = mybir.AxisListType.X

RING = 4
CH8, CH11 = 8 * P, 11 * P
FFN_PAIRS = KF
FFN_GU_QUADS, FFN_DOWN_QUADS = 2 * KF // RING, 2 * KD // RING
FFN_QUADS = FFN_GU_QUADS + FFN_DOWN_QUADS
FFN_TILES = 2 * KF + KD

HF, HI, HQ, HGATE, GA, GB = 0, 4, 8, 12, 16, 24
CQ, CKV, KPE, KPS = 32, 35, 37, 38
UQ, UKV, PA, PR, OUT = 39, 47, 55, 63, 71
MIX_TILES, MIX_QUADS = 79, 15
GATED = 33
LAYER_QUADS = 2 * FFN_QUADS + MIX_QUADS
LAYER_TILES = 2 * FFN_TILES + MIX_TILES

LEVELS = 10
MASKED_LEVELS = 8
HALF = [0] + [2 ** i for i in range(LEVELS - 1)]

TOKEN_TILES = ((0, P), (P, P), (2 * P, T - 2 * P))

VEC = {}
_at = 0
for _name, _n in (("norms", 56), ("small", 12), ("lb_raw", 8), ("ffn_pre", 32), ("ffn_post", 32),
                  ("mix_pre", 16), ("mix_post", 16), ("kv", 8), ("b_in", 16), ("conv_w", 32),
                  ("conv_b", 8), ("b_r", 8), ("b_i", 8), ("lam", 8), ("b_out", 8)):
    VEC[_name] = _at
    _at += _n
N_VEC = _at

CONST = {}
_at = 0
for _name, _n in (("ones", P), ("ident", P), ("cos", T), ("sin", T), ("causal", 3 * P),
                  ("causal_tail", T), ("eps", 1)):
    CONST[_name] = _at
    _at += _n
N_CONST = _at


def k8(w):
    k, m = w.shape[0] // P, w.shape[1] // P
    return np.ascontiguousarray(w.reshape(k, P, m, P).transpose(2, 1, 0, 3)).reshape(m, P, k * P)


def k_few(w):
    k, m = w.shape[0] // P, w.shape[1] // P
    tiles = w.reshape(k, P, m, P).transpose(2, 0, 1, 3).reshape(k * m // 8, 8, P, P)
    return np.ascontiguousarray(tiles.transpose(0, 2, 1, 3)).reshape(-1, P, CH8)


def down_chunks(w):
    tiles = w.reshape(2, 11, P, KD, P).transpose(3, 0, 2, 1, 4)
    return np.ascontiguousarray(tiles).reshape(2 * KD, P, CH11)


def constants():
    c = np.zeros((P, N_CONST), np.float32)

    def put(name, a):
        c[:a.shape[0], CONST[name]:CONST[name] + a.shape[1]] = a

    put("ones", np.ones((P, P)))
    put("ident", np.eye(P))
    half = ROPE // 2
    inv = np.float32(10000.0) ** (-np.arange(half, dtype=np.float32) / np.float32(half))
    ang = (inv.astype(np.float32)[:, None] * np.arange(T, dtype=np.float32)[None, :]).astype(np.float32)
    put("cos", np.tile(np.cos(ang), (2 * P // ROPE, 1)))
    put("sin", np.tile(np.concatenate([-np.sin(ang), np.sin(ang)]), (P // ROPE, 1)))
    triangle = np.where(np.arange(P)[None, :] <= np.arange(P)[:, None], 0.0, NEG_BIG)
    put("causal", np.concatenate([triangle, np.zeros((P, P)), triangle], 1))
    put("causal_tail", np.where(np.arange(T)[None, :] <= SEQ + np.arange(16)[:, None], 0.0, NEG_BIG))
    put("eps", np.full((P, 1), EPS))
    dist = 255 - np.arange(512)
    n = np.maximum(dist, 0)
    exact = N_BUCKETS // 2
    nf = np.maximum(n, 1).astype(np.float32)
    large = exact + (np.log(nf / np.float32(exact)).astype(np.float32)
                     / np.float32(np.log(MAX_DISTANCE / exact)) * np.float32(N_BUCKETS - exact)).astype(np.int32)
    bucket = np.where(n < exact, n, np.minimum(large, N_BUCKETS - 1))
    row = np.where(dist >= 0, bucket, N_BUCKETS)
    bucket_rows = (row[None, :] == np.arange(N_BUCKETS + 1)[:, None]).astype(np.float32)
    s, t = np.arange(P)[:, None], np.arange(P)[None, :]
    masks = [s == t]
    for m in HALF[1:MASKED_LEVELS]:
        masks.append((s // (2 * m) == t // (2 * m)) & (s % (2 * m) < m) & (t % (2 * m) >= m))
    return c, np.stack(masks, 1).astype(np.float32).reshape(P, MASKED_LEVELS * P), bucket_rows


def mixer_order():
    steps = [("tile", t) for t in range(HGATE)] + [("turn_v", 0), ("decay", 0)]
    level = 0
    for t in range(HGATE, UQ):
        steps.append(("tile", t))
        if (t - HGATE) % 2 == 1 and level < LEVELS:
            steps.append(("level", level))
            level += 1
    steps += [("level", n) for n in range(level, LEVELS)]
    steps += [("rec_out", h) for h in range(HG_HEADS)] + [("rec_norm", h) for h in range(HG_HEADS)]
    steps += [("latent_norm", 0), ("latent_norm", 1)]
    steps += [("tile", t) for t in range(UQ, PA)] + [("turn_v2", 0)]
    steps += [("scores", 0)]
    for h in range(HEADS):
        steps += ([("scores", h + 1)] if h + 1 < HEADS else []) + [("attend", h)]
    return steps + [("tile", t) for t in range(PA, MIX_TILES)]


MIXER = mixer_order()

SCORE_ROWS = ((P, 0, P), (P, P, 3 * P), (T - 2 * P, 3 * P, 3 * P + T))


def mixer_parts(t):
    for first, k, n, chunk in ((UQ, 3, 8, UQ), (UKV, 2, 8, UQ + 3), (PA, 4, 8, UQ + 5), (PR, 4, 8, UQ + 9)):
        if first <= t < first + n:
            return [(chunk + ((t - first) * k + i) // 8, ((t - first) * k + i) % 8) for i in range(k)]
    chunk = t if t < UQ else t - OUT + UQ + 13
    return [(chunk, i) for i in range(8)]


def chunks_ended(t):
    return [c for c, i in mixer_parts(t) if i == 7]


def gated(t):
    return t + 1 if t < HI else t + 1 - 4


def slot_before(t):
    return t - 8 if t - 4 in range(HI, HQ) else t - 4


def program(nc, a):
    with ExitStack() as ctx:
        arena = ctx.enter_context(nc.sbuf_tensor("arena", [P, 52176], F32))
        base, end = nc.sbuf_base - 52176 * 4, nc.sbuf_base
        top = [base]

        def at(name, shape, dt, where=None):
            place = top if where is None else where
            size = int(np.prod(shape[1:])) * (1 if dt == U8 else 4)
            h = nc.alloc_sbuf_tensor_at(name, shape, dt, offset=place[0])
            place[0] += (size + 31) // 32 * 32
            assert place[0] <= end, (name, place[0] - end)
            return h

        raw = at("raw", [P, RING, CH11], F32)
        whi = at("whi", [P, RING, CH11], F32R)
        wlo = at("wlo", [P, RING, CH11], F32R)
        h = at("h", [P, KD, T], F32)
        xhi = at("xhi", [P, KD, T], F32R)
        xlo = at("xlo", [P, KD, T], F32R)
        consts = at("consts", [P, N_CONST], F32)
        masks = at("masks", [P, MASKED_LEVELS, P], U8)
        vec = at("vec", [P, N_VEC], F32)
        z = at("z", [P, 4, T], F32)
        sil = at("sil", [P, 2, T], F32)
        sqt = at("sqt", [P, 2, T], F32)
        acc = at("acc", [P, T], F32)
        std = at("std", [P, T], F32)
        rstd = at("rstd", [P, T], F32)
        rlat = at("rlat", [P, 2, T], F32)
        lb = at("lb", [P, 4, DEPTH * HG_HEADS], F32)
        lbs = lb[:, 0, :]
        one_lb = lb[:, 1, :]
        negmax = at("negmax", [P, 2, 3], F32)
        sums = at("sums", [P, 2, 3], F32)
        lam = at("lam", [P, 4, KD], F32)
        idle = at("idle", [P, 1], F32)
        hbase = top[0]
        hidhi = at("hidhi", [P, KF, T], F32R)
        hidlo = at("hidlo", [P, KF, T], F32R)
        ebase = top[0]

        H, E = [hbase], [ebase]
        midbase = H[0]
        midhi, midlo = at("midhi", [P, KD, T], F32R, H), at("midlo", [P, KD, T], F32R, H)
        rechi, reclo = at("rechi", [P, 4, T], F32R, H), at("reclo", [P, 4, T], F32R, H)
        atthi, attlo = at("atthi", [P, 4, T], F32R, H), at("attlo", [P, 4, T], F32R, H)
        lathi, latlo = at("lathi", [P, 5, T], F32R, H), at("latlo", [P, 5, T], F32R, H)
        krot = at("krot", [P, T], F32, H)
        M = [midbase]
        gate = at("gate", [P, 4, T], F32, M)
        gate_flat = gate[:, :, :].rearrange("p h t -> p (h t)")[:, 0:MASKED_LEVELS * P]
        vtok = at("vtok", [P, 3, 512], F32, M)
        dec0 = at("dec0", [P, 4, T], F32, M)
        dec1 = at("dec1", [P, 4, 144], F32, M)
        dec2 = at("dec2", [P, 4, 16], F32, M)
        assert M[0] <= midbase + 2 * KD * T * 4
        sga, sgb = at("sga", [P, KD, T], F32, E), at("sgb", [P, KD, T], F32, E)
        recbase = E[0]
        pre, suf = at("pre", [P, 4, T], F32, E), at("suf", [P, 4, T], F32, E)
        hq, hk = at("hq", [P, 4, T], F32, E), at("hk", [P, 4, T], F32, E)
        qd, kd = at("qd", [P, 4, T], F32, E), at("kd", [P, 4, T], F32, E)
        A = [recbase]
        qn, qr = at("qn", [P, 4, T], F32, A), at("qr", [P, 2, T], F32, A)
        kn, vtok2 = at("kn", [P, 4, T], F32, A), at("vtok2", [P, 3, 512], F32, A)
        sc = at("sc", [P, 2, 656], F32, A)
        pt = at("pt", [P, 2, 432], F32, A)
        assert A[0] <= end

        E = [ebase]
        y = at("y", [P, KD, T], F32, E)
        kvbase = E[0]
        k2 = at("k2", [P, KD, SEQ], F32, E)
        vt2 = at("vt2", [P, 2, KD * P], F32, E)
        bias = at("bias", [P, HEADS, 3 * P], F32, E)
        brow = at("brow", [P, 512], F32, E)
        R = [kvbase]
        sr, si = at("sr", [P, KD, SEQ], F32, R), at("si", [P, KD, SEQ], F32, R)
        yg = at("yg", [P, KD, SEQ], F32, R)
        xb = at("xb", [P, 2, SEQ + 3], F32, R)
        H = [hbase]
        cv = at("cv", [P, KD, SEQ], F32, H)
        cvhi, cvlo = at("cvhi", [P, KD, SEQ], F32R, H), at("cvlo", [P, KD, SEQ], F32R, H)
        outhi, outlo = at("outhi", [P, KD, SEQ], F32R, H), at("outlo", [P, KD, SEQ], F32R, H)
        H = [hbase + 2 * KD * T * 4]
        q2 = at("q2", [P, KD, SEQ], F32, H)
        sc2 = at("sc2", [P, 2, 3 * P], F32, H)
        pt2 = at("pt2", [P, 2, 3 * P], F32, H)
        onehot = at("onehot", [P, 512], F32, H)
        relt = at("relt", [P, HEADS], F32, H)
        assert H[0] <= ebase

        bank = [ctx.enter_context(nc.psum_tensor(f"bank{i}", [P, 512], F32)) for i in range(8)]
        NORM = 7

        def const(name, n):
            return consts[:, CONST[name]:CONST[name] + n]

        ones, ident, eps = const("ones", P), const("ident", P), const("eps", 1)

        def vcol(name, i):
            return vec[:, VEC[name] + i:VEC[name] + i + 1]

        def norm_gain(x, k):
            if isinstance(x, int):
                return vcol("norms", 8 * x + k)
            return vec[:, bass.ds(x * 8 + VEC["norms"] + k, 1)]

        scratch = nc.dram_tensor("bias_rows", [HEADS, P, 513], F32, kind="Internal").ap()

        def sem(name):
            return ctx.enter_context(nc.semaphore(name))

        landed = [sem(f"landed{i}") for i in range(RING)]
        hi_made, lo_made, chunk_used = sem("hi_made"), sem("lo_made"), sem("chunk_used")
        tile_done, tile_read = sem("tile_done"), sem("tile_read")
        consts_in, h_in = sem("consts_in"), sem("h_in")
        h_made, x_hi_made, x_lo_made = sem("h_made"), sem("x_hi_made"), sem("x_lo_made")
        sq_made, sum_made, std_made, rstd_made = sem("sq_made"), sem("sum_made"), sem("std_made"), sem("rstd_made")
        gate_scaled, up_scaled, silu_made = sem("gate_scaled"), sem("up_scaled"), sem("silu_made")
        hid_made, hid_hi_made, hid_lo_made = sem("hid_made"), sem("hid_hi_made"), sem("hid_lo_made")
        act_took = sem("act_took")
        lb_asked, lb_exp, lam_asked = sem("lb_asked"), sem("lb_exp"), sem("lam_asked")
        decay_made, log_made, suffix_cleared, k_made = sem("decay_made"), sem("log_made"), sem("suffix_cleared"), sem("k_made")
        v_turned, v_taken = sem("v_turned"), sem("v_taken")
        sums_ready, exp_made, level_ready, level_done = sem("sums_ready"), sem("exp_made"), sem("level_ready"), sem("level_done")
        rec_done, rec_taken, rec_sq, rec_sum, rec_std, rec_f, rec_hi, rec_lo = (
            sem(n) for n in ("rec_done", "rec_taken", "rec_sq", "rec_sum", "rec_std", "rec_f", "rec_hi", "rec_lo"))
        kd_ready, level_taken = sem("kd_ready"), sem("level_taken")
        lat_sq, lat_lo, lat_z = sem("lat_sq"), sem("lat_lo"), sem("lat_z")
        krot_made, qrot_made = sem("krot_made"), sem("qrot_made")
        v2_turned, v2_taken = sem("v2_turned"), sem("v2_taken")
        scores_done, max_made, probs_made, probs_normed, probs_turned, probs_taken = (
            sem(n) for n in ("scores_done", "max_made", "probs_made", "probs_normed", "probs_turned", "probs_taken"))
        att_done, att_hi, att_lo = sem("att_done"), sem("att_hi"), sem("att_lo")
        merged, mid_hi_made, mid_lo_made, y_scaled = sem("merged"), sem("mid_hi_made"), sem("mid_lo_made"), sem("y_scaled")
        branch_made = sem("branch_made")
        xb_made, conv_begun, conv_made, cv_hi_made, cv_lo_made = (
            sem(n) for n in ("xb_made", "conv_begun", "conv_made", "cv_hi_made", "cv_lo_made"))
        b_act_took, lam_step, coef_made, decay2_made, root_made, root_asked = (
            sem(n) for n in ("b_act_took", "lam_step", "coef_made", "decay2_made", "root_made", "root_asked"))
        out_f, out_hi_made, out_lo_made = sem("out_f"), sem("out_hi_made"), sem("out_lo_made")
        kv_turned, kv_taken = sem("kv_turned"), sem("kv_taken")
        rel_in, brow_done, brow_made, brow_out, bias_in = (
            sem(n) for n in ("rel_in", "brow_done", "brow_made", "brow_out", "bias_in"))
        s2_done, s2_max, s2_exp, s2_normed, s2_turned, s2_taken, o2_done, o2_hi, o2_lo = (
            sem(n) for n in ("s2_done", "s2_max", "s2_exp", "s2_normed", "s2_turned", "s2_taken", "o2_done", "o2_hi", "o2_lo"))
        stored = sem("stored")

        block = ctx.enter_context(nc.Block())

        def layer_stage(l, which):
            q, j, n = ((0, 0, 0), (FFN_QUADS, FFN_TILES, 1), (FFN_QUADS + MIX_QUADS, FFN_TILES + MIX_TILES, 4))[which]
            return dict(q=l * LAYER_QUADS + q, j=l * LAYER_TILES + j, x=l * 3 + which, n=l * 5 + n,
                        f=l * 2 + which // 2, c=0)

        Q2, J2 = DEPTH * LAYER_QUADS, DEPTH * LAYER_TILES
        REC_QUADS, REC_TILES, KV_QUADS, KV_TILES, ATT_QUADS, ATT_TILES = 7, 40, 4, 16, 4, 16
        F4 = dict(q=Q2, j=J2, x=7, n=11, f=4, c=N_META)
        REC = dict(q=Q2 + FFN_QUADS, j=J2 + FFN_TILES, x=8, n=13, c=N_META)
        F5 = dict(q=REC["q"] + REC_QUADS, j=REC["j"] + REC_TILES, x=9, n=15, f=5, c=N_META)
        KV = dict(q=F5["q"] + FFN_QUADS, j=F5["j"] + FFN_TILES, x=10, n=17, c=N_META)
        F6 = dict(q=KV["q"] + KV_QUADS, j=KV["j"] + KV_TILES, x=11, n=18, f=6, c=N_META)
        ATT = dict(q=F6["q"] + FFN_QUADS, j=F6["j"] + FFN_TILES, x=12, n=19, c=N_META)
        F7 = dict(q=ATT["q"] + ATT_QUADS, j=ATT["j"] + ATT_TILES, x=13, n=21, f=7, c=N_META)
        GAIN2 = {7: ("ffn_pre", 0), 8: ("mix_pre", 0), 9: ("ffn_pre", 8), 10: ("kv", 0), 11: ("ffn_pre", 16),
                 12: ("mix_pre", 8), 13: ("ffn_pre", 24)}
        UPDATE = {7: 7, 8: 8, 9: 9, 10: 10, 12: 11, 13: 12, 14: 13}

        def squares(x, n):
            return n - 3 if isinstance(n, int) and n >= 10 else x + 1

        SQUARES = {n: squares(0, n) for n in range(10, 23)}

        def gain(x, k):
            if not isinstance(x, int) or x < 7:
                return norm_gain(x, k)
            name, first = GAIN2[x]
            return vcol(name, first + k)

        @block.sync
        def _(sp):
            def load(src, q, k, cols):
                if not isinstance(q, int) or q >= 1:
                    sp.wait_ge(lo_made, (q - 1) * RING + k + 1)
                sp.dma_start(raw[:, k, 0:cols], src).then_inc(landed[k], 16)

            def stream(array, first, q, quads, cols):
                with sp.Fori(0, quads) as b:
                    for k in range(RING):
                        load(array[b * RING + first + k], b + q, k, cols)

            def ffn_weights(q, f):
                stream(a["ffn_gu"], f * 2 * KF, q, FFN_GU_QUADS, CH8)
                stream(a["ffn_down"], f * 2 * KD, q + FFN_GU_QUADS, FFN_DOWN_QUADS, CH11)

            sp.dma_start(h[:, :, :], a["h0"]).then_inc(h_in, 16)
            sp.dma_start(vec[:, :], a["vectors"]).then_inc(consts_in, 16)
            for k in range(RING):
                load(a["ffn_gu"][k], 0, k, CH8)
            sp.dma_start(consts[:, :], a["consts"]).then_inc(consts_in, 16)
            sp.dma_start(gate_flat, a["masks"]).then_inc(consts_in, 16)
            stream(a["ffn_gu"], RING, 1, FFN_GU_QUADS - 1, CH8)
            stream(a["ffn_down"], 0, FFN_GU_QUADS, FFN_DOWN_QUADS, CH11)
            stream(a["mix"], 0, FFN_QUADS, MIX_QUADS, CH8)
            ffn_weights(FFN_QUADS + MIX_QUADS, 1)
            with sp.Fori(1, DEPTH) as l:
                ffn_weights(l * LAYER_QUADS, l * 2)
                stream(a["mix"], l * MIX_QUADS * RING, l * LAYER_QUADS + FFN_QUADS, MIX_QUADS, CH8)
                ffn_weights(l * LAYER_QUADS + FFN_QUADS + MIX_QUADS, l * 2 + 1)
            ffn_weights(F4["q"], 4)
            stream(a["rec"], 0, REC["q"], REC_QUADS, CH8)
            ffn_weights(F5["q"], 5)
            sp.wait_ge(tile_done, KV["j"])
            sp.dma_start(onehot[0:N_BUCKETS + 1, :], a["bucket_rows"]).then_inc(rel_in, 16)
            sp.dma_start(relt[0:N_BUCKETS + 1, :], a["rel_rows"]).then_inc(rel_in, 16)
            stream(a["kv"], 0, KV["q"], KV_QUADS, CH8)
            sp.wait_ge(brow_made, 1)
            for hd in range(HEADS):
                sp.dma_start(bass.AP(scratch.tensor, hd * P * 513, [[P * 513, 1], [513, P], [1, 512]]),
                             brow[hd:hd + 1, :].unsqueeze(1).to_broadcast([1, P, 512])).then_inc(brow_out, 16)
            sp.wait_ge(brow_out, 16 * HEADS)
            sp.dma_start(bias[:, :, :], bass.AP(scratch.tensor, P - 1, [[512, P], [P * 513, HEADS], [1, 3 * P]])
                         ).then_inc(bias_in, 16)
            ffn_weights(F6["q"], 6)
            stream(a["att"], 0, ATT["q"], ATT_QUADS, CH8)
            ffn_weights(F7["q"], 7)
            for m in range(KD):
                sp.wait_ge(h_made, 8 * 6 + m + 1)
                sp.dma_start(a["out"][:, m, :], h[:, m, N_META:T]).then_inc(stored, 16)
            sp.wait_ge(stored, 16 * KD)

        @block.tensor
        def _(pe):
            def split_product(out, parts, xh, xl, waits=None):
                last = len(parts) - 1
                for i, (slot, tile) in enumerate(parts):
                    if waits:
                        waits(i)
                    w = slice(tile * P, tile * P + P)
                    pe.matmul(out, wlo[:, slot, w], xh(i), start=(i == 0), stop=False)
                    pe.matmul(out, whi[:, slot, w], xl(i), start=False, stop=False)
                    mm = pe.matmul(out, whi[:, slot, w], xh(i), start=False, stop=(i == last))
                mm.then_inc(tile_done, 1)

            def norm_sum(src, c, ready, value):
                pe.wait_ge(ready, value)
                pe.matmul(bank[NORM][:, 0:T - c], ones, src, start=True, stop=True).then_inc(sum_made, 1)

            def inputs_ready(x):
                return lambda i: pe.wait_ge(x_lo_made, x * 8 + i + 1)

            def k8_tile(q, k, count, b, src, c, waits=None):
                pe.wait_ge(lo_made, q * RING + k + 1)
                if count is not None:
                    pe.wait_ge(tile_read, count)
                hi, lo = src
                cut = (lambda t, i: t[:, i, c:T]) if t_wide(hi) else (lambda t, i: t[:, i, :])
                split_product(bank[b][:, 0:T - c], [(k, i) for i in range(8)],
                              lambda i: cut(hi, i), lambda i: cut(lo, i), waits)

            def t_wide(t):
                return t.shape[2] == T

            def ffn(q, j, x, n, f, c, main_norm=True):
                def quad(b, first=False):
                    for k in range(RING):
                        k8_tile(b + q, k, None if first else b * RING + j + k - 3, k, (xhi, xlo), c,
                                inputs_ready(x) if first and k == 0 else None)
                        if first and k == 0 and main_norm:
                            norm_sum(acc[:, c:T], c, sq_made, squares(x, n))

                quad(0, first=True)
                with pe.Fori(1, FFN_GU_QUADS) as b:
                    quad(b)
                with pe.Fori(0, FFN_DOWN_QUADS) as b:
                    for m in range(2):
                        for k in (2 * m, 2 * m + 1):
                            pe.wait_ge(lo_made, (b + q + FFN_GU_QUADS) * RING + k + 1)
                        pe.wait_ge(tile_read, b * 2 + j + 2 * KF + m - 1)
                        pe.wait_ge(hid_lo_made, f * KF + KF - 2)

                        def waits(i):
                            if i >= KF - 2:
                                pe.wait_ge(hid_lo_made, f * KF + i + 1)

                        split_product(bank[4 + m][:, 0:T - c], [(2 * m + i // 11, i % 11) for i in range(KF)],
                                      lambda i: hidhi[:, i, c:T], lambda i: hidlo[:, i, c:T], waits)

            def mixer(l):
                st = layer_stage(l, 1)
                q, j, x, n = st["q"], st["j"], st["x"], st["n"]
                sources = {UQ: (lathi, latlo, 0), UKV: (lathi, latlo, 3), PA: (atthi, attlo, 0),
                           PR: (rechi, reclo, 0), OUT: (midhi, midlo, 0)}
                for step, i in MIXER:
                    if step == "tile":
                        t, parts = i, mixer_parts(i)
                        first = max([s for s in (0, *sources) if s <= t])
                        hi, lo, at_k = sources.get(first, (xhi, xlo, 0))
                        waits = None
                        if t == 0:
                            waits = inputs_ready(x)
                        if t == UQ:
                            pe.wait_ge(lat_lo, l * 5 + 3)
                        if t == UKV:
                            pe.wait_ge(lat_lo, l * 5 + 5)
                        if t == PA:
                            pe.wait_ge(att_lo, l * 4 + 4)
                        if t == PR:
                            pe.wait_ge(rec_lo, l * 4 + 4)
                        if t == OUT:
                            waits = lambda k: pe.wait_ge(mid_lo_made, l * 8 + k + 1)
                        for chunk in sorted({ch for ch, _ in parts}):
                            pe.wait_ge(lo_made, q * RING + chunk + 1)
                        if t >= OUT + 2:
                            pe.wait_ge(tile_read, j + t - 1)
                        elif 4 <= t < OUT:
                            pe.wait_ge(tile_read, j + t - 3)
                        split_product(bank[t % 4 if t < OUT else 4 + t % 2][:, 0:T], [(ch % RING, tile) for ch, tile in parts],
                                      lambda k: hi[:, at_k + k, :], lambda k: lo[:, at_k + k, :], waits)
                        if t == 0:
                            norm_sum(acc[:, :], 0, sq_made, squares(x, n))
                    elif step == "turn_v":
                        pe.wait_ge(tile_read, j + HQ)
                        for s, (at_t, size) in enumerate(TOKEN_TILES):
                            for hd in range(HG_HEADS):
                                tr = pe.transpose(bank[4 + s][0:size, hd * P:hd * P + P],
                                                  qd[:, hd, at_t:at_t + size], ident)
                            tr.then_inc(v_turned, 1)
                    elif step == "level":
                        level_products(l, i)
                    elif step == "rec_out":
                        if i == 0:
                            pe.wait_ge(level_taken, l * LEVELS + LEVELS)
                        if i >= 2:
                            pe.wait_ge(rec_taken, l * 4 + i - 1)
                        o = bank[4 + i % 2]
                        v = slice(i * P, i * P + P)
                        pe.matmul(o[:, 0:T], vtok[:, 0, v], dec0[:, i, :], start=True, stop=False)
                        pe.matmul(o[:, P:T], vtok[:, 1, v], dec1[:, i, :], start=False, stop=False)
                        pe.matmul(o[:, 2 * P:T], vtok[0:16, 2, v], dec2[0:16, i, :], start=False,
                                  stop=True).then_inc(rec_done, 1)
                    elif step == "rec_norm":
                        pe.wait_ge(rec_taken, l * 4 + i + 1)
                        if i == 0:
                            pe.wait_ge(level_taken, l * LEVELS + LEVELS)
                        else:
                            pe.wait_ge(rec_std, l * 4 + i)
                        pe.matmul(bank[6][:, 0:T], ones, suf[:, i, :], start=True, stop=True).then_inc(rec_sum, 1)
                    elif step == "latent_norm":
                        if i == 1:
                            pe.wait_ge(std_made, n + 2)
                        norm_sum(sil[:, i, :], 0, lat_sq, l * 2 + i + 1)
                    elif step == "turn_v2":
                        pe.wait_ge(tile_read, j + PA)
                        pe.wait_ge(rec_taken, l * 4 + 4)
                        pe.wait_ge(rec_std, l * 4 + 4)
                        for s, (at_t, size) in enumerate(TOKEN_TILES):
                            for m in range(4):
                                tr = pe.transpose(bank[4 + s][0:size, m * P:m * P + P],
                                                  z[:, m, at_t:at_t + size], ident)
                            tr.then_inc(v2_turned, 1)
                    elif step == "scores":
                        hd = i
                        if hd == 0:
                            pe.wait_ge(v2_taken, l * 3 + 3)
                            pe.wait_ge(qrot_made, l * 2 + 2)
                            pe.wait_ge(krot_made, l + 1)
                        if hd >= 2:
                            pe.wait_ge(max_made, l * HEADS + hd - 1)
                        r, r2 = NOPE * (hd % 2), ROPE * (hd % 4)
                        for (at_t, size), keys, out in (
                                (TOKEN_TILES[0], P, bank[4 + hd % 2][:, 0:P]),
                                (TOKEN_TILES[1], 2 * P, bank[4 + hd % 2][:, P:3 * P]),
                                (TOKEN_TILES[2], T, bank[2 + hd % 2][0:16, 0:T])):
                            pe.matmul(out, qn[r:r + NOPE, hd // 2, at_t:at_t + size],
                                      kn[r:r + NOPE, hd // 2, 0:keys], start=True, stop=False)
                            mm = pe.matmul(out, qr[r2:r2 + ROPE, hd // 4, at_t:at_t + size],
                                           krot[r2:r2 + ROPE, 0:keys], start=False, stop=True)
                        mm.then_inc(scores_done, 1)
                    elif step == "attend":
                        hd, p = i, i % 2
                        pe.wait_ge(probs_normed, l * HEADS + hd + 1)
                        if hd >= 1:
                            pe.wait_ge(probs_taken, l * HEADS + hd)
                        turned = bank[6]
                        for rows, at_s, size, out in (
                                (P, 0, P, turned[:, 0:P]), (P, P, P, turned[:, P:2 * P]),
                                (16, 3 * P, P, turned[:, 2 * P:T]), (P, 2 * P, P, turned[:, T:T + P]),
                                (16, 4 * P, P, turned[:, T + P:T + P + 16]),
                                (16, 5 * P, 16, turned[0:16, T + P + 16:T + P + 32])):
                            tr = pe.transpose(out, sc[0:rows, p, at_s:at_s + size], ident[0:rows, 0:rows])
                        tr.then_inc(probs_turned, 1)
                        pe.wait_ge(probs_taken, l * HEADS + hd + 1)
                        if hd % 2 == 0 and hd >= 4:
                            pe.wait_ge(att_lo, l * 4 + hd // 2 - 1)
                        r = V_HEAD * (hd % 2)
                        o = bank[hd // 2 % 2]
                        v = slice(hd * V_HEAD, hd * V_HEAD + V_HEAD)
                        pe.matmul(o[r:r + V_HEAD, 0:T], vtok2[:, 0, v], pt[:, p, 0:T], start=True, stop=False)
                        pe.matmul(o[r:r + V_HEAD, P:T], vtok2[:, 1, v], pt[:, p, T:T + P + 16],
                                  start=False, stop=False)
                        pe.matmul(o[r:r + V_HEAD, 2 * P:T], vtok2[0:16, 2, v], pt[0:16, p, T + P + 16:T + P + 32],
                                  start=False, stop=True).then_inc(att_done, 1)

            def level_products(l, i):
                pe.wait_ge(level_ready, l * LEVELS + i + 1)
                if i == 0:
                    pe.wait_ge(v_taken, l * 3 + 3)
                else:
                    pe.wait_ge(kd_ready, l * (LEVELS - 1) + i)
                    pe.wait_ge(level_taken, l * LEVELS + i)
                keys = hk if i == 0 else kd
                for hd in range(HG_HEADS):
                    def pairs(b, col, s, t, size_s, size_t):
                        return pe.matmul(bank[b][0:size_s, col:col + size_t], keys[:, hd, s:s + size_s],
                                         qd[:, hd, t:t + size_t], start=True, stop=True)
                    if i < MASKED_LEVELS:
                        pairs(4, hd * P, 0, 0, P, P)
                        mm = pairs(5, hd * P, P, P, P, P)
                        if HALF[i] <= 8:
                            mm = pairs(6, hd * 16, 2 * P, 2 * P, 16, 16)
                    elif HALF[i] == P:
                        mm = pairs(4, hd * P, 0, P, P, P)
                    else:
                        pairs(4, hd * 16, 0, 2 * P, P, 16)
                        mm = pairs(4, 64 + hd * 16, P, 2 * P, P, 16)
                mm.then_inc(level_done, 1)

            def recurrent():
                q, j, x, n, c = (REC[k] for k in "qjxnc")
                for t in range(16):
                    k8_tile(q + t // RING, t % RING, None if t < 4 else j + t - 3, t % 4, (xhi, xlo), c,
                            inputs_ready(x) if t == 0 else None)
                    if t == 0:
                        norm_sum(acc[:, c:T], c, sq_made, SQUARES[n])
                for t in range(16, 32):
                    hd, u = (t - 16) // 4, (t - 16) % 4
                    pe.wait_ge(lo_made, (q + 4 + hd // RING) * RING + hd % RING + 1)
                    pe.wait_ge(cv_lo_made, 2 * hd + 2)
                    pe.wait_ge(tile_read, j + t - 3)
                    split_product(bank[t % 4][:, 0:T - c], [(hd % RING, 2 * u + i) for i in range(2)],
                                  lambda i: cvhi[:, 2 * hd + i, :], lambda i: cvlo[:, 2 * hd + i, :])
                for m in range(KD):
                    t = 32 + m
                    k8_tile(q + 5 + m // RING, m % RING, j + t - 1 if m >= 2 else None, 4 + m % 2, (outhi, outlo), c,
                            (lambda i: pe.wait_ge(out_lo_made, i + 1)) if m == 0 else None)
                norm_sum(acc[:, c:T], c, sq_made, SQUARES[n + 1])

            def keys_values():
                q, j, x, n, c = (KV[k] for k in "qjxnc")
                for t in range(16):
                    k8_tile(q + t // RING, t % RING, None if t < 4 else j + t - 3, t % 4, (midhi, midlo), c,
                            inputs_ready(x) if t == 0 else None)
                    if t == 0:
                        norm_sum(acc[:, c:T], c, sq_made, SQUARES[n])
                        pe.wait_ge(rel_in, 32)
                        pe.matmul(bank[6][0:HEADS, :], relt[0:N_BUCKETS + 1, :], onehot[0:N_BUCKETS + 1, :],
                                  start=True, stop=True).then_inc(brow_done, 1)
                    if t >= 9:
                        turn_value(t - 9, j)
                turn_value(7, j)

            def turn_value(m, j):
                pe.wait_ge(tile_read, j + 8 + m + 1)
                if m >= 2:
                    pe.wait_ge(kv_taken, m - 1)
                for s in range(2):
                    tr = pe.transpose(bank[4 + m % 2][:, s * P:s * P + P],
                                      z[:, m % 4, N_META + s * P:N_META + s * P + P], ident)
                tr.then_inc(kv_turned, 1)

            def attention():
                q, j, x, n, c = (ATT[k] for k in "qjxnc")
                for t in range(8):
                    k8_tile(q + t // RING, t % RING, None if t < 4 else j + t - 3, t % 4, (xhi, xlo), c,
                            inputs_ready(x) if t == 0 else None)
                    if t == 0:
                        norm_sum(acc[:, c:T], c, sq_made, SQUARES[n])
                pe.wait_ge(tile_read, j + 8)
                scores2(0)
                for hd in range(HEADS):
                    if hd + 1 < HEADS:
                        scores2(hd + 1)
                    p = hd % 2
                    pe.wait_ge(s2_normed, hd + 1)
                    if hd >= 1:
                        pe.wait_ge(s2_taken, hd)
                    pe.transpose(bank[6][:, 0:P], sc2[:, p, 0:P], ident)
                    pe.transpose(bank[6][:, P:2 * P], sc2[:, p, P:2 * P], ident)
                    pe.transpose(bank[6][:, 2 * P:3 * P], sc2[:, p, 2 * P:3 * P], ident).then_inc(s2_turned, 1)
                    pe.wait_ge(s2_taken, hd + 1)
                    if hd >= 2:
                        pe.wait_ge(o2_lo, hd - 1)
                    v = slice(hd * P, hd * P + P)
                    pe.matmul(bank[p][:, 0:SEQ], vt2[:, 0, v], pt2[:, p, 0:2 * P], start=True, stop=False)
                    pe.matmul(bank[p][:, P:SEQ], vt2[:, 1, v], pt2[:, p, 2 * P:3 * P], start=False,
                              stop=True).then_inc(o2_done, 1)
                pe.wait_ge(o2_lo, HEADS)
                for m in range(KD):
                    t = 8 + m
                    k8_tile(q + 2 + m // RING, m % RING, j + t - 1 if m >= 2 else None, 4 + m % 2, (midhi, midlo), c)
                norm_sum(acc[:, c:T], c, sq_made, SQUARES[n + 1])

            def scores2(hd):
                if hd >= 2:
                    pe.wait_ge(s2_max, hd - 1)
                pe.matmul(bank[4 + hd % 2][:, 0:P], q2[:, hd, 0:P], k2[:, hd, 0:P], start=True, stop=True)
                pe.matmul(bank[4 + hd % 2][:, P:3 * P], q2[:, hd, P:SEQ], k2[:, hd, :], start=True,
                          stop=True).then_inc(s2_done, 1)

            pe.wait_ge(consts_in, 48)
            with pe.Fori(0, DEPTH) as l:
                ffn(**layer_stage(l, 0))
                mixer(l)
                ffn(**layer_stage(l, 2))
            norm_sum(acc[:, :], 0, sq_made, SQUARES[10])
            post_ffn = lambda st, post: norm_sum(acc[:, N_META:T], N_META, sq_made, SQUARES[post])
            ffn(**F4)
            post_ffn(F4, 12)
            recurrent()
            ffn(**F5)
            post_ffn(F5, 16)
            keys_values()
            ffn(**F6, main_norm=False)
            post_ffn(F6, 18)
            attention()
            ffn(**F7)
            post_ffn(F7, 22)

        @block.scalar
        def _(act):
            def split_hi(q, k, cols, done):
                act.wait_ge(landed[k], (q + 1) * 16)
                if not isinstance(done, int) or done > 0:
                    act.wait_ge(tile_done, done)
                act.activation(whi[:, k, 0:cols], raw[:, k, 0:cols], ACT.Copy).then_inc(hi_made, 1)

            def norm_std(n, c, out=std, size=D_MODEL):
                act.wait_ge(sum_made, n + 1)
                act.activation(out[:, c:T], bank[NORM][:, 0:T - c], ACT.Sqrt, scale=1.0 / size,
                               bias=eps).then_inc(std_made, 1)

            def x_hi(x, k, c, to=xhi):
                at_k = bass.ds(k, 1) if not isinstance(k, int) else slice(k, k + 1)
                act.activation(to[:, at_k, c:T], h[:, at_k, c:T], ACT.Identity, scale=gain(x, k)).then_inc(x_hi_made, 1)

            def ffn(q, j, x, n, f, c, main_norm=True):
                def quad(b, next_cols, first=False):
                    for p in range(2):
                        i = b * 2 + p
                        tile = b * RING + j + 2 * p
                        split_hi(b + q + 1, 2 * p, next_cols, tile + 1)
                        if first and p == 0 and main_norm:
                            norm_std(n, c)
                        act.wait_ge(tile_read, tile + 1)
                        if not first:
                            act.wait_ge(hid_made, f * KF + i - 1)
                        act.activation(sil[:, p, c:T], z[:, p, c:T], ACT.Silu).then_inc(silu_made, 1)
                        split_hi(b + q + 1, 2 * p + 1, next_cols, tile + 2)
                        act.wait_ge(hid_made, f * KF + i + 1)
                        at_i = bass.ds(i, 1) if not isinstance(i, int) else slice(i, i + 1)
                        act.activation(hidhi[:, at_i, c:T], z[:, 2 + p:3 + p, c:T], ACT.Copy).then_inc(hid_hi_made, 1)

                quad(0, CH8, first=True)
                with act.Fori(1, FFN_GU_QUADS - 1) as b:
                    quad(b, CH8)
                quad(FFN_GU_QUADS - 1, CH11)

            def ffn_down(q, j, x, n, f, c, main_norm=True, tail=True):
                def quad(b, next_cols):
                    for p in range(2):
                        done = b * 2 + j + 2 * KF + p + 1
                        if in_layers(c):
                            act.wait_ge(tile_read, done)
                            x_hi(x + 1, b * 2 + p, c)
                        if next_cols:
                            for k in (2 * p, 2 * p + 1):
                                split_hi(b + q + FFN_GU_QUADS + 1, k, next_cols, done)

                with act.Fori(0, FFN_DOWN_QUADS - 1) as b:
                    quad(b, CH11)
                quad(FFN_DOWN_QUADS - 1, CH8 if tail else 0)

            def in_layers(c):
                return c == 0

            def mixer(l):
                st = layer_stage(l, 1)
                q, j, x, n = st["q"], st["j"], st["x"], st["n"]
                for step, i in MIXER:
                    if step == "tile":
                        t = i
                        read = j + t + 1
                        if t == 0:
                            norm_std(n, 0)
                        if t < HI:
                            act.wait_ge(tile_read, read)
                            act.activation(pre[:, t, :], z[:, t % 4, :], ACT.Sigmoid)
                            act.activation(hk[:, t, :], z[:, t % 4, :], ACT.Sigmoid, scale=-1.0).then_inc(act_took, 1)
                        elif HQ <= t < CQ:
                            to, func = ((hq, ACT.Silu) if t < HGATE else (gate, ACT.Silu) if t < GA else
                                        (sga, ACT.Sigmoid) if t < GB else (sgb, ACT.Sigmoid))
                            k = t - (HQ if t < HGATE else HGATE if t < GA else GA if t < GB else GB)
                            act.wait_ge(tile_read, read)
                            act.activation(to[:, k, :], z[:, t % 4, :], func).then_inc(act_took, 1)
                        elif CQ <= t < KPE:
                            act.wait_ge(tile_read, read)
                            act.activation(lathi[:, t - CQ, :], z[:, t % 4, :], ACT.Identity,
                                           scale=small(l, t - CQ)).then_inc(act_took, 1)
                        elif PR <= t < OUT:
                            m = t - PR
                            act.wait_ge(merged, l * 8 + m + 1)
                            act.activation(midhi[:, m, :], sga[:, m, :], ACT.Copy).then_inc(mid_hi_made, 1)
                        elif t >= OUT:
                            act.wait_ge(tile_read, read)
                            x_hi(x + 1, t - OUT, 0)
                        for ch in chunks_ended(t):
                            split_hi(q + (ch + RING) // RING, ch % RING, CH8, j + t + 1)
                    elif step == "turn_v":
                        for s, (_, size) in enumerate(TOKEN_TILES):
                            act.wait_ge(v_turned, l * 3 + s + 1)
                            act.activation(vtok[0:size, s, :], bank[4 + s][0:size, :], ACT.Copy).then_inc(v_taken, 1)
                    elif step == "decay":
                        act.wait_ge(decay_made, l + 1)
                        act.activation(pre[:, :, :], pre[:, :, :], ACT.Ln).then_inc(log_made, 1)
                    elif step == "level" and i >= 1:
                        act.wait_ge(sums_ready, l * (LEVELS - 1) + i)
                        act.wait_ge(level_done, l * LEVELS + i)
                        act.activation(qd[:, :, :], pre[:, :, :], ACT.Exp)
                        act.activation(kd[:, :, :], suf[:, :, :], ACT.Exp).then_inc(exp_made, 1)
                    elif step == "rec_out":
                        act.wait_ge(rec_done, l * 4 + i + 1)
                        act.activation(pre[:, i, :], bank[4 + i % 2][:, 0:T], ACT.Copy)
                        act.activation(suf[:, i, :], bank[4 + i % 2][:, 0:T], ACT.Square).then_inc(rec_taken, 1)
                    elif step == "rec_norm":
                        act.wait_ge(rec_sum, l * 4 + i + 1)
                        act.activation(kd[:, i, :], bank[6][:, 0:T], ACT.Sqrt, scale=1.0 / HG_DIM,
                                       bias=eps).then_inc(rec_std, 1)
                        act.wait_ge(rec_f, l * 4 + i + 1)
                        act.activation(rechi[:, i, :], pre[:, i, :], ACT.Copy).then_inc(rec_hi, 1)
                    elif step == "latent_norm":
                        if i == 1:
                            act.wait_ge(rstd_made, n + 2)
                        norm_std(n + 1 + i, 0, size=(Q_LORA, KV_LORA)[i])
                    elif step == "turn_v2":
                        for s, (_, size) in enumerate(TOKEN_TILES):
                            act.wait_ge(v2_turned, l * 3 + s + 1)
                            act.activation(vtok2[0:size, s, :], bank[4 + s][0:size, :], ACT.Copy).then_inc(v2_taken, 1)
                    elif step == "scores":
                        hd, p = i, i % 2
                        act.wait_ge(max_made, l * HEADS + hd + 1)
                        for e, (rows, a0, a1) in enumerate(SCORE_ROWS):
                            last = act.activation(sc[0:rows, p, a0:a1], sc[0:rows, p, a0:a1], ACT.Exp,
                                                  bias=negmax[0:rows, p, e:e + 1],
                                                  accum_out=sums[0:rows, p, e:e + 1])
                        last.then_inc(probs_made, 1)
                    elif step == "attend":
                        hd, p = i, i % 2
                        act.wait_ge(probs_turned, l * HEADS + hd + 1)
                        if hd >= 2:
                            act.wait_ge(att_done, l * HEADS + hd - 1)
                        act.activation(pt[:, p, 0:T + P + 16], bank[6][:, 0:T + P + 16], ACT.Copy)
                        act.activation(pt[0:16, p, T + P + 16:T + P + 32], bank[6][0:16, T + P + 16:T + P + 32],
                                       ACT.Copy).then_inc(probs_taken, 1)
                        if hd % 2 == 1:
                            act.wait_ge(att_done, l * HEADS + hd + 1)
                            act.activation(atthi[:, hd // 2, :], bank[hd // 2 % 2][:, 0:T], ACT.Copy).then_inc(att_hi, 1)

            def small(l, k):
                return vec[:, bass.ds(l * 6 + VEC["small"] + k, 1)]

            def inputs_from_h(x, u, c, to=xhi):
                for k in range(KD):
                    act.wait_ge(h_made, 8 * (u - 7) + k + 1)
                    x_hi(x, k, c, to)

            def recurrent():
                q, j, x, n, c = (REC[k] for k in "qjxnc")
                for t in range(16):
                    split_hi(q + 1 + t // RING, t % RING, CH8, j + t + 1)
                    if t == 0:
                        norm_std(n, c)
                    act.wait_ge(tile_read, j + t + 1)
                    m = t % 8
                    if t < 8:
                        if m >= 2:
                            act.wait_ge(conv_made, m - 1)
                        else:
                            act.wait_ge(xb_made, 1)
                        act.activation(xb[:, m % 2, 3:], z[:, t % 4, c:T], ACT.Identity, bias=vcol("b_in", m))
                        act.drain()
                        act.activation(cv[:, m, :], xb[:, m % 2, 3:], ACT.Identity, scale=vcol("conv_w", 24 + m),
                                       bias=vcol("conv_b", m)).then_inc(conv_begun, 1)
                        if m >= 1:
                            conv_hi(m - 1)
                    else:
                        if m == 0:
                            conv_hi(7)
                        act.activation(yg[:, m, :], z[:, t % 4, c:T], ACT.Gelu_apprx_tanh,
                                       bias=vcol("b_in", 8 + m)).then_inc(b_act_took, 1)
                for t in range(16, 32):
                    hd, u = (t - 16) // 4, (t - 16) % 4
                    to = (sr, si)[u // 2]
                    act.wait_ge(tile_read, j + t + 1)
                    act.activation(to[:, 2 * hd + u % 2, :], z[:, t % 4, c:T], ACT.Sigmoid).then_inc(b_act_took, 1)
                    if u == 3:
                        split_hi(q + 5 + hd // RING, hd % RING, CH8, j + t + 1)
                act.drain()
                act.wait_ge(coef_made, 1)
                for m in range(KD):
                    act.activation(y[:, m, 0:SEQ], sr[:, m, :], ACT.Tanh, scale=lam[:, 0, m:m + 1])
                act.drain()
                for m in range(KD):
                    act.activation(sr[:, m, :], sr[:, m, :], ACT.Exp, scale=lam[:, 0, m:m + 1]).then_inc(decay2_made, 1)
                act.wait_ge(root_asked, 1)
                act.activation(y[:, :, 0:SEQ], y[:, :, 0:SEQ], ACT.Sqrt, scale=-1.0).then_inc(root_made, 1)
                for m in range(KD):
                    act.wait_ge(out_f, m + 1)
                    act.activation(outhi[:, m, :], yg[:, m, :], ACT.Copy).then_inc(out_hi_made, 1)
                for m in range(KD):
                    split_hi(q + 6 + m // RING, m % RING, CH8, j + 32 + m + 1)
                norm_std(n + 1, c)
                inputs_from_h(9, 9, c)

            def conv_hi(m):
                act.wait_ge(conv_made, m + 1)
                act.activation(cvhi[:, m, :], cv[:, m, :], ACT.Copy).then_inc(cv_hi_made, 1)

            def keys_values():
                q, j, x, n, c = (KV[k] for k in "qjxnc")
                for t in range(16):
                    split_hi(q + 1 + t // RING, t % RING, CH8, j + t + 1)
                    if t == 0:
                        norm_std(n, c)
                        act.wait_ge(brow_done, 1)
                        act.activation(brow[0:HEADS, :], bank[6][0:HEADS, :], ACT.Copy).then_inc(brow_made, 1)
                    if t < 8:
                        x_hi(11, t, c)
                    if t >= 9:
                        value_out(t - 9)
                value_out(7)

            def value_out(m):
                act.wait_ge(kv_turned, m + 1)
                act.activation(vt2[:, :, m * P:m * P + P],
                               bank[4 + m % 2][:, 0:2 * P].rearrange("p (s d) -> p s d", s=2), ACT.Copy
                               ).then_inc(kv_taken, 1)

            def attention():
                q, j, x, n, c = (ATT[k] for k in "qjxnc")
                for t in range(8):
                    split_hi(q + 1 + t // RING, t % RING, CH8, j + t + 1)
                    if t == 0:
                        norm_std(n, c)

                def exponentials(hd):
                    p = hd % 2
                    act.wait_ge(s2_max, hd + 1)
                    for e, (rows, a0, a1) in enumerate(SCORE_ROWS[0:2]):
                        last = act.activation(sc2[:, p, a0:a1], sc2[:, p, a0:a1], ACT.Exp,
                                              bias=negmax[:, p, e:e + 1], accum_out=sums[:, p, e:e + 1])
                    last.then_inc(s2_exp, 1)

                exponentials(0)
                for hd in range(HEADS):
                    if hd + 1 < HEADS:
                        exponentials(hd + 1)
                    p = hd % 2
                    act.wait_ge(s2_turned, hd + 1)
                    if hd >= 2:
                        act.wait_ge(o2_done, hd - 1)
                    act.activation(pt2[:, p, :], bank[6][:, 0:3 * P], ACT.Copy).then_inc(s2_taken, 1)
                    act.wait_ge(o2_done, hd + 1)
                    act.activation(midhi[:, hd, c:T], bank[p][:, 0:SEQ], ACT.Copy).then_inc(o2_hi, 1)
                for m in range(KD):
                    split_hi(q + 3 + m // RING, m % RING, CH8, j + 8 + m + 1)
                norm_std(n + 1, c)
                inputs_from_h(13, 12, c)

            act.wait_ge(h_in, 16)
            act.wait_ge(consts_in, 48)
            for k in range(KD):
                x_hi(0, k, 0)
            for k in range(RING):
                split_hi(0, k, CH8, 0)
            act.wait_ge(lb_asked, 1)
            act.activation(lb[:, 2, :], lb[:, 2, :], ACT.Exp).then_inc(lb_exp, 1)
            act.wait_ge(lam_asked, 1)
            act.activation(lam[:, 1, :], lam[:, 1, :], ACT.Exp).then_inc(lam_step, 1)
            act.wait_ge(lam_asked, 2)
            act.activation(lam[:, 3, :], lam[:, 2, :], ACT.Ln).then_inc(lam_step, 1)
            with act.Fori(0, DEPTH) as l:
                ffn(**layer_stage(l, 0))
                ffn_down(**layer_stage(l, 0))
                mixer(l)
                ffn(**layer_stage(l, 2))
                ffn_down(**layer_stage(l, 2))
            norm_std(10, 0)
            inputs_from_h(7, 7, N_META)
            ffn(**F4)
            ffn_down(**F4)
            norm_std(12, N_META)
            inputs_from_h(8, 8, N_META)
            recurrent()
            ffn(**F5)
            ffn_down(**F5)
            norm_std(16, N_META)
            inputs_from_h(10, 10, N_META, midhi)
            keys_values()
            ffn(**F6, main_norm=False)
            ffn_down(**F6)
            norm_std(18, N_META)
            inputs_from_h(12, 11, N_META)
            attention()
            ffn(**F7)
            ffn_down(**F7, tail=False)
            norm_std(22, N_META)

        @block.vector
        def _(dve):
            def split_lo(q, k, cols):
                dve.wait_ge(hi_made, q * RING + k + 1)
                dve.tensor_tensor(wlo[:, k, 0:cols], raw[:, k, 0:cols], whi[:, k, 0:cols].bitcast(F32),
                                  ALU.subtract).then_inc(lo_made, 1)

            def norm_rstd(n, c, to=rstd):
                dve.wait_ge(std_made, n + 1)
                dve.reciprocal(to[:, c:T], std[:, c:T]).then_inc(rstd_made, 1)
                dve.drain()

            def x_lo(x, k, c, to=xlo, hi=xhi):
                at_k = bass.ds(k, 1) if not isinstance(k, int) else slice(k, k + 1)
                dve.wait_ge(x_hi_made, x * 8 + k + 1)
                dve.scalar_tensor_tensor(to[:, at_k, c:T], h[:, at_k, c:T], gain(x, k),
                                         hi[:, at_k, c:T].bitcast(F32), ALU.mult, ALU.subtract).then_inc(x_lo_made, 1)

            def ffn(q, j, x, n, f, c, main_norm=True):
                def quad(b, next_cols, first=False):
                    for p in range(2):
                        i = b * 2 + p
                        tile = b * RING + j + 2 * p
                        dve.wait_ge(tile_done, tile + 1)
                        if first and p == 0 and main_norm:
                            norm_rstd(n, c)
                        if not first:
                            dve.wait_ge(silu_made, f * KF + i - 1)
                        dve.tensor_tensor(z[:, p, c:T], bank[2 * p][:, 0:T - c], rstd[:, c:T],
                                          ALU.mult).then_inc(tile_read, 1)
                        split_lo(b + q + 1, 2 * p, next_cols)
                        dve.wait_ge(tile_done, tile + 2)
                        if not first:
                            dve.wait_ge(hid_lo_made, f * KF + i - 1)
                        dve.tensor_tensor(z[:, 2 + p, c:T], bank[2 * p + 1][:, 0:T - c], rstd[:, c:T],
                                          ALU.mult).then_inc(tile_read, 1)
                        split_lo(b + q + 1, 2 * p + 1, next_cols)

                quad(0, CH8, first=True)
                with dve.Fori(1, FFN_GU_QUADS - 1) as b:
                    quad(b, CH8)
                quad(FFN_GU_QUADS - 1, CH11)

            def ffn_down(q, j, x, n, f, c, main_norm=True, tail=True):
                def quad(b, next_cols):
                    for p in range(2):
                        m = b * 2 + p
                        at_m = bass.ds(m, 1) if not isinstance(m, int) else slice(m, m + 1)
                        dve.wait_ge(tile_done, m + j + 2 * KF + 1)
                        if c == 0:
                            dve.scalar_tensor_tensor(h[:, at_m, c:T], bank[4 + p][:, 0:T - c].unsqueeze(1), 0.5,
                                                     h[:, at_m, c:T], ALU.mult, ALU.add).then_inc(tile_read, 1)
                        else:
                            dve.tensor_copy(y[:, at_m, c:T], bank[4 + p][:, 0:T - c].unsqueeze(1)).then_inc(tile_read, 1)
                        if c == 0:
                            x_lo(x + 1, m, c)
                        if next_cols:
                            split_lo(b + q + FFN_GU_QUADS + 1, 2 * p, next_cols)
                            split_lo(b + q + FFN_GU_QUADS + 1, 2 * p + 1, next_cols)

                with dve.Fori(0, FFN_DOWN_QUADS - 1) as b:
                    quad(b, CH11)
                quad(FFN_DOWN_QUADS - 1, CH8 if tail else 0)

            def mixer(l):
                st = layer_stage(l, 1)
                q, j, x, n = st["q"], st["j"], st["x"], st["n"]

                def tile(t):
                    b = bank[t % 4 if t < OUT else 4 + t % 2][:, 0:T]
                    dve.wait_ge(tile_done, j + t + 1)
                    if t == 0:
                        norm_rstd(n, 0)
                    plain = {HI: (qd, 0), HQ: (z, None), UQ: (qn, 0)}
                    if t < HI or HQ <= t < UQ:
                        if t >= KPE:
                            dve.wait_ge(lat_z, l * 5 + t - 4 - CQ + 1)
                        elif t >= 4:
                            dve.wait_ge(act_took, l * GATED + gated(slot_before(t)))
                            if t - 4 >= CQ:
                                dve.wait_ge(lat_z, l * 5 + t - 4 - CQ + 1)
                        dve.tensor_tensor(z[:, t % 4, :], b, rstd[:, :], ALU.mult).then_inc(tile_read, 1)
                        if CQ < t <= KPE:
                            latent_lo(t - 1)
                        if t == KPS:
                            dve.drain()
                            dve.tensor_tensor(z[:, KPE % 4, :], z[:, KPE % 4, :], const("cos", T), ALU.mult)
                            dve.tensor_tensor(z[:, KPS % 4, :], z[:, KPS % 4, :], const("sin", T), ALU.mult)
                            dve.drain()
                            dve.tensor_tensor(krot[:, :], z[:, KPE % 4, :], z[:, KPS % 4, :],
                                              ALU.add).then_inc(krot_made, 1)
                    elif t < HQ:
                        dve.tensor_tensor(qd[:, t - HI, :], b, rstd[:, :], ALU.mult).then_inc(tile_read, 1)
                    elif t < UKV:
                        m = t - UQ
                        if m == 0:
                            dve.wait_ge(rec_lo, l * 4 + 4)
                        to = qn[:, m, :] if m < 4 else qr[:, m - 4, :] if m < 6 else z[:, t % 4, :]
                        dve.scalar_tensor_tensor(to, b, QK_SCALE, rlat[:, 0, :], ALU.mult, ALU.mult
                                                 ).then_inc(tile_read, 1)
                        if m >= 6:
                            dve.drain()
                            dve.tensor_tensor(z[:, t % 4, :], z[:, t % 4, :], const("sin", T), ALU.mult)
                            dve.tensor_tensor(qr[:, m - 6, :], qr[:, m - 6, :], const("cos", T), ALU.mult)
                            dve.drain()
                            dve.tensor_tensor(qr[:, m - 6, :], qr[:, m - 6, :], z[:, t % 4, :],
                                              ALU.add).then_inc(qrot_made, 1)
                    elif t < PA:
                        m = t - UKV
                        to = kn[:, m, :] if m < 4 else z[:, m - 4, :]
                        dve.tensor_tensor(to, b, rlat[:, 1, :], ALU.mult).then_inc(tile_read, 1)
                    elif t < PR:
                        m = t - PA
                        dve.tensor_tensor(sga[:, m, :], b, sga[:, m, :], ALU.mult).then_inc(tile_read, 1)
                    elif t < OUT:
                        m = t - PR
                        if m >= 4:
                            dve.wait_ge(merged, l * 8 + m - 3)
                        dve.tensor_tensor(z[:, t % 4, :], b, sgb[:, m, :], ALU.mult).then_inc(tile_read, 1)
                    else:
                        m = t - OUT
                        dve.tensor_tensor(h[:, m, :], b, h[:, m, :], ALU.add).then_inc(tile_read, 1)
                        x_lo(x + 1, m, 0)
                    for ch in chunks_ended(t):
                        split_lo(q + (ch + RING) // RING, ch % RING, CH8)

                def latent_lo(t):
                    dve.wait_ge(act_took, l * GATED + gated(t))
                    dve.scalar_tensor_tensor(latlo[:, t - CQ, :], z[:, t % 4, :], small(l, t - CQ),
                                             lathi[:, t - CQ, :].bitcast(F32), ALU.mult, ALU.subtract
                                             ).then_inc(lat_lo, 1)

                def decay():
                    dve.wait_ge(act_took, l * GATED + 4)
                    for hd in range(HG_HEADS):
                        col = bass.ds(l * HG_HEADS + hd, 1)
                        dve.tensor_scalar(pre[:, hd, :], pre[:, hd, :], one_lb[:, col], lbs[:, col], ALU.mult, ALU.add)
                        dve.tensor_scalar(hk[:, hd, :], hk[:, hd, :], one_lb[:, col], None, ALU.mult)
                    dve.drain()
                    dve.tensor_scalar(pre[:, :, :], pre[:, :, :], F_MIN, None, ALU.max)
                    dve.drain()
                    dve.tensor_scalar(suf[:, :, :], pre[:, :, :], LN_SPLIT, 1.0 / LN_SPLIT - 1.0, ALU.is_lt, ALU.mult)
                    dve.drain()
                    dve.scalar_tensor_tensor(flat(pre), flat(suf), 1.0, flat(pre), ALU.add, ALU.mult
                                             ).then_inc(decay_made, 1)
                    for b in (dec0, dec1, dec2):
                        dve.memset(b[:, :, :], 0.0)
                    dve.wait_ge(log_made, l + 1)
                    dve.scalar_tensor_tensor(flat(pre), flat(suf), -LN_SHIFT * LN_SPLIT, flat(pre), ALU.mult, ALU.add)
                    dve.drain()
                    dve.memset(suf[:, :, :], 0.0).then_inc(sums_ready, 1)

                def level(i):
                    if i == 0:
                        dve.wait_ge(act_took, l * GATED + gated(HQ + 3))
                        dve.wait_ge(v_turned, l * 3 + 3)
                        dve.tensor_scalar(qd[:, :, :], hq[:, :, :], HG_SCALE, None, ALU.mult).then_inc(level_ready, 1)
                        return
                    dve.wait_ge(exp_made, l * (LEVELS - 1) + i)
                    dve.scalar_tensor_tensor(flat(qd), flat(qd), HG_SCALE, flat(hq), ALU.mult, ALU.mult
                                             ).then_inc(level_ready, 1)
                    if i < LEVELS - 1:
                        half = HALF[i]
                        if half <= 8:
                            cut = lambda b: flat(b).rearrange("p (b two m) -> p b two m", two=2, m=half)
                            first, second = (lambda v: v[:, :, 0, :]), (lambda v: v[:, :, 1, :])
                            end = lambda v, side: v[:, :, side, half - 1:half]
                        else:
                            cut = lambda b: b[:, :, 0:2 * P].rearrange("p h (b two m) -> p h b two m", two=2, m=half)
                            first, second = (lambda v: v[:, :, :, 0, :]), (lambda v: v[:, :, :, 1, :])
                            end = lambda v, side: v[:, :, :, side, half - 1:half]
                        vs, vp = cut(suf), cut(pre)
                        dve.tensor_tensor(first(vs), first(vs), end(vp, 1).to_broadcast(list(first(vs).shape)), ALU.add)
                        dve.drain()
                        dve.tensor_tensor(second(vp), second(vp), end(vp, 0).to_broadcast(list(second(vp).shape)),
                                          ALU.add).then_inc(sums_ready, 1)

                def take(i):
                    dve.wait_ge(level_done, l * LEVELS + i + 1)
                    dve.memset(idle[:, :], 0.0)
                    by_head = lambda b, size: bank[b][:, 0:4 * size].rearrange("p (h t) -> p h t", h=4)
                    if i < MASKED_LEVELS:
                        mask = masks[:, i, :].unsqueeze(1).to_broadcast([P, 4, P])
                        if HALF[i] <= 8:
                            dve.copy_predicated(dec2[0:16, :, :], masks[0:16, i, 0:16].unsqueeze(1).to_broadcast([16, 4, 16]),
                                                by_head(6, 16)[0:16])
                        dve.copy_predicated(dec0[:, :, 0:P], mask, by_head(4, P))
                        dve.copy_predicated(dec1[:, :, 0:P], mask, by_head(5, P)).then_inc(level_taken, 1)
                    elif HALF[i] == P:
                        dve.tensor_copy(dec0[:, :, P:2 * P], by_head(4, P)).then_inc(level_taken, 1)
                    else:
                        dve.tensor_copy(dec0[:, :, 2 * P:T], by_head(4, 16))
                        dve.tensor_copy(dec1[:, :, P:P + 16],
                                        bank[4][:, 64:128].rearrange("p (h t) -> p h t", h=4)).then_inc(level_taken, 1)

                def scores(hd):
                    p = hd % 2
                    dve.wait_ge(scores_done, l * HEADS + hd + 1)
                    if hd >= 2:
                        dve.wait_ge(probs_turned, l * HEADS + hd - 1)
                    dve.tensor_tensor(sc[:, p, 0:3 * P], bank[4 + p][:, 0:3 * P], const("causal", 3 * P), ALU.add)
                    dve.tensor_tensor(sc[0:16, p, 3 * P:3 * P + T], bank[2 + p][0:16, 0:T],
                                      const("causal_tail", T)[0:16], ALU.add)
                    dve.drain()
                    for e, (rows, a0, a1) in enumerate(SCORE_ROWS):
                        last = dve.tensor_reduce(negmax[0:rows, p, e:e + 1], sc[0:rows, p, a0:a1], AX_X, ALU.max,
                                                 negate=True)
                    last.then_inc(max_made, 1)

                def attend(hd):
                    p = hd % 2
                    dve.wait_ge(probs_made, l * HEADS + hd + 1)
                    dve.reciprocal(sums[:, p, 0:2], sums[:, p, 0:2])
                    dve.reciprocal(sums[0:16, p, 2:3], sums[0:16, p, 2:3])
                    dve.drain()
                    for e, (rows, a0, a1) in enumerate(SCORE_ROWS):
                        last = dve.tensor_scalar(sc[0:rows, p, a0:a1], sc[0:rows, p, a0:a1],
                                                 sums[0:rows, p, e:e + 1], None, ALU.mult)
                    last.then_inc(probs_normed, 1)
                    if hd % 2 == 0 and hd >= 2:
                        pair_lo(hd // 2 - 1)

                def pair_lo(pair):
                    dve.wait_ge(att_hi, l * 4 + pair + 1)
                    dve.tensor_tensor(attlo[:, pair, :], bank[pair % 2][:, 0:T], atthi[:, pair, :].bitcast(F32),
                                      ALU.subtract).then_inc(att_lo, 1)

                for step, i in MIXER:
                    if step == "tile":
                        if i == PA:
                            pair_lo(3)
                        tile(i)
                    elif step == "decay":
                        decay()
                    elif step == "level":
                        if i >= 1:
                            take(i - 1)
                        level(i)
                    elif step == "rec_out" and i == 0:
                        take(LEVELS - 1)
                    elif step == "rec_norm":
                        dve.wait_ge(rec_std, l * 4 + i + 1)
                        dve.reciprocal(kd[:, i, :], kd[:, i, :])
                        dve.drain()
                        dve.scalar_tensor_tensor(pre[:, i, :], pre[:, i, :], small(l, 5), kd[:, i, :],
                                                 ALU.mult, ALU.mult)
                        dve.drain()
                        dve.tensor_tensor(pre[:, i, :], pre[:, i, :], gate[:, i, :], ALU.mult).then_inc(rec_f, 1)
                    elif step == "latent_norm":
                        norm_rstd(n + 1 + i, 0, rlat[:, i, :])
                    elif step == "scores":
                        scores(i)
                    elif step == "attend":
                        attend(i)

            def flat(b):
                return b[:, :, :].rearrange("p h t -> p (h t)")

            def small(l, k):
                return vec[:, bass.ds(l * 6 + VEC["small"] + k, 1)]

            def update(n, post, weight, c=N_META):
                norm_rstd(n, c)
                for k in range(KD):
                    dve.scalar_tensor_tensor(y[:, k, c:T], y[:, k, c:T], vcol(*post(k)), rstd[:, c:T],
                                             ALU.mult, ALU.mult)
                dve.drain()
                for k in range(KD):
                    dve.scalar_tensor_tensor(h[:, k, c:T], y[:, k, c:T], weight, h[:, k, c:T],
                                             ALU.mult, ALU.add).then_inc(h_made, 1)

            def recurrent():
                q, j, x, n, c = (REC[k] for k in "qjxnc")

                def conv(m):
                    dve.wait_ge(conv_begun, m + 1)
                    for tap in range(3):
                        op = dve.scalar_tensor_tensor(cv[:, m, :], xb[:, m % 2, tap:tap + SEQ],
                                                      vcol("conv_w", 8 * tap + m), cv[:, m, :], ALU.mult, ALU.add)
                        if tap < 2:
                            dve.drain()
                    op.then_inc(conv_made, 1)

                dve.wait_ge(tile_done, j)
                dve.memset(xb[:, :, 0:3], 0.0).then_inc(xb_made, 1)
                for t in range(32):
                    dve.wait_ge(tile_done, j + t + 1)
                    if t == 0:
                        norm_rstd(n, c)
                    if 4 <= t < 12:
                        dve.wait_ge(conv_begun, t - 3)
                    elif t >= 12:
                        dve.wait_ge(b_act_took, t - 11)
                    if t < 16:
                        dve.tensor_tensor(z[:, t % 4, c:T], bank[t % 4][:, 0:SEQ], rstd[:, c:T],
                                          ALU.mult).then_inc(tile_read, 1)
                        if 1 <= t <= 8:
                            conv(t - 1)
                    else:
                        hd, u = (t - 16) // 4, (t - 16) % 4
                        dve.tensor_scalar(z[:, t % 4, c:T], bank[t % 4][:, 0:SEQ],
                                          vcol(("b_r", "b_i")[u // 2], 2 * hd + u % 2), None,
                                          ALU.add).then_inc(tile_read, 1)
                    if t < 16:
                        split_lo(q + 1 + t // RING, t % RING, CH8)
                    elif (t - 16) % 4 == 3:
                        split_lo(q + 5, (t - 16) // 4, CH8)
                dve.wait_ge(decay2_made, KD)
                dve.tensor_tensor(q2[:, :, :], sr[:, :, :], sr[:, :, :], ALU.mult)
                dve.drain()
                dve.scalar_tensor_tensor(y[:, :, 0:SEQ], q2[:, :, :], 1.0, y[:, :, 0:SEQ],
                                         ALU.add, ALU.mult).then_inc(root_asked, 1)
                dve.tensor_tensor(si[:, :, :], si[:, :, :], cv[:, :, :], ALU.mult)
                dve.wait_ge(root_made, 1)
                dve.drain()
                for m in range(KD):
                    dve.tensor_tensor(si[:, m, :], si[:, m, :], y[:, m, 0:SEQ], ALU.mult)
                    dve.drain()
                    dve.tensor_tensor_scan(cv[:, m, :], sr[:, m, :], si[:, m, :], 0.0, ALU.mult, ALU.add)
                    dve.drain()
                    dve.tensor_tensor(yg[:, m, :], yg[:, m, :], cv[:, m, :], ALU.mult).then_inc(out_f, 1)
                for m in range(KD):
                    dve.wait_ge(tile_done, j + 32 + m + 1)
                    dve.tensor_scalar(y[:, m, c:T], bank[4 + m % 2][:, 0:SEQ], vcol("b_out", m), None,
                                      ALU.add).then_inc(tile_read, 1)
                    split_lo(q + 6 + m // RING, m % RING, CH8)

            def keys_values():
                q, j, x, n, c = (KV[k] for k in "qjxnc")
                for t in range(16):
                    dve.wait_ge(tile_done, j + t + 1)
                    if t == 0:
                        norm_rstd(n, c)
                    if t >= 12:
                        dve.wait_ge(kv_turned, t - 11)
                    to = k2[:, t, :] if t < 8 else z[:, t % 4, c:T]
                    dve.tensor_tensor(to, bank[t % 4][:, 0:SEQ], rstd[:, c:T], ALU.mult).then_inc(tile_read, 1)
                    if t < 8:
                        x_lo(11, t, c)
                    split_lo(q + 1 + t // RING, t % RING, CH8)

            def attention():
                q, j, x, n, c = (ATT[k] for k in "qjxnc")
                for t in range(8):
                    dve.wait_ge(tile_done, j + t + 1)
                    if t == 0:
                        norm_rstd(n, c)
                    dve.scalar_tensor_tensor(q2[:, t, :], bank[t % 4][:, 0:SEQ], MOBA_SCALE, rstd[:, c:T],
                                             ALU.mult, ALU.mult).then_inc(tile_read, 1)
                    split_lo(q + 1 + t // RING, t % RING, CH8)

                def scores(hd):
                    p = hd % 2
                    dve.wait_ge(s2_done, hd + 1)
                    if hd >= 2:
                        dve.wait_ge(s2_turned, hd - 1)
                    dve.tensor_tensor(sc2[:, p, 0:P], bank[4 + p][:, 0:P], bias[:, hd, P:2 * P], ALU.add)
                    dve.tensor_tensor(sc2[:, p, P:3 * P], bank[4 + p][:, P:3 * P], bias[:, hd, 0:2 * P], ALU.add)
                    dve.drain()
                    dve.tensor_reduce(negmax[:, p, 0:1], sc2[:, p, 0:P], AX_X, ALU.max, negate=True)
                    dve.tensor_reduce(negmax[:, p, 1:2], sc2[:, p, P:3 * P], AX_X, ALU.max,
                                      negate=True).then_inc(s2_max, 1)

                dve.wait_ge(bias_in, 16)
                scores(0)
                for hd in range(HEADS):
                    if hd + 1 < HEADS:
                        scores(hd + 1)
                    p = hd % 2
                    dve.wait_ge(s2_exp, hd + 1)
                    dve.reciprocal(sums[:, p, 0:2], sums[:, p, 0:2])
                    dve.drain()
                    dve.tensor_scalar(sc2[:, p, 0:P], sc2[:, p, 0:P], sums[:, p, 0:1], None, ALU.mult)
                    dve.tensor_scalar(sc2[:, p, P:3 * P], sc2[:, p, P:3 * P], sums[:, p, 1:2], None,
                                      ALU.mult).then_inc(s2_normed, 1)
                    if hd >= 1:
                        out_lo(hd - 1, c)
                out_lo(7, c)
                for m in range(KD):
                    dve.wait_ge(tile_done, j + 8 + m + 1)
                    dve.tensor_copy(y[:, m, c:T], bank[4 + m % 2][:, 0:SEQ]).then_inc(tile_read, 1)
                    split_lo(q + 3 + m // RING, m % RING, CH8)

            def out_lo(hd, c):
                dve.wait_ge(o2_hi, hd + 1)
                dve.tensor_tensor(midlo[:, hd, c:T], bank[hd % 2][:, 0:SEQ], midhi[:, hd, c:T].bitcast(F32),
                                  ALU.subtract).then_inc(o2_lo, 1)

            dve.wait_ge(h_in, 16)
            dve.wait_ge(consts_in, 48)
            for k in range(KD):
                x_lo(0, k, 0)
            for k in range(RING):
                split_lo(0, k, CH8)
            dve.tensor_copy(masks[:, :, :].rearrange("p l t -> p (l t)"), gate_flat)
            r0, r1 = vec[:, VEC["lb_raw"]:VEC["lb_raw"] + 4], vec[:, VEC["lb_raw"] + 4:VEC["lb_raw"] + 8]
            dve.tensor_tensor(lb[:, 3, 0:4], r0, r1, ALU.max)
            dve.drain()
            dve.tensor_tensor(lb[:, 2, 0:4], r0, lb[:, 3, 0:4], ALU.subtract)
            dve.tensor_tensor(lb[:, 2, 4:8], r1, lb[:, 3, 0:4], ALU.subtract).then_inc(lb_asked, 1)
            dve.wait_ge(lb_exp, 1)
            dve.tensor_tensor(lb[:, 3, 0:4], lb[:, 2, 0:4], lb[:, 2, 4:8], ALU.add)
            dve.drain()
            dve.reciprocal(lb[:, 3, 0:4], lb[:, 3, 0:4])
            dve.drain()
            for s in range(2):
                dve.tensor_tensor(lb[:, 2, 4 * s:4 * s + 4], lb[:, 2, 4 * s:4 * s + 4], lb[:, 3, 0:4], ALU.mult)
            dve.drain()
            dve.tensor_tensor(lbs[:, 0:4], lb[:, 2, 0:4], lb[:, 2, 0:4], ALU.subtract)
            dve.tensor_tensor(lb[:, 3, 0:4], lb[:, 2, 0:4], lb[:, 2, 4:8], ALU.add)
            dve.drain()
            dve.tensor_tensor(lbs[:, 4:8], lb[:, 3, 0:4], lb[:, 2, 0:4], ALU.subtract)
            dve.drain()
            dve.tensor_scalar(one_lb[:, :], lbs[:, :], -1.0, 1.0, ALU.mult, ALU.add)
            raw_lam = vec[:, VEC["lam"]:VEC["lam"] + KD]
            neg_abs, u1, ln_u, coef = lam[:, 1, :], lam[:, 2, :], lam[:, 3, :], lam[:, 0, :]
            dve.tensor_scalar(coef, raw_lam, -1.0, None, ALU.mult)
            dve.drain()
            dve.tensor_tensor(neg_abs, coef, raw_lam, ALU.min).then_inc(lam_asked, 1)
            dve.wait_ge(lam_step, 1)
            dve.tensor_scalar(u1, neg_abs, 1.0, None, ALU.add).then_inc(lam_asked, 1)
            dve.tensor_scalar(coef, coef, 0.0, None, ALU.max)
            dve.wait_ge(lam_step, 2)
            small_e = negmax[:, :, :].rearrange("p a b -> p (a b)")
            tmp, same = lb[:, 2, :], lb[:, 3, :]
            dve.drain()
            dve.tensor_scalar(tmp, u1, 1.0, TINY, ALU.subtract, ALU.max)
            dve.tensor_scalar(same, u1, 1.0, None, ALU.is_equal)
            dve.drain()
            dve.reciprocal(tmp, tmp)
            dve.tensor_tensor(same, same, neg_abs, ALU.mult)
            dve.tensor_tensor(ln_u, ln_u, neg_abs, ALU.mult)
            dve.drain()
            dve.tensor_tensor(ln_u, ln_u, tmp, ALU.mult)
            dve.tensor_tensor(coef, coef, same, ALU.add)
            dve.drain()
            dve.tensor_tensor(coef, coef, ln_u, ALU.add)
            dve.drain()
            dve.tensor_scalar(coef, coef, -LRU_C, None, ALU.mult).then_inc(coef_made, 1)
            with dve.Fori(0, DEPTH) as l:
                ffn(**layer_stage(l, 0))
                ffn_down(**layer_stage(l, 0))
                mixer(l)
                ffn(**layer_stage(l, 2))
                ffn_down(**layer_stage(l, 2))
            c = N_META
            norm_rstd(10, 0)
            for k in range(KD):
                dve.scalar_tensor_tensor(h[:, k, c:T], h[:, k, c:T], norm_gain(6, k), rstd[:, c:T],
                                         ALU.mult, ALU.mult).then_inc(h_made, 1)
            inputs = lambda x, to=xlo, hi=xhi: [x_lo(x, k, c, to, hi) for k in range(KD)]
            inputs(7)
            ffn(**F4)
            ffn_down(**F4)
            update(12, lambda k: ("ffn_post", k), 0.5)
            inputs(8)
            recurrent()
            update(14, lambda k: ("mix_post", k), 1.0)
            inputs(9)
            ffn(**F5)
            ffn_down(**F5)
            update(16, lambda k: ("ffn_post", 8 + k), 0.5)
            inputs(10, midlo, midhi)
            keys_values()
            ffn(**F6, main_norm=False)
            ffn_down(**F6)
            update(18, lambda k: ("ffn_post", 16 + k), 0.5)
            inputs(12)
            attention()
            update(20, lambda k: ("mix_post", 8 + k), 1.0)
            inputs(13)
            ffn(**F7)
            ffn_down(**F7, tail=False)
            update(22, lambda k: ("ffn_post", 24 + k), 0.5)

        @block.gpsimd
        def _(pool):
            def squares_of(src, c, last_sum, ready):
                pool.wait_ge(sum_made, last_sum)
                for k in range(KD):
                    ready(k)
                    pool.tensor_tensor((sqt[:, k % 2, c:T] if k else acc[:, c:T]), src[:, k, c:T], src[:, k, c:T], ALU.mult)
                    pool.drain()
                    if k:
                        op = pool.tensor_tensor(acc[:, c:T], acc[:, c:T], sqt[:, k % 2, c:T], ALU.add)
                op.then_inc(sq_made, 1)

            def of_update(u, last_sum):
                squares_of(h, N_META, last_sum, lambda k: pool.wait_ge(h_made, 8 * (u - 7) + k + 1))

            def of_branch(j, last_sum):
                squares_of(y, N_META, last_sum, lambda k: pool.wait_ge(tile_read, j + k + 1))

            def ffn(q, j, x, n, f, c, main_norm=True):
                with pool.Fori(0, KF // 2) as b:
                    for p in range(2):
                        i = b * 2 + p
                        pool.wait_ge(silu_made, f * KF + i + 1)
                        pool.wait_ge(tile_read, b * RING + j + 2 * p + 2)
                        pool.tensor_tensor(z[:, 2 + p, c:T], sil[:, p, c:T], z[:, 2 + p, c:T],
                                           ALU.mult).then_inc(hid_made, 1)
                        pool.wait_ge(hid_hi_made, f * KF + i + 1)
                        at_i = bass.ds(i, 1)
                        pool.tensor_tensor(hidlo[:, at_i, c:T], z[:, 2 + p:3 + p, c:T],
                                           hidhi[:, at_i, c:T].bitcast(F32), ALU.subtract).then_inc(hid_lo_made, 1)

            def mixer(l):
                st = layer_stage(l, 1)
                j, n = st["j"], st["n"]
                for step, i in MIXER:
                    if step == "tile" and CQ <= i < KPE:
                        which, first = (0, i == CQ) if i < CKV else (1, i == CKV)
                        pool.wait_ge(tile_read, j + i + 1)
                        dst = sil[:, which, :] if first else sqt[:, i % 2, :]
                        pool.tensor_tensor(dst, z[:, i % 4, :], z[:, i % 4, :], ALU.mult).then_inc(lat_z, 1)
                        pool.drain()
                        if not first:
                            op = pool.tensor_tensor(sil[:, which, :], sil[:, which, :], sqt[:, i % 2, :], ALU.add)
                            if i in (CKV - 1, KPE - 1):
                                op.then_inc(lat_sq, 1)
                    elif step == "level" and i >= 1:
                        pool.wait_ge(exp_made, l * (LEVELS - 1) + i)
                        pool.tensor_tensor(kd[:, :, :], kd[:, :, :], hk[:, :, :], ALU.mult).then_inc(kd_ready, 1)
                    elif step == "rec_norm":
                        pool.wait_ge(rec_hi, l * 4 + i + 1)
                        pool.tensor_tensor(reclo[:, i, :], pre[:, i, :], rechi[:, i, :].bitcast(F32),
                                           ALU.subtract).then_inc(rec_lo, 1)
                    elif step == "tile" and PR <= i < OUT:
                        m = i - PR
                        pool.wait_ge(tile_read, j + i + 1)
                        pool.tensor_tensor(sga[:, m, :], sga[:, m, :], z[:, i % 4, :], ALU.add).then_inc(merged, 1)
                        pool.wait_ge(mid_hi_made, l * 8 + m + 1)
                        pool.tensor_tensor(midlo[:, m, :], sga[:, m, :], midhi[:, m, :].bitcast(F32),
                                           ALU.subtract).then_inc(mid_lo_made, 1)
                squares_of(h, 0, n + 1, lambda k: pool.wait_ge(tile_read, j + OUT + k + 1))

            def of_layer(st):
                squares_of(h, 0, st["n"] + 1, lambda k: pool.wait_ge(tile_read, st["j"] + 2 * KF + k + 1))

            pool.wait_ge(h_in, 16)
            for k in range(KD):
                pool.tensor_tensor((sqt[:, k % 2, :] if k else acc[:, :]), h[:, k, :], h[:, k, :], ALU.mult)
                pool.drain()
                if k:
                    op = pool.tensor_tensor(acc[:, :], acc[:, :], sqt[:, k % 2, :], ALU.add)
            op.then_inc(sq_made, 1)
            with pool.Fori(0, DEPTH) as l:
                ffn(**layer_stage(l, 0))
                of_layer(layer_stage(l, 0))
                mixer(l)
                ffn(**layer_stage(l, 2))
                of_layer(layer_stage(l, 2))
            of_update(7, 11)
            ffn(**F4)
            of_branch(F4["j"] + 2 * KF, 12)
            of_update(8, 13)
            for m in range(KD):
                pool.wait_ge(cv_hi_made, m + 1)
                pool.tensor_tensor(cvlo[:, m, :], cv[:, m, :], cvhi[:, m, :].bitcast(F32),
                                   ALU.subtract).then_inc(cv_lo_made, 1)
            for m in range(KD):
                pool.wait_ge(out_hi_made, m + 1)
                pool.tensor_tensor(outlo[:, m, :], yg[:, m, :], outhi[:, m, :].bitcast(F32),
                                   ALU.subtract).then_inc(out_lo_made, 1)
            of_branch(REC["j"] + 32, 14)
            of_update(9, 15)
            ffn(**F5)
            of_branch(F5["j"] + 2 * KF, 16)
            of_update(10, 17)
            ffn(**F6)
            of_branch(F6["j"] + 2 * KF, 18)
            of_update(11, 19)
            of_branch(ATT["j"] + 8, 20)
            of_update(12, 21)
            ffn(**F7)
            of_branch(F7["j"] + 2 * KF, 22)


def pad_to(a, width):
    return np.concatenate([a, np.zeros((a.shape[0], width - a.shape[1]), a.dtype)], 1)


def feature_columns(v):
    return v.reshape(-1, P).T


def mixer_weights(w_in, w_uq, w_ukv, w_pa, w_pr, w_out):
    sizes = (Q_LORA, KV_LORA, ROPE, 512, 512, 512, 512, D_MODEL, D_MODEL)
    cq, ckv, kpe, hq, hf, hi, hg, ga, gb = np.split(w_in, np.cumsum(sizes)[:-1], 1)
    swap = np.r_[ROPE // 2:ROPE, 0:ROPE // 2]
    first = np.concatenate([hf, hi, hq, hg, ga, gb, cq, ckv, np.tile(kpe, (1, 4)), np.tile(kpe[:, swap], (1, 4))], 1)
    q = w_uq.reshape(Q_LORA, HEADS, NOPE + ROPE)
    nope, rope = q[:, :, :NOPE], q[:, :, NOPE:]
    uq = np.concatenate([t.reshape(Q_LORA, -1) for t in (nope, rope, rope[:, :, swap])], 1)
    kv = w_ukv.reshape(KV_LORA, HEADS, NOPE + V_HEAD)
    ukv = np.concatenate([kv[:, :, :NOPE].reshape(KV_LORA, -1), kv[:, :, NOPE:].reshape(KV_LORA, -1)], 1)
    return np.concatenate([k8(first), k_few(uq), k_few(ukv), k_few(w_pa), k_few(w_pr), k8(w_out)])


def pairs(gate, up):
    d = gate.shape[0]
    return np.stack([gate.reshape(d, KF, P), up.reshape(d, KF, P)], 2).reshape(d, -1)


def lay_out(i):
    gu, down = [], []
    for l in range(DEPTH):
        for n in ("ffn1", "ffn2"):
            w = i[n + "_w_gu"][l]
            gu.append(k8(pairs(w[:, :D_FF], w[:, D_FF:])))
            down.append(down_chunks(i[n + "_w_down"][l]))
    for l in range(DEPTH):
        for n in ("ffn1", "ffn2"):
            gu.append(k8(pairs(i[n + "_w_gate_2"][l], i[n + "_w_up_2"][l])))
            down.append(down_chunks(i[n + "_w_down_2"][l]))
    x = np.concatenate([i["meta_tokens"], i["x"][0]], 0)
    norms = [i[n][l] for l in range(DEPTH) for n in ("ffn1_norm", "mix_norm", "ffn2_norm")] + [i["final_norm"]]
    small = [v for l in range(DEPTH) for v in (i["q_norm"][l], i["kv_norm"][l], i["hg_norm"][l])]
    by_ffn = lambda n: [i[f"{f}_{n}_2"][l] for l in range(DEPTH) for f in ("ffn1", "ffn2")]
    vectors = norms + small + [i["hg_lb_raw"]] + by_ffn("pre_g") + by_ffn("post_g") + [
        i["mix_pre_g_2"], i["mix_post_g_2"], i["kv_norm_g_2"], i["lru_b_in_2"][0], i["lru_conv_w_2"][0],
        i["lru_conv_b_2"][0], i["lru_b_r_2"][0], i["lru_b_i_2"][0], i["lru_lambda_2"][0], i["lru_b_out_2"][0]]
    consts, masks, bucket_rows = constants()
    heads = [k_few(np.concatenate([i["lru_w_r_2"][0, n], i["lru_w_i_2"][0, n]], 1)) for n in range(4)]
    return {
        "h0": np.ascontiguousarray(x.T.reshape(KD, P, T).transpose(1, 0, 2)),
        "vectors": np.ascontiguousarray(np.concatenate([feature_columns(v) for v in vectors], 1)),
        "consts": consts,
        "masks": masks,
        "bucket_rows": bucket_rows,
        "rel_rows": np.concatenate([i["rel_bias_2"].T, np.full((1, HEADS), NEG_BIG, np.float32)], 0),
        "ffn_gu": np.concatenate(gu),
        "ffn_down": np.concatenate(down),
        "mix": np.concatenate([mixer_weights(i["w_in"][l], i["w_uq"][l], i["w_ukv"][l], i["w_proj_attn"][l],
                                             i["w_proj_rec"][l], i["w_out"][l]) for l in range(DEPTH)]),
        "rec": np.concatenate([k8(i["lru_w_in_2"][0])] + heads + [k8(i["lru_w_out_2"][0])]),
        "kv": k8(i["w_kv_2"]),
        "att": np.concatenate([k8(i["attn_w_q_2"][0]), k8(i["attn_w_o_2"][0])]),
    }


def kernel(**inputs):
    import concourse.bacc as bacc
    from concourse.bass_utils import run_bass_kernel_spmd

    arrays = lay_out({n: np.asarray(v) for n, v in inputs.items()})
    nc = bacc.Bacc("TRN2", target_bir_lowering=False, num_devices=1)
    aps = {n: nc.dram_tensor(n, v.shape, mybir.dt.from_np(v.dtype), kind="ExternalInput").ap()
           for n, v in arrays.items()}
    aps["out"] = nc.dram_tensor("out", (P, KD, SEQ), F32, kind="ExternalOutput").ap()
    program(nc, aps)
    got = run_bass_kernel_spmd(nc, [arrays], core_ids=[0]).results[0]["out"]
    return np.ascontiguousarray(got.transpose(2, 1, 0)).reshape(1, SEQ, D_MODEL)
```

```python
from contextlib import ExitStack

import numpy as np
import concourse.bass as bass
from concourse import mybir

P = 128
D_MODEL, SEQ, N_META, D_FF, DEPTH = 1024, 256, 16, 2816, 2
T = SEQ + N_META
KD = D_MODEL // P
KF = D_FF // P
HEADS, NOPE, ROPE, V_HEAD = 8, 64, 32, 64
Q_LORA, KV_LORA = 384, 256
QK_SCALE = float((NOPE + ROPE) ** -0.5)
HG_HEADS, HG_DIM = 4, 128
HG_SCALE = float(HG_DIM ** -0.5)
HEAD_DIM = 128
MOBA_SCALE = float(HEAD_DIM ** -0.5)
N_BUCKETS, MAX_DISTANCE = 32, 128
EPS = 1e-6
F_MIN = 1e-20
NEG_BIG = -1e30
LRU_C = 8.0
LN_SPLIT = 2.0 ** -32
LN_SHIFT = float(32 * np.log(2.0))
TINY = 1e-30

F32, F32R, U8 = mybir.dt.float32, mybir.dt.float32r, mybir.dt.uint8
ACT = mybir.ActivationFunctionType
ALU = mybir.AluOpType
AX_X = mybir.AxisListType.X

RING = 4
CH8, CH11 = 8 * P, 11 * P
FFN_PAIRS = KF
FFN_GU_QUADS, FFN_DOWN_QUADS = 2 * KF // RING, 2 * KD // RING
FFN_QUADS = FFN_GU_QUADS + FFN_DOWN_QUADS
FFN_TILES = 2 * KF + KD

HF, HQ, HI, HGATE, GA, CQ, CKV, KPE, KPS = 0, 4, 8, 12, 16, 24, 27, 29, 30
GB1, UQ, UKV, GB2, PR, PA, OUT = 31, 35, 43, 51, 55, 63, 71
MIX_TILES, MIX_QUADS = 79, 15
TAKEN = [*range(HF, HI), *range(HGATE, KPE), *range(GB1, UQ), *range(GB2, PR)]
LAYER_QUADS = 2 * FFN_QUADS + MIX_QUADS
LAYER_TILES = 2 * FFN_TILES + MIX_TILES

LEVELS = 10
MASKED_LEVELS = 8
HALF = [0] + [2 ** i for i in range(LEVELS - 1)]

TAIL = T - 32
TOKEN_TILES = ((0, P), (P, P), (2 * P, T - 2 * P))

VEC = {}
_at = 0
for _name, _n in (("norms", 56), ("small", 12), ("lb_raw", 8), ("ffn_pre", 32), ("ffn_post", 32),
                  ("mix_pre", 16), ("mix_post", 16), ("kv", 8), ("b_in", 16), ("conv_w", 32),
                  ("conv_b", 8), ("b_r", 8), ("b_i", 8), ("lam", 8), ("b_out", 8)):
    VEC[_name] = _at
    _at += _n
N_VEC = _at

CONST = {}
_at = 0
for _name, _n in (("ones", P), ("ident", P), ("cos", T), ("sin", T), ("causal", 3 * P),
                  ("causal_tail", T), ("eps", 1)):
    CONST[_name] = _at
    _at += _n
N_CONST = _at


def k8(w):
    k, m = w.shape[0] // P, w.shape[1] // P
    return np.ascontiguousarray(w.reshape(k, P, m, P).transpose(2, 1, 0, 3)).reshape(m, P, k * P)


def k_few(w):
    k, m = w.shape[0] // P, w.shape[1] // P
    tiles = w.reshape(k, P, m, P).transpose(2, 0, 1, 3).reshape(k * m // 8, 8, P, P)
    return np.ascontiguousarray(tiles.transpose(0, 2, 1, 3)).reshape(-1, P, CH8)


def down_chunks(w):
    tiles = w.reshape(2, 11, P, KD, P).transpose(3, 0, 2, 1, 4)
    return np.ascontiguousarray(tiles).reshape(2 * KD, P, CH11)


def constants():
    c = np.zeros((P, N_CONST), np.float32)

    def put(name, a):
        c[:a.shape[0], CONST[name]:CONST[name] + a.shape[1]] = a

    put("ones", np.ones((P, P)))
    put("ident", np.eye(P))
    half = ROPE // 2
    inv = np.float32(10000.0) ** (-np.arange(half, dtype=np.float32) / np.float32(half))
    ang = (inv.astype(np.float32)[:, None] * np.arange(T, dtype=np.float32)[None, :]).astype(np.float32)
    put("cos", np.tile(np.cos(ang), (2 * P // ROPE, 1)))
    put("sin", np.tile(np.concatenate([-np.sin(ang), np.sin(ang)]), (P // ROPE, 1)))
    triangle = np.where(np.arange(P)[None, :] <= np.arange(P)[:, None], 0.0, NEG_BIG)
    put("causal", np.concatenate([triangle, np.zeros((P, P)), triangle], 1))
    put("causal_tail", np.where(np.arange(T)[None, :] <= TAIL + np.arange(P)[:, None] % 32, 0.0, NEG_BIG))
    put("eps", np.full((P, 1), EPS))
    dist = 255 - np.arange(512)
    n = np.maximum(dist, 0)
    exact = N_BUCKETS // 2
    nf = np.maximum(n, 1).astype(np.float32)
    large = exact + (np.log(nf / np.float32(exact)).astype(np.float32)
                     / np.float32(np.log(MAX_DISTANCE / exact)) * np.float32(N_BUCKETS - exact)).astype(np.int32)
    bucket = np.where(n < exact, n, np.minimum(large, N_BUCKETS - 1))
    row = np.where(dist >= 0, bucket, N_BUCKETS)
    bucket_rows = (row[None, :] == np.arange(N_BUCKETS + 1)[:, None]).astype(np.float32)
    s, t = np.arange(P)[:, None], np.arange(P)[None, :]
    masks = [s == t]
    for m in HALF[1:MASKED_LEVELS]:
        masks.append((s // (2 * m) == t // (2 * m)) & (s % (2 * m) < m) & (t % (2 * m) >= m))
    return c, np.stack(masks, 1).astype(np.float32).reshape(P, MASKED_LEVELS * P), bucket_rows


def mixer_order():
    steps = [("tile", t) for t in range(HQ)]
    for hd in range(HG_HEADS):
        steps += [("tile", HQ + hd), ("decay", hd)]
    steps += [("tile", HI), ("tile", HI + 1), ("log_decay", 0), ("tile", HI + 2), ("tile", HI + 3),
              ("tile", HGATE), ("turn_v", 0)]
    for level in range(LEVELS + 1):
        if level < LEVELS:
            steps.append(("level", level))
        if level >= 1:
            steps.append(("pairs", level - 1))
        if level + 1 < LEVELS:
            steps.append(("exps", level + 1))
        if level >= 1:
            steps += [("take", level - 1), ("tile", HGATE + 2 * level)]
        if level < LEVELS:
            steps.append(("tile", HGATE + 2 * level + 1))
    steps += [("rec_out", 0), ("rec_out", 1), ("tile", GB1 + 2), ("rec_out", 2), ("rec_out", 3), ("tile", GB1 + 3)]
    steps += [("latent_norm", 0), ("rec_norm", 0), ("latent_norm", 1)]
    for i in range(1, 4):
        steps += [("tile", UQ + 2 * i - 2), ("tile", UQ + 2 * i - 1), ("rec_norm", i)]
    steps += [("tile", t) for t in range(UQ + 6, GB2)] + [("turn_v2", 0), ("scores", 0), ("tail_scores", 0), ("tail", 0)]
    for h in range(HEADS):
        steps.append(("norm", h))
        if h + 1 < HEADS:
            steps.append(("scores", h + 1))
        if h == 2:
            steps.append(("tail_scores", 1))
        steps.append(("turn", h))
        steps += [("tile", GB2 + h)] if h < 4 else [("tile", PR + 2 * (h - 4)), ("tile", PR + 2 * (h - 4) + 1)]
        if h == 3:
            steps.append(("tail", 1))
        steps.append(("attend", h))
    return steps + [("tile", t) for t in range(PA, MIX_TILES)]


MIXER = mixer_order()
SCORE_ROWS = ((0, P), (P, 3 * P))


def mixer_parts(t):
    for first, k, n, chunk in ((UQ, 3, 8, 35), (UKV, 2, 8, 38), (GB2, 8, 4, 40), (PR, 4, 8, 44), (PA, 4, 8, 48),
                               (OUT, 8, 8, 52)):
        if first <= t < first + n:
            return [(chunk + ((t - first) * k + i) // 8, ((t - first) * k + i) % 8) for i in range(k)]
    return [(t, i) for i in range(8)]


def chunks_ended(t):
    return [c for c, i in mixer_parts(t) if i == 7]


def taken(t):
    return TAKEN.index(t) + 1


def mixer_bank(t):
    return 4 + t % 2 if t >= OUT else t % 2 if GB2 <= t < PA else t % 4


def z_place(t):
    return t - UKV - 4 if UKV + 4 <= t < GB2 else t % 4


def z_before():
    last, before = {}, {}
    for t in [*range(HF, HI), *range(HGATE, UQ), UQ + 6, UQ + 7, *range(UKV + 4, PR)]:
        before[t] = last.get(z_place(t))
        last[z_place(t)] = t
    return before


Z_BEFORE = z_before()


def program(nc, a):
    with ExitStack() as ctx:
        arena = ctx.enter_context(nc.sbuf_tensor("arena", [P, 52176], F32))
        base, end = nc.sbuf_base - 52176 * 4, nc.sbuf_base
        top = [base]

        def at(name, shape, dt, where=None):
            place = top if where is None else where
            size = int(np.prod(shape[1:])) * (1 if dt == U8 else 4)
            h = nc.alloc_sbuf_tensor_at(name, shape, dt, offset=place[0])
            place[0] += (size + 31) // 32 * 32
            assert place[0] <= end, (name, place[0] - end)
            return h

        raw = at("raw", [P, RING, CH11], F32)
        whi = at("whi", [P, RING, CH11], F32R)
        wlo = at("wlo", [P, RING, CH11], F32R)
        h = at("h", [P, KD, T], F32)
        xhi = at("xhi", [P, KD, T], F32R)
        xlo = at("xlo", [P, KD, T], F32R)
        consts = at("consts", [P, N_CONST], F32)
        masks = at("masks", [P, MASKED_LEVELS, P], U8)
        vec = at("vec", [P, N_VEC], F32)
        z = at("z", [P, 4, T], F32)
        sil = at("sil", [P, 2, T], F32)
        sqt = at("sqt", [P, 2, T], F32)
        acc = at("acc", [P, T], F32)
        std = at("std", [P, T], F32)
        rstd = at("rstd", [P, T], F32)
        rlat = at("rlat", [P, 2, T], F32)
        lb = at("lb", [P, 4, DEPTH * HG_HEADS], F32)
        lbs = lb[:, 0, :]
        one_lb = lb[:, 1, :]
        negmax = at("negmax", [P, 2, 3], F32)
        sums = at("sums", [P, 2, 3], F32)
        lam = at("lam", [P, 4, KD], F32)
        idle, warm = at("idle", [P, 1], F32), at("warm", [P, 1], F32)
        hbase = top[0]
        hidhi = at("hidhi", [P, KF, T], F32R)
        hidlo = at("hidlo", [P, KF, T], F32R)
        ebase = top[0]

        H, E = [hbase], [ebase]
        midbase = H[0]
        midhi, midlo = at("midhi", [P, KD, T], F32R, H), at("midlo", [P, KD, T], F32R, H)
        rechi, reclo = at("rechi", [P, 4, T], F32R, H), at("reclo", [P, 4, T], F32R, H)
        att_at = H[0]
        atthi, attlo = at("atthi", [P, 4, T], F32R, H), at("attlo", [P, 4, T], F32R, H)
        lat_at = H[0]
        lathi, latlo = at("lathi", [P, 5, T], F32R, H), at("latlo", [P, 5, T], F32R, H)
        krot = at("krot", [P, T], F32, H)
        M = [midbase]
        gate = at("gate", [P, 4, T], F32, M)
        gate_flat = gate[:, :, :].rearrange("p h t -> p (h t)")[:, 0:MASKED_LEVELS * P]
        vtok = at("vtok", [P, 3, 512], F32, M)
        dec0 = at("dec0", [P, 4, T], F32, M)
        dec1 = at("dec1", [P, 4, 144], F32, M)
        dec2 = at("dec2", [P, 4, 16], F32, M)
        assert M[0] <= midbase + 2 * KD * T * 4
        sga, sgb = at("sga", [P, KD, T], F32, E), at("sgb", [P, KD, T], F32, E)
        recbase = E[0]
        pre, suf = at("pre", [P, 4, T], F32, E), at("suf", [P, 4, T], F32, E)
        hq, hk = at("hq", [P, 4, T], F32, E), at("hk", [P, 4, T], F32, E)
        qd0, kd0 = at("qd0", [P, 4, T], F32, E), at("kd0", [P, 4, T], F32, E)
        L = [att_at]
        qd1, kd1 = at("qd1", [P, 4, T], F32, L), at("kd1", [P, 4, T], F32, L)
        qds, kds = (qd0, qd1), (kd0, kd1)
        A = [recbase + 2 * 4 * T * 4]
        qn, kn = at("qn", [P, 4, T], F32, A), at("kn", [P, 4, T], F32, A)
        qr = at("qr", [P, 2, T], F32, A)
        sc = at("sc", [P, 2, 3 * P], F32, A)
        pt = at("pt", [P, 2, 3 * P], F32, A)
        vtok2 = at("vtok2", [P, 3, 512], F32, [recbase])
        ptail = at("ptail", [P, 2, 3 * P], F32, [lat_at])
        sct = sil
        assert A[0] <= end

        E = [ebase]
        y = at("y", [P, KD, T], F32, E)
        kvbase = E[0]
        k2 = at("k2", [P, KD, SEQ], F32, E)
        vt2 = at("vt2", [P, 2, KD * P], F32, E)
        bias = at("bias", [P, HEADS, 3 * P], F32, E)
        brow = at("brow", [P, 512], F32, E)
        R = [kvbase]
        sr, si = at("sr", [P, KD, SEQ], F32, R), at("si", [P, KD, SEQ], F32, R)
        yg = at("yg", [P, KD, SEQ], F32, R)
        xb = at("xb", [P, 2, SEQ + 3], F32, R)
        H = [hbase]
        cv = at("cv", [P, KD, SEQ], F32, H)
        cvhi, cvlo = at("cvhi", [P, KD, SEQ], F32R, H), at("cvlo", [P, KD, SEQ], F32R, H)
        outhi, outlo = at("outhi", [P, KD, SEQ], F32R, H), at("outlo", [P, KD, SEQ], F32R, H)
        H = [hbase + 2 * KD * T * 4]
        q2 = at("q2", [P, KD, SEQ], F32, H)
        sc2 = at("sc2", [P, 2, 3 * P], F32, H)
        pt2 = at("pt2", [P, 2, 3 * P], F32, H)
        onehot = at("onehot", [P, 512], F32, H)
        relt = at("relt", [P, HEADS], F32, H)
        assert H[0] <= ebase

        bank = [ctx.enter_context(nc.psum_tensor(f"bank{i}", [P, 512], F32)) for i in range(8)]
        NORM = 7
        PAIR_BANKS = (bank[2], bank[7])

        def const(name, n):
            return consts[:, CONST[name]:CONST[name] + n]

        ones, ident, eps = const("ones", P), const("ident", P), const("eps", 1)

        def vcol(name, i):
            return vec[:, VEC[name] + i:VEC[name] + i + 1]

        def norm_gain(x, k):
            if isinstance(x, int):
                return vcol("norms", 8 * x + k)
            return vec[:, bass.ds(x * 8 + VEC["norms"] + k, 1)]

        scratch = nc.dram_tensor("bias_rows", [HEADS, P, 513], F32, kind="Internal").ap()

        def sem(name):
            return ctx.enter_context(nc.semaphore(name))

        landed = [sem(f"landed{i}") for i in range(RING)]
        hi_made, lo_made = sem("hi_made"), sem("lo_made")
        tile_done, tile_read = sem("tile_done"), sem("tile_read")
        vec_in, consts_in, masks_in, h_in = sem("vec_in"), sem("consts_in"), sem("masks_in"), (sem("h_in0"), sem("h_in1"))
        h_made, x_hi_made, x_lo_made = sem("h_made"), sem("x_hi_made"), sem("x_lo_made")
        sq_made, sum_made, std_made, rstd_made = sem("sq_made"), sem("sum_made"), sem("std_made"), sem("rstd_made")
        silu_made = sem("silu_made")
        hid_made, hid_hi_made, hid_lo_made = sem("hid_made"), sem("hid_hi_made"), sem("hid_lo_made")
        act_took = sem("act_took")
        lb_asked, lb_exp, lam_asked = sem("lb_asked"), sem("lb_exp"), sem("lam_asked")
        decay_made, log_made, cleared = sem("decay_made"), sem("log_made"), sem("cleared")
        v_turned, v_taken = sem("v_turned"), sem("v_taken")
        sums_ready, exp_made, level_ready, level_done = sem("sums_ready"), sem("exp_made"), sem("level_ready"), sem("level_done")
        rec_done, rec_taken, rec_sq, rec_sum, rec_std, rec_f, rec_hi, rec_lo = (
            sem(n) for n in ("rec_done", "rec_taken", "rec_sq", "rec_sum", "rec_std", "rec_f", "rec_hi", "rec_lo"))
        kd_ready, level_taken = sem("kd_ready"), sem("level_taken")
        lat_sq, lat_lo, lat_z = sem("lat_sq"), sem("lat_lo"), sem("lat_z")
        krot_made, qrot_made = sem("krot_made"), sem("qrot_made")
        v2_turned, v2_taken = sem("v2_turned"), sem("v2_taken")
        scores_done, max_made, probs_made, probs_normed, probs_turned, probs_taken = (
            sem(n) for n in ("scores_done", "max_made", "probs_made", "probs_normed", "probs_turned", "probs_taken"))
        tail_done, tail_max, tail_exp, tail_normed, tail_turned, tail_taken = (
            sem(n) for n in ("tail_done", "tail_max", "tail_exp", "tail_normed", "tail_turned", "tail_taken"))
        att_done, att_hi, att_lo = sem("att_done"), sem("att_hi"), sem("att_lo")
        merged, mid_hi_made, mid_lo_made = sem("merged"), sem("mid_hi_made"), sem("mid_lo_made")
        xb_made, conv_begun, conv_made, cv_hi_made, cv_lo_made = (
            sem(n) for n in ("xb_made", "conv_begun", "conv_made", "cv_hi_made", "cv_lo_made"))
        b_act_took, lam_step, coef_made, decay2_made, root_made, root_asked = (
            sem(n) for n in ("b_act_took", "lam_step", "coef_made", "decay2_made", "root_made", "root_asked"))
        gated_made, scan_made = sem("gated_made"), sem("scan_made")
        out_f, out_hi_made, out_lo_made = sem("out_f"), sem("out_hi_made"), sem("out_lo_made")
        kv_turned, kv_taken = sem("kv_turned"), sem("kv_taken")
        rel_in, brow_done, brow_made, brow_out, bias_in = (
            sem(n) for n in ("rel_in", "brow_done", "brow_made", "brow_out", "bias_in"))
        s2_done, s2_max, s2_exp, s2_normed, s2_turned, s2_taken, o2_done, o2_hi, o2_lo = (
            sem(n) for n in ("s2_done", "s2_max", "s2_exp", "s2_normed", "s2_turned", "s2_taken", "o2_done", "o2_hi", "o2_lo"))
        stored = sem("stored")

        block = ctx.enter_context(nc.Block())

        def early_bank(t):
            return (0, 1, 2, 3, 4, 5, 6, 3)[t] if t < 8 else t % RING

        def layer_stage(l, which):
            q, j, n = ((0, 0, 0), (FFN_QUADS, FFN_TILES, 1), (FFN_QUADS + MIX_QUADS, FFN_TILES + MIX_TILES, 4))[which]
            return dict(q=l * LAYER_QUADS + q, j=l * LAYER_TILES + j, x=l * 3 + which, n=l * 5 + n,
                        f=l * 2 + which // 2, c=0)

        Q2, J2 = DEPTH * LAYER_QUADS, DEPTH * LAYER_TILES
        REC_QUADS, REC_TILES, KV_QUADS, KV_TILES, ATT_QUADS, ATT_TILES = 7, 40, 4, 16, 4, 16
        F4 = dict(q=Q2, j=J2, x=7, n=11, f=4, c=N_META)
        REC = dict(q=Q2 + FFN_QUADS, j=J2 + FFN_TILES, x=8, n=13, c=N_META)
        F5 = dict(q=REC["q"] + REC_QUADS, j=REC["j"] + REC_TILES, x=9, n=15, f=5, c=N_META)
        KV = dict(q=F5["q"] + FFN_QUADS, j=F5["j"] + FFN_TILES, x=10, n=17, c=N_META)
        F6 = dict(q=KV["q"] + KV_QUADS, j=KV["j"] + KV_TILES, x=11, n=18, f=6, c=N_META)
        ATT = dict(q=F6["q"] + FFN_QUADS, j=F6["j"] + FFN_TILES, x=12, n=19, c=N_META)
        F7 = dict(q=ATT["q"] + ATT_QUADS, j=ATT["j"] + ATT_TILES, x=13, n=21, f=7, c=N_META)
        GAIN2 = {7: ("ffn_pre", 0), 8: ("mix_pre", 0), 9: ("ffn_pre", 8), 10: ("kv", 0), 11: ("ffn_pre", 16),
                 12: ("mix_pre", 8), 13: ("ffn_pre", 24)}

        def squares(x, n):
            return n - 3 if isinstance(n, int) and n >= 10 else x + 1

        SQUARES = {n: squares(0, n) for n in range(10, 23)}

        def gain(x, k):
            if not isinstance(x, int) or x < 7:
                return norm_gain(x, k)
            name, first = GAIN2[x]
            return vcol(name, first + k)

        @block.sync
        def _(sp):
            def load(src, q, k, cols):
                if not isinstance(q, int) or q >= 1:
                    sp.wait_ge(lo_made, (q - 1) * RING + k + 1)
                sp.dma_start(raw[:, k, 0:cols], src).then_inc(landed[k], 16)

            def stream(array, first, q, quads, cols):
                with sp.Fori(0, quads) as b:
                    for k in range(RING):
                        load(array[b * RING + first + k], b + q, k, cols)

            def ffn_weights(q, f):
                stream(a["ffn_gu"], f * 2 * KF, q, FFN_GU_QUADS, CH8)
                stream(a["ffn_down"], f * 2 * KD, q + FFN_GU_QUADS, FFN_DOWN_QUADS, CH11)

            sp.dma_start(vec[:, :], a["vectors"]).then_inc(vec_in, 16)
            for s in range(2):
                sp.dma_start(h[:, 4 * s:4 * s + 4, :], a["h0"][:, 4 * s:4 * s + 4, :]).then_inc(h_in[s], 16)
            for k in range(2):
                load(a["ffn_gu"][k], 0, k, CH8)
            sp.dma_start(consts[:, :], a["consts"]).then_inc(consts_in, 16)
            for k in range(2, RING):
                load(a["ffn_gu"][k], 0, k, CH8)
            sp.dma_start(gate_flat, a["masks"]).then_inc(masks_in, 16)
            stream(a["ffn_gu"], RING, 1, FFN_GU_QUADS - 1, CH8)
            stream(a["ffn_down"], 0, FFN_GU_QUADS, FFN_DOWN_QUADS, CH11)
            stream(a["mix"], 0, FFN_QUADS, MIX_QUADS, CH8)
            ffn_weights(FFN_QUADS + MIX_QUADS, 1)
            with sp.Fori(1, DEPTH) as l:
                ffn_weights(l * LAYER_QUADS, l * 2)
                stream(a["mix"], l * MIX_QUADS * RING, l * LAYER_QUADS + FFN_QUADS, MIX_QUADS, CH8)
                ffn_weights(l * LAYER_QUADS + FFN_QUADS + MIX_QUADS, l * 2 + 1)
            ffn_weights(F4["q"], 4)
            stream(a["rec"], 0, REC["q"], REC_QUADS, CH8)
            ffn_weights(F5["q"], 5)
            stream(a["kv"], 0, KV["q"], 1, CH8)
            sp.wait_ge(tile_done, KV["j"])
            sp.dma_start(onehot[0:N_BUCKETS + 1, :], a["bucket_rows"]).then_inc(rel_in, 16)
            sp.dma_start(relt[0:N_BUCKETS + 1, :], a["rel_rows"]).then_inc(rel_in, 16)
            stream(a["kv"], RING, KV["q"] + 1, KV_QUADS - 1, CH8)
            sp.wait_ge(brow_made, 1)
            for hd in range(HEADS):
                sp.dma_start(bass.AP(scratch.tensor, hd * P * 513, [[P * 513, 1], [513, P], [1, 512]]),
                             brow[hd:hd + 1, :].unsqueeze(1).to_broadcast([1, P, 512])).then_inc(brow_out, 16)
            sp.wait_ge(brow_out, 16 * HEADS)
            sp.dma_start(bias[:, :, :], bass.AP(scratch.tensor, P - 1, [[512, P], [P * 513, HEADS], [1, 3 * P]])
                         ).then_inc(bias_in, 16)
            ffn_weights(F6["q"], 6)
            stream(a["att"], 0, ATT["q"], ATT_QUADS, CH8)
            ffn_weights(F7["q"], 7)
            for m in range(KD):
                sp.wait_ge(h_made, 8 * 6 + m + 1)
                sp.dma_start(a["out"][:, m, :], h[:, m, N_META:T]).then_inc(stored, 16)
            sp.wait_ge(stored, 16 * KD)

        @block.tensor
        def _(pe):
            def split_product(out, parts, xh, xl, waits=None):
                last = len(parts) - 1
                for i, (slot, tile) in enumerate(parts):
                    if waits:
                        waits(i)
                    w = slice(tile * P, tile * P + P)
                    pe.matmul(out, wlo[:, slot, w], xh(i), start=(i == 0), stop=False)
                    pe.matmul(out, whi[:, slot, w], xl(i), start=False, stop=False)
                    mm = pe.matmul(out, whi[:, slot, w], xh(i), start=False, stop=(i == last))
                mm.then_inc(tile_done, 1)

            def norm_sum(src, c, ready, value):
                pe.wait_ge(ready, value)
                pe.matmul(bank[NORM][:, 0:T - c], ones, src, start=True, stop=True).then_inc(sum_made, 1)

            def k8_tile(q, k, count, b, src, c, waits=None):
                pe.wait_ge(lo_made, q * RING + k + 1)
                if count is not None:
                    pe.wait_ge(tile_read, count)
                hi, lo = src
                cut = (lambda t, i: t[:, i, c:T]) if t_wide(hi) else (lambda t, i: t[:, i, :])
                split_product(bank[b][:, 0:T - c], [(k, i) for i in range(8)],
                              lambda i: cut(hi, i), lambda i: cut(lo, i), waits)

            def t_wide(t):
                return t.shape[2] == T

            def first_tiles(q, group, src, c, ready, norm=None):
                hi, lo = src
                at_c = c if t_wide(hi) else 0

                def products(k, i):
                    out, w = bank[k][:, 0:T - c], slice(i * P, i * P + P)
                    pe.matmul(out, wlo[:, k, w], hi[:, i, at_c:], start=(i == 0), stop=False)
                    pe.matmul(out, whi[:, k, w], lo[:, i, at_c:], start=False, stop=False)
                    return pe.matmul(out, whi[:, k, w], hi[:, i, at_c:], start=False, stop=(i == 7))

                for k in range(group):
                    pe.wait_ge(lo_made, q * RING + k + 1)
                for i in range(6):
                    ready(i)
                    for k in range(group):
                        products(k, i)
                for k in range(group):
                    for i in (6, 7):
                        if k == 0:
                            ready(i)
                        mm = products(k, i)
                    mm.then_inc(tile_done, 1)
                    if norm and k == (0 if group == RING else group - 1):
                        norm()

            def inputs_ready(x):
                return lambda i: pe.wait_ge(x_lo_made, x * 8 + i + 1)

            def input_norm(x, n, c):
                return lambda: norm_sum(acc[:, c:T], c, sq_made, squares(x, n))

            def stage_tiles(q, j, x, n, src, c, tiles):
                first_tiles(q, RING, src, c, inputs_ready(x), input_norm(x, n, c))
                for t in range(RING, tiles):
                    k8_tile(q + t // RING, t % RING, j + t - 3 if t >= 7 else None, early_bank(t), src, c)

            def ffn(q, j, x, n, f, c, main_norm=True):
                group = RING if c else 2
                first_tiles(q, group, (xhi, xlo), c, inputs_ready(x), input_norm(x, n, c) if main_norm else None)
                for t in range(group, 2 * RING):
                    k8_tile(q + t // RING, t % RING, j + 4 if t == 7 else None, early_bank(t), (xhi, xlo), c)
                with pe.Fori(2, FFN_GU_QUADS) as b:
                    for k in range(RING):
                        k8_tile(b + q, k, b * RING + j + k - 3, k, (xhi, xlo), c)
                with pe.Fori(0, FFN_DOWN_QUADS) as b:
                    for m in range(2):
                        for k in (2 * m, 2 * m + 1):
                            pe.wait_ge(lo_made, (b + q + FFN_GU_QUADS) * RING + k + 1)
                        pe.wait_ge(tile_read, b * 2 + j + 2 * KF + m - 1)
                        pe.wait_ge(hid_lo_made, f * KF + KF - 2)

                        def waits(i):
                            if i >= KF - 2:
                                pe.wait_ge(hid_lo_made, f * KF + i + 1)

                        split_product(bank[4 + m][:, 0:T - c], [(2 * m + i // 11, i % 11) for i in range(KF)],
                                      lambda i: hidhi[:, i, c:T], lambda i: hidlo[:, i, c:T], waits)

            def mixer(l):
                st = layer_stage(l, 1)
                q, j, x, n = st["q"], st["j"], st["x"], st["n"]
                sources = {UQ: (lathi, latlo, 0), UKV: (lathi, latlo, 3), GB2: (xhi, xlo, 0),
                           PR: (rechi, reclo, 0), PA: (atthi, attlo, 0), OUT: (midhi, midlo, 0)}
                for step, i in MIXER:
                    if (step, i) == ("tile", 0):
                        first_tiles(q, 2, (xhi, xlo), 0, inputs_ready(x), input_norm(x, n, 0))
                    elif step == "tile" and i > 1:
                        t, parts = i, mixer_parts(i)
                        first = max([s for s in (0, *sources) if s <= t])
                        hi, lo, at_k = sources.get(first, (xhi, xlo, 0))
                        waits = None
                        if t == UQ:
                            pe.wait_ge(lat_lo, l * 5 + 3)
                        if t == UKV:
                            pe.wait_ge(lat_lo, l * 5 + 5)
                        if t == PA:
                            pe.wait_ge(att_lo, l * 4 + 4)
                        if t == PR:
                            pe.wait_ge(rec_lo, l * 4 + 4)
                        if t == OUT:
                            waits = lambda k: pe.wait_ge(mid_lo_made, l * 8 + k + 1)
                        for chunk in sorted({ch for ch, _ in parts}):
                            pe.wait_ge(lo_made, q * RING + chunk + 1)
                        if GB2 <= t < PA + 4 or t >= OUT + 2:
                            pe.wait_ge(tile_read, j + t - 1)
                        elif 4 <= t < OUT:
                            pe.wait_ge(tile_read, j + t - 3)
                        split_product(bank[mixer_bank(t)][:, 0:T], [(ch % RING, tile) for ch, tile in parts],
                                      lambda k: hi[:, at_k + k, :], lambda k: lo[:, at_k + k, :], waits)
                    elif step == "turn_v":
                        pe.wait_ge(tile_read, j + HGATE)
                        for s, (at_t, size) in enumerate(TOKEN_TILES):
                            for hd in range(HG_HEADS):
                                tr = pe.transpose(bank[4 + s][0:size, hd * P:hd * P + P],
                                                  qd0[:, hd, at_t:at_t + size], ident)
                            tr.then_inc(v_turned, 1)
                    elif step == "pairs":
                        level_products(l, i)
                    elif step == "rec_out":
                        if i == 0:
                            pe.wait_ge(level_taken, l * LEVELS + LEVELS)
                        if i >= 2:
                            pe.wait_ge(rec_taken, l * 4 + i - 1)
                        o = bank[4 + i % 2]
                        v = slice(i * P, i * P + P)
                        pe.matmul(o[:, 0:T], vtok[:, 0, v], dec0[:, i, :], start=True, stop=False)
                        pe.matmul(o[:, P:T], vtok[:, 1, v], dec1[:, i, :], start=False, stop=False)
                        pe.matmul(o[:, 2 * P:T], vtok[0:16, 2, v], dec2[0:16, i, :], start=False,
                                  stop=True).then_inc(rec_done, 1)
                    elif step == "rec_norm":
                        pe.wait_ge(rec_taken, l * 4 + i + 1)
                        if i == 0:
                            pe.wait_ge(level_taken, l * LEVELS + LEVELS)
                        else:
                            pe.wait_ge(rec_std, l * 4 + i)
                        pe.matmul(bank[6][:, 0:T], ones, suf[:, i, :], start=True, stop=True).then_inc(rec_sum, 1)
                    elif step == "latent_norm":
                        if i == 1:
                            pe.wait_ge(std_made, n + 2)
                        norm_sum(sil[:, i, :], 0, lat_sq, l * 2 + i + 1)
                    elif step == "turn_v2":
                        pe.wait_ge(tile_read, j + GB2)
                        pe.wait_ge(rec_taken, l * 4 + 4)
                        pe.wait_ge(rec_std, l * 4 + 4)
                        pe.wait_ge(rec_lo, l * 4 + 4)
                        for s, (at_t, size) in enumerate(TOKEN_TILES):
                            for m in range(4):
                                tr = pe.transpose(bank[4 + s][0:size, m * P:m * P + P],
                                                  z[:, m, at_t:at_t + size], ident)
                            tr.then_inc(v2_turned, 1)
                    elif step == "scores":
                        hd = i
                        if hd == 0:
                            pe.wait_ge(v2_taken, l * 3 + 3)
                            pe.wait_ge(qrot_made, l * 2 + 2)
                            pe.wait_ge(krot_made, l + 1)
                        if hd >= 2:
                            pe.wait_ge(max_made, l * HEADS + hd - 1)
                        if hd == 3:
                            pe.wait_ge(tail_max, l * 2 + 1)
                        for at_t, keys, out in ((0, P, bank[4 + hd % 2][:, 0:P]),
                                                (P, 2 * P, bank[4 + hd % 2][:, P:3 * P])):
                            mm = query_key(hd, at_t, P, keys, out)
                        mm.then_inc(scores_done, 1)
                    elif step == "tail_scores":
                        for hh in range(4):
                            mm = query_key(4 * i + hh, TAIL, 32, T, bank[3][32 * hh:32 * hh + 32, 0:T])
                        mm.then_inc(tail_done, 1)
                    elif step == "tail":
                        pe.wait_ge(tail_normed, l * 2 + i + 1)
                        if i == 1:
                            pe.wait_ge(probs_taken, l * HEADS + 4)
                        for k, size in enumerate((P, P, 16)):
                            tr = pe.transpose(bank[6][0:size, k * P:k * P + P], sct[:, i, k * P:k * P + size], ident)
                        tr.then_inc(tail_turned, 1)
                    elif step == "turn":
                        hd, p = i, i % 2
                        pe.wait_ge(probs_normed, l * HEADS + hd + 1)
                        if hd % 4 == 0:
                            pe.wait_ge(tail_taken, l * 2 + hd // 4 + 1)
                        if hd >= 1:
                            pe.wait_ge(probs_taken, l * HEADS + hd)
                        for k in range(3):
                            tr = pe.transpose(bank[6][:, k * P:k * P + P], sc[:, p, k * P:k * P + P], ident)
                        tr.then_inc(probs_turned, 1)
                    elif step == "attend":
                        hd, p = i, i % 2
                        pe.wait_ge(probs_taken, l * HEADS + hd + 1)
                        if hd % 2 == 0 and hd >= 4:
                            pe.wait_ge(att_lo, l * 4 + hd // 2 - 1)
                        r, g, tail = V_HEAD * (hd % 2), hd // 4, 32 * (hd % 4) + 16
                        o = PAIR_BANKS[hd // 2 % 2][r:r + V_HEAD, :]
                        v = slice(hd * V_HEAD, hd * V_HEAD + V_HEAD)
                        pe.matmul(o[:, 0:2 * P], vtok2[:, 0, v], pt[:, p, 0:2 * P], start=True, stop=False)
                        pe.matmul(o[:, P:2 * P], vtok2[:, 1, v], pt[:, p, 2 * P:3 * P], start=False, stop=False)
                        for k, rows in enumerate((P, P, 16)):
                            mm = pe.matmul(o[:, 2 * P:T], vtok2[0:rows, k, v],
                                           ptail[0:rows, g, k * P + tail:k * P + tail + 16],
                                           start=False, stop=(k == 2))
                        mm.then_inc(att_done, 1)

            def query_key(hd, at_t, size, keys, out):
                r, r2 = NOPE * (hd % 2), ROPE * (hd % 4)
                pe.matmul(out, qn[r:r + NOPE, hd // 2, at_t:at_t + size], kn[r:r + NOPE, hd // 2, 0:keys],
                          start=True, stop=False)
                return pe.matmul(out, qr[r2:r2 + ROPE, hd // 4, at_t:at_t + size], krot[r2:r2 + ROPE, 0:keys],
                                 start=False, stop=True)

            def level_products(l, i):
                pe.wait_ge(level_ready, l * LEVELS + i + 1)
                if i == 0:
                    pe.wait_ge(v_taken, l * 3 + 3)
                else:
                    pe.wait_ge(kd_ready, l * (LEVELS - 1) + i)
                    pe.wait_ge(level_taken, l * LEVELS + i)
                keys, qd = hk if i == 0 else kds[i % 2], qds[i % 2]
                for hd in range(HG_HEADS):
                    def pairs(b, col, s, t, size_s, size_t):
                        return pe.matmul(bank[b][0:size_s, col:col + size_t], keys[:, hd, s:s + size_s],
                                         qd[:, hd, t:t + size_t], start=True, stop=True)
                    if i < MASKED_LEVELS:
                        pairs(4, hd * P, 0, 0, P, P)
                        mm = pairs(5, hd * P, P, P, P, P)
                        if HALF[i] <= 8:
                            mm = pairs(6, hd * 16, 2 * P, 2 * P, 16, 16)
                    elif HALF[i] == P:
                        mm = pairs(4, hd * P, 0, P, P, P)
                    else:
                        pairs(4, hd * 16, 0, 2 * P, P, 16)
                        mm = pairs(4, 64 + hd * 16, P, 2 * P, P, 16)
                mm.then_inc(level_done, 1)

            def recurrent():
                q, j, x, n, c = (REC[k] for k in "qjxnc")
                stage_tiles(q, j, x, n, (xhi, xlo), c, 16)
                for t in range(16, 32):
                    hd, u = (t - 16) // 4, (t - 16) % 4
                    pe.wait_ge(lo_made, (q + 4 + hd // RING) * RING + hd % RING + 1)
                    pe.wait_ge(cv_lo_made, 2 * hd + 2)
                    pe.wait_ge(tile_read, j + t - 3)
                    split_product(bank[t % 4][:, 0:T - c], [(hd % RING, 2 * u + i) for i in range(2)],
                                  lambda i: cvhi[:, 2 * hd + i, :], lambda i: cvlo[:, 2 * hd + i, :])
                first_tiles(q + 5, RING, (outhi, outlo), c, lambda i: pe.wait_ge(out_lo_made, i + 1))
                for m in range(RING, KD):
                    k8_tile(q + 6, m - RING, j + 32 + 4 if m == 7 else None, early_bank(m), (outhi, outlo), c)
                norm_sum(acc[:, c:T], c, sq_made, SQUARES[n + 1])

            def keys_values():
                q, j, x, n, c = (KV[k] for k in "qjxnc")
                stage_tiles(q, j, x, n, (midhi, midlo), c, 8)
                pe.wait_ge(rel_in, 32)
                pe.wait_ge(tile_read, j + 7)
                pe.matmul(bank[6][0:HEADS, :], relt[0:N_BUCKETS + 1, :], onehot[0:N_BUCKETS + 1, :],
                          start=True, stop=True).then_inc(brow_done, 1)
                for t in range(8, 16):
                    k8_tile(q + t // RING, t % RING, j + t - 3, t % RING, (midhi, midlo), c)
                    if t >= 9:
                        turn_value(t - 9, j)
                turn_value(7, j)

            def turn_value(m, j):
                pe.wait_ge(tile_read, j + 8 + m + 1)
                if m >= 2:
                    pe.wait_ge(kv_taken, m - 1)
                for s in range(2):
                    tr = pe.transpose(bank[4 + m % 2][:, s * P:s * P + P],
                                      z[:, m % 4, N_META + s * P:N_META + s * P + P], ident)
                tr.then_inc(kv_turned, 1)

            def attention():
                q, j, x, n, c = (ATT[k] for k in "qjxnc")
                stage_tiles(q, j, x, n, (xhi, xlo), c, 8)
                pe.wait_ge(tile_read, j + 8)
                scores2(0)
                scores2(1)
                for hd in range(HEADS):
                    p = hd % 2
                    pe.wait_ge(s2_normed, hd + 1)
                    if hd >= 1:
                        pe.wait_ge(s2_taken, hd)
                    pe.transpose(bank[6][:, 0:P], sc2[:, p, 0:P], ident)
                    pe.transpose(bank[6][:, P:2 * P], sc2[:, p, P:2 * P], ident)
                    pe.transpose(bank[6][:, 2 * P:3 * P], sc2[:, p, 2 * P:3 * P], ident).then_inc(s2_turned, 1)
                    if hd + 2 < HEADS:
                        scores2(hd + 2)
                    pe.wait_ge(s2_taken, hd + 1)
                    if hd >= 2:
                        pe.wait_ge(o2_lo, hd - 1)
                    v = slice(hd * P, hd * P + P)
                    pe.matmul(bank[p][:, 0:SEQ], vt2[:, 0, v], pt2[:, p, 0:2 * P], start=True, stop=False)
                    pe.matmul(bank[p][:, P:SEQ], vt2[:, 1, v], pt2[:, p, 2 * P:3 * P], start=False,
                              stop=True).then_inc(o2_done, 1)
                pe.wait_ge(o2_lo, HEADS)
                for m in range(KD):
                    t = 8 + m
                    k8_tile(q + 2 + m // RING, m % RING, j + t - 1 if m >= 2 else None, 4 + m % 2, (midhi, midlo), c)
                norm_sum(acc[:, c:T], c, sq_made, SQUARES[n + 1])

            def scores2(hd):
                if hd >= 2:
                    pe.wait_ge(s2_max, hd - 1)
                pe.matmul(bank[4 + hd % 2][:, 0:P], q2[:, hd, 0:P], k2[:, hd, 0:P], start=True, stop=True)
                pe.matmul(bank[4 + hd % 2][:, P:3 * P], q2[:, hd, P:SEQ], k2[:, hd, :], start=True,
                          stop=True).then_inc(s2_done, 1)

            pe.wait_ge(consts_in, 16)
            with pe.Fori(0, DEPTH) as l:
                ffn(**layer_stage(l, 0))
                mixer(l)
                ffn(**layer_stage(l, 2))
            norm_sum(acc[:, :], 0, sq_made, SQUARES[10])
            post_ffn = lambda st, post: norm_sum(acc[:, N_META:T], N_META, sq_made, SQUARES[post])
            ffn(**F4)
            post_ffn(F4, 12)
            recurrent()
            ffn(**F5)
            post_ffn(F5, 16)
            keys_values()
            ffn(**F6, main_norm=False)
            post_ffn(F6, 18)
            attention()
            ffn(**F7)
            post_ffn(F7, 22)

        @block.scalar
        def _(act):
            def split_hi(q, k, cols, done):
                act.wait_ge(landed[k], (q + 1) * 16)
                if not isinstance(done, int) or done > 0:
                    act.wait_ge(tile_done, done)
                act.activation(whi[:, k, 0:cols], raw[:, k, 0:cols], ACT.Copy).then_inc(hi_made, 1)

            def norm_std(n, c, out=std, size=D_MODEL):
                act.wait_ge(sum_made, n + 1)
                act.activation(out[:, c:T], bank[NORM][:, 0:T - c], ACT.Sqrt, scale=1.0 / size,
                               bias=eps).then_inc(std_made, 1)

            def x_hi(x, k, c, to=xhi):
                at_k = bass.ds(k, 1) if not isinstance(k, int) else slice(k, k + 1)
                act.activation(to[:, at_k, c:T], h[:, at_k, c:T], ACT.Identity, scale=gain(x, k)).then_inc(x_hi_made, 1)

            def first_splits(q, j):
                for k in range(RING):
                    split_hi(q + 1, k, CH8, j + k + 1)

            def warm_sqrt():
                act.activation(warm[:, :], warm[:, :], ACT.Sqrt)

            def ffn(q, j, x, n, f, c, main_norm=True):
                def quad(b, next_cols, first=False):
                    if first:
                        first_splits(q, j)
                        if main_norm:
                            norm_std(n, c)
                    for p in range(2):
                        i = b * 2 + p
                        tile = b * RING + j + 2 * p
                        if not first:
                            split_hi(b + q + 1, 2 * p, next_cols, tile + 1)
                        act.wait_ge(tile_read, tile + 1)
                        if not first:
                            act.wait_ge(hid_made, f * KF + i - 1)
                        act.activation(sil[:, p, c:T], z[:, p, c:T], ACT.Silu).then_inc(silu_made, 1)
                        if not first:
                            split_hi(b + q + 1, 2 * p + 1, next_cols, tile + 2)
                        act.wait_ge(hid_made, f * KF + i + 1)
                        at_i = bass.ds(i, 1) if not isinstance(i, int) else slice(i, i + 1)
                        act.activation(hidhi[:, at_i, c:T], z[:, 2 + p:3 + p, c:T], ACT.Copy).then_inc(hid_hi_made, 1)

                quad(0, CH8, first=True)
                with act.Fori(1, FFN_GU_QUADS - 1) as b:
                    quad(b, CH8)
                quad(FFN_GU_QUADS - 1, CH11)

            def ffn_down(q, j, x, n, f, c, main_norm=True, tail=True):
                def quad(b, next_cols):
                    for p in range(2):
                        done = b * 2 + j + 2 * KF + p + 1
                        if in_layers(c):
                            act.wait_ge(tile_read, done)
                            x_hi(x + 1, b * 2 + p, c)
                        if next_cols:
                            for k in (2 * p, 2 * p + 1):
                                split_hi(b + q + FFN_GU_QUADS + 1, k, next_cols, done)

                with act.Fori(0, FFN_DOWN_QUADS - 1) as b:
                    quad(b, CH11)
                quad(FFN_DOWN_QUADS - 1, CH8 if tail else 0)
                if not in_layers(c):
                    warm_sqrt()

            def in_layers(c):
                return c == 0

            def mixer(l):
                st = layer_stage(l, 1)
                q, j, x, n = st["q"], st["j"], st["x"], st["n"]
                for step, i in MIXER:
                    if step == "tile":
                        t = i
                        read = j + t + 1
                        if t == 0:
                            norm_std(n, 0)
                        if 0 < t < OUT:
                            mixer_splits(t, q, j)
                        if t == UKV:
                            rec_high(l, 3)
                        if t < HQ:
                            act.wait_ge(tile_read, read)
                            act.activation(pre[:, t, :], z[:, t % 4, :], ACT.Sigmoid)
                            act.activation(hk[:, t, :], z[:, t % 4, :], ACT.Sigmoid, scale=-1.0).then_inc(act_took, 1)
                        elif t in TAKEN and not CQ <= t < KPE:
                            act.wait_ge(tile_read, read)
                            if t < HI:
                                act.activation(hq[:, t - HQ, :], z[:, t % 4, :], ACT.Silu).then_inc(act_took, 1)
                            elif t < GA:
                                act.activation(gate[:, t - HGATE, :], z[:, t % 4, :], ACT.Silu).then_inc(act_took, 1)
                            else:
                                to = (sga[:, t - GA, :] if t < CQ else
                                      sgb[:, t - GB1 if t < UQ else t - GB2 + 4, :])
                                act.activation(to, z[:, t % 4, :], ACT.Tanh, scale=0.5).then_inc(act_took, 1)
                        elif CQ <= t < KPE:
                            act.wait_ge(tile_read, read)
                            act.activation(lathi[:, t - CQ, :], z[:, t % 4, :], ACT.Identity,
                                           scale=small(l, t - CQ)).then_inc(act_took, 1)
                        elif PA <= t < OUT:
                            m = t - PA
                            act.wait_ge(merged, l * 8 + m + 1)
                            act.activation(midhi[:, m, :], sga[:, m, :], ACT.Copy).then_inc(mid_hi_made, 1)
                        elif t >= OUT:
                            act.wait_ge(tile_read, read)
                            x_hi(x + 1, t - OUT, 0)
                        if not 0 < t < OUT:
                            mixer_splits(t, q, j)
                    elif step == "turn_v":
                        for s, (_, size) in enumerate(TOKEN_TILES):
                            act.wait_ge(v_turned, l * 3 + s + 1)
                            act.activation(vtok[0:size, s, :], bank[4 + s][0:size, :], ACT.Copy).then_inc(v_taken, 1)
                    elif step == "decay" and i == HG_HEADS - 1:
                        act.wait_ge(decay_made, l + 1)
                        act.activation(pre[:, :, :], pre[:, :, :], ACT.Ln).then_inc(log_made, 1)
                    elif step == "exps":
                        act.wait_ge(sums_ready, l * (LEVELS - 1) + i)
                        if i >= 2:
                            act.wait_ge(level_done, l * LEVELS + i - 1)
                        act.activation(qds[i % 2][:, :, :], pre[:, :, :], ACT.Exp)
                        act.activation(kds[i % 2][:, :, :], suf[:, :, :], ACT.Exp).then_inc(exp_made, 1)
                    elif step == "rec_out":
                        act.wait_ge(rec_done, l * 4 + i + 1)
                        act.activation(pre[:, i, :], bank[4 + i % 2][:, 0:T], ACT.Copy)
                        act.activation(suf[:, i, :], bank[4 + i % 2][:, 0:T], ACT.Square).then_inc(rec_taken, 1)
                    elif step == "rec_norm":
                        act.wait_ge(rec_sum, l * 4 + i + 1)
                        act.activation(kd0[:, i, :], bank[6][:, 0:T], ACT.Sqrt, scale=1.0 / HG_DIM,
                                       bias=eps).then_inc(rec_std, 1)
                        if i >= 1:
                            rec_high(l, i - 1)
                    elif step == "latent_norm":
                        if i == 1:
                            act.wait_ge(rstd_made, n + 2)
                        norm_std(n + 1 + i, 0, size=(Q_LORA, KV_LORA)[i])
                    elif step == "turn_v2":
                        for s, (_, size) in enumerate(TOKEN_TILES):
                            act.wait_ge(v2_turned, l * 3 + s + 1)
                            act.activation(vtok2[0:size, s, :], bank[4 + s][0:size, :], ACT.Copy).then_inc(v2_taken, 1)
                    elif step == "scores":
                        hd, p = i, i % 2
                        act.wait_ge(max_made, l * HEADS + hd + 1)
                        for e, (a0, a1) in enumerate(SCORE_ROWS):
                            last = act.activation(sc[:, p, a0:a1], sc[:, p, a0:a1], ACT.Exp,
                                                  bias=negmax[:, p, e:e + 1], accum_out=sums[:, p, e:e + 1])
                        last.then_inc(probs_made, 1)
                    elif step == "tail_scores":
                        act.wait_ge(tail_max, l * 2 + i + 1)
                        act.activation(sct[:, i, :], sct[:, i, :], ACT.Exp, bias=negmax[:, i, 2:3],
                                       accum_out=sums[:, i, 2:3]).then_inc(tail_exp, 1)
                    elif step == "tail":
                        act.wait_ge(tail_turned, l * 2 + i + 1)
                        act.activation(ptail[:, i, 0:2 * P], bank[6][:, 0:2 * P], ACT.Copy)
                        act.activation(ptail[0:16, i, 2 * P:3 * P], bank[6][0:16, 2 * P:3 * P],
                                       ACT.Copy).then_inc(tail_taken, 1)
                    elif step == "turn":
                        hd, p = i, i % 2
                        act.wait_ge(probs_turned, l * HEADS + hd + 1)
                        if hd >= 2:
                            act.wait_ge(att_done, l * HEADS + hd - 1)
                        act.activation(pt[:, p, :], bank[6][:, 0:3 * P], ACT.Copy).then_inc(probs_taken, 1)
                    elif step == "attend":
                        hd = i
                        if hd % 2 == 1:
                            act.wait_ge(att_done, l * HEADS + hd + 1)
                            act.activation(atthi[:, hd // 2, :], PAIR_BANKS[hd // 2 % 2][:, 0:T], ACT.Copy).then_inc(att_hi, 1)

            def mixer_splits(t, q, j):
                for ch in chunks_ended(t):
                    split_hi(q + (ch + RING) // RING, ch % RING, CH8, j + t + 1)

            def rec_high(l, hd):
                act.wait_ge(rec_f, l * 4 + hd + 1)
                act.activation(rechi[:, hd, :], pre[:, hd, :], ACT.Copy).then_inc(rec_hi, 1)

            def small(l, k):
                return vec[:, bass.ds(l * 6 + VEC["small"] + k, 1)]

            def inputs_from_h(x, u, c, to=xhi):
                for k in range(KD):
                    act.wait_ge(h_made, 8 * (u - 7) + k + 1)
                    x_hi(x, k, c, to)

            def recurrent():
                q, j, x, n, c = (REC[k] for k in "qjxnc")
                first_splits(q, j)
                norm_std(n, c)
                for t in range(16):
                    if t >= RING:
                        split_hi(q + 1 + t // RING, t % RING, CH8, j + t + 1)
                    act.wait_ge(tile_read, j + t + 1)
                    m = t % 8
                    if t < 8:
                        if m >= 2:
                            act.wait_ge(conv_made, m - 1)
                        else:
                            act.wait_ge(xb_made, 1)
                        act.activation(xb[:, m % 2, 3:], z[:, t % 4, c:T], ACT.Identity, bias=vcol("b_in", m))
                        act.drain()
                        act.activation(cv[:, m, :], xb[:, m % 2, 3:], ACT.Identity, scale=vcol("conv_w", 24 + m),
                                       bias=vcol("conv_b", m)).then_inc(conv_begun, 1)
                        if m >= 1:
                            conv_hi(m - 1)
                    else:
                        if m == 0:
                            conv_hi(7)
                        act.activation(yg[:, m, :], z[:, t % 4, c:T], ACT.Gelu_apprx_tanh,
                                       bias=vcol("b_in", 8 + m)).then_inc(b_act_took, 1)
                for t in range(16, 32):
                    hd, u = (t - 16) // 4, (t - 16) % 4
                    to = (sr, si)[u // 2]
                    act.wait_ge(tile_read, j + t + 1)
                    act.activation(to[:, 2 * hd + u % 2, :], z[:, t % 4, c:T], ACT.Sigmoid).then_inc(b_act_took, 1)
                    if u == 3:
                        split_hi(q + 5 + hd // RING, hd % RING, CH8, j + t + 1)
                act.drain()
                act.wait_ge(coef_made, 1)
                for m in range(KD):
                    act.activation(y[:, m, 0:SEQ], sr[:, m, :], ACT.Tanh, scale=lam[:, 0, m:m + 1])
                act.drain()
                for m in range(KD):
                    act.activation(sr[:, m, :], sr[:, m, :], ACT.Exp, scale=lam[:, 0, m:m + 1]).then_inc(decay2_made, 1)
                for m in range(KD):
                    act.wait_ge(root_asked, m + 1)
                    act.activation(y[:, m, 0:SEQ], y[:, m, 0:SEQ], ACT.Sqrt, scale=-1.0).then_inc(root_made, 1)
                for m in range(KD):
                    act.wait_ge(out_f, m + 1)
                    act.activation(outhi[:, m, :], yg[:, m, :], ACT.Copy).then_inc(out_hi_made, 1)
                for m in range(KD):
                    split_hi(q + 6 + m // RING, m % RING, CH8, j + 32 + m + 1)
                norm_std(n + 1, c)
                inputs_from_h(9, 9, c)

            def conv_hi(m):
                act.wait_ge(conv_made, m + 1)
                act.activation(cvhi[:, m, :], cv[:, m, :], ACT.Copy).then_inc(cv_hi_made, 1)

            def keys_values():
                q, j, x, n, c = (KV[k] for k in "qjxnc")
                first_splits(q, j)
                norm_std(n, c)
                for t in range(16):
                    if t >= RING:
                        split_hi(q + 1 + t // RING, t % RING, CH8, j + t + 1)
                    if t == 7:
                        act.wait_ge(brow_done, 1)
                        act.activation(brow[0:HEADS, :], bank[6][0:HEADS, :], ACT.Copy).then_inc(brow_made, 1)
                    if t < 8:
                        x_hi(11, t, c)
                    if t >= 9:
                        value_out(t - 9)
                value_out(7)

            def value_out(m):
                act.wait_ge(kv_turned, m + 1)
                act.activation(vt2[:, :, m * P:m * P + P],
                               bank[4 + m % 2][:, 0:2 * P].rearrange("p (s d) -> p s d", s=2), ACT.Copy
                               ).then_inc(kv_taken, 1)

            def attention():
                q, j, x, n, c = (ATT[k] for k in "qjxnc")
                first_splits(q, j)
                norm_std(n, c)
                for t in range(RING, 8):
                    split_hi(q + 1 + t // RING, t % RING, CH8, j + t + 1)

                def exponentials(hd):
                    p = hd % 2
                    act.wait_ge(s2_max, hd + 1)
                    for e, (a0, a1) in enumerate(SCORE_ROWS):
                        last = act.activation(sc2[:, p, a0:a1], sc2[:, p, a0:a1], ACT.Exp,
                                              bias=negmax[:, p, e:e + 1], accum_out=sums[:, p, e:e + 1])
                    last.then_inc(s2_exp, 1)

                exponentials(0)
                exponentials(1)
                for hd in range(HEADS):
                    p = hd % 2
                    act.wait_ge(s2_turned, hd + 1)
                    if hd >= 2:
                        act.wait_ge(o2_done, hd - 1)
                    act.activation(pt2[:, p, :], bank[6][:, 0:3 * P], ACT.Copy).then_inc(s2_taken, 1)
                    if hd + 2 < HEADS:
                        exponentials(hd + 2)
                    act.wait_ge(o2_done, hd + 1)
                    act.activation(midhi[:, hd, c:T], bank[p][:, 0:SEQ], ACT.Copy).then_inc(o2_hi, 1)
                for m in range(KD):
                    split_hi(q + 3 + m // RING, m % RING, CH8, j + 8 + m + 1)
                warm_sqrt()
                norm_std(n + 1, c)
                inputs_from_h(13, 12, c)

            act.wait_ge(vec_in, 16)
            for k in range(KD):
                if k % 4 == 0:
                    act.wait_ge(h_in[k // 4], 16)
                x_hi(0, k, 0)
            for k in range(RING):
                split_hi(0, k, CH8, 0)
            act.wait_ge(consts_in, 16)
            act.activation(warm[:, :], eps, ACT.Copy)
            act.wait_ge(lb_asked, 1)
            act.activation(lb[:, 2, :], lb[:, 2, :], ACT.Exp).then_inc(lb_exp, 1)
            act.wait_ge(lam_asked, 1)
            act.activation(lam[:, 1, :], lam[:, 1, :], ACT.Exp).then_inc(lam_step, 1)
            act.wait_ge(lam_asked, 2)
            act.activation(lam[:, 3, :], lam[:, 2, :], ACT.Ln).then_inc(lam_step, 1)
            with act.Fori(0, DEPTH) as l:
                ffn(**layer_stage(l, 0))
                ffn_down(**layer_stage(l, 0))
                mixer(l)
                ffn(**layer_stage(l, 2))
                ffn_down(**layer_stage(l, 2))
            norm_std(10, 0)
            inputs_from_h(7, 7, N_META)
            ffn(**F4)
            ffn_down(**F4)
            norm_std(12, N_META)
            inputs_from_h(8, 8, N_META)
            recurrent()
            ffn(**F5)
            ffn_down(**F5)
            norm_std(16, N_META)
            inputs_from_h(10, 10, N_META, midhi)
            keys_values()
            ffn(**F6, main_norm=False)
            ffn_down(**F6)
            norm_std(18, N_META)
            inputs_from_h(12, 11, N_META)
            attention()
            ffn(**F7)
            ffn_down(**F7, tail=False)
            norm_std(22, N_META)

        @block.vector
        def _(dve):
            def split_lo(q, k, cols):
                dve.wait_ge(hi_made, q * RING + k + 1)
                dve.tensor_tensor(wlo[:, k, 0:cols], raw[:, k, 0:cols], whi[:, k, 0:cols].bitcast(F32),
                                  ALU.subtract).then_inc(lo_made, 1)

            def norm_rstd(n, c, to=rstd):
                dve.wait_ge(std_made, n + 1)
                dve.reciprocal(to[:, c:T], std[:, c:T]).then_inc(rstd_made, 1)
                dve.drain()

            def x_lo(x, k, c, to=xlo, hi=xhi):
                at_k = bass.ds(k, 1) if not isinstance(k, int) else slice(k, k + 1)
                dve.wait_ge(x_hi_made, x * 8 + k + 1)
                dve.scalar_tensor_tensor(to[:, at_k, c:T], h[:, at_k, c:T], gain(x, k),
                                         hi[:, at_k, c:T].bitcast(F32), ALU.mult, ALU.subtract).then_inc(x_lo_made, 1)

            def first_splits(q):
                for k in range(RING):
                    split_lo(q + 1, k, CH8)

            def ffn(q, j, x, n, f, c, main_norm=True):
                def quad(b, next_cols, first=False, banks=(0, 1, 2, 3)):
                    if first:
                        first_splits(q)
                        if main_norm:
                            norm_rstd(n, c)
                    for p in range(2):
                        i = b * 2 + p
                        tile = b * RING + j + 2 * p
                        dve.wait_ge(tile_done, tile + 1)
                        if not first:
                            dve.wait_ge(silu_made, f * KF + i - 1)
                        dve.tensor_tensor(z[:, p, c:T], bank[banks[2 * p]][:, 0:T - c], rstd[:, c:T],
                                          ALU.mult).then_inc(tile_read, 1)
                        if not first:
                            split_lo(b + q + 1, 2 * p, next_cols)
                        dve.wait_ge(tile_done, tile + 2)
                        if not first:
                            dve.wait_ge(hid_lo_made, f * KF + i - 1)
                        dve.tensor_tensor(z[:, 2 + p, c:T], bank[banks[2 * p + 1]][:, 0:T - c], rstd[:, c:T],
                                          ALU.mult).then_inc(tile_read, 1)
                        if not first:
                            split_lo(b + q + 1, 2 * p + 1, next_cols)

                quad(0, CH8, first=True)
                quad(1, CH8, banks=(4, 5, 6, 3))
                with dve.Fori(2, FFN_GU_QUADS - 1) as b:
                    quad(b, CH8)
                quad(FFN_GU_QUADS - 1, CH11)

            def ffn_down(q, j, x, n, f, c, main_norm=True, tail=True):
                def quad(b, next_cols):
                    for p in range(2):
                        m = b * 2 + p
                        at_m = bass.ds(m, 1) if not isinstance(m, int) else slice(m, m + 1)
                        dve.wait_ge(tile_done, m + j + 2 * KF + 1)
                        if c == 0:
                            dve.scalar_tensor_tensor(h[:, at_m, c:T], bank[4 + p][:, 0:T - c].unsqueeze(1), 0.5,
                                                     h[:, at_m, c:T], ALU.mult, ALU.add).then_inc(tile_read, 1)
                        else:
                            dve.tensor_copy(y[:, at_m, c:T], bank[4 + p][:, 0:T - c].unsqueeze(1)).then_inc(tile_read, 1)
                        if c == 0:
                            x_lo(x + 1, m, c)
                        if next_cols:
                            split_lo(b + q + FFN_GU_QUADS + 1, 2 * p, next_cols)
                            split_lo(b + q + FFN_GU_QUADS + 1, 2 * p + 1, next_cols)

                with dve.Fori(0, FFN_DOWN_QUADS - 1) as b:
                    quad(b, CH11)
                quad(FFN_DOWN_QUADS - 1, CH8 if tail else 0)

            def mixer(l):
                st = layer_stage(l, 1)
                q, j, x, n = st["q"], st["j"], st["x"], st["n"]

                def tile(t):
                    b = bank[mixer_bank(t)][:, 0:T]
                    dve.wait_ge(tile_done, j + t + 1)
                    if t == 0:
                        norm_rstd(n, 0)
                    z_free(t)
                    if t < HI or HGATE <= t < UQ or GB2 <= t < PR:
                        dve.tensor_tensor(z[:, t % 4, :], b, rstd[:, :], ALU.mult).then_inc(tile_read, 1)
                        if CQ < t <= KPE:
                            latent_lo(t - 1)
                        if t == KPS:
                            dve.drain()
                            dve.tensor_tensor(z[:, KPE % 4, :], z[:, KPE % 4, :], const("cos", T), ALU.mult)
                            dve.tensor_tensor(z[:, KPS % 4, :], z[:, KPS % 4, :], const("sin", T), ALU.mult)
                            dve.drain()
                            dve.tensor_tensor(krot[:, :], z[:, KPE % 4, :], z[:, KPS % 4, :],
                                              ALU.add).then_inc(krot_made, 1)
                    elif t < HGATE:
                        dve.tensor_tensor(qd0[:, t - HI, :], b, rstd[:, :], ALU.mult).then_inc(tile_read, 1)
                    elif t < UKV:
                        m = t - UQ
                        to = qn[:, m, :] if m < 4 else qr[:, m - 4, :] if m < 6 else z[:, t % 4, :]
                        dve.scalar_tensor_tensor(to, b, QK_SCALE, rlat[:, 0, :], ALU.mult, ALU.mult
                                                 ).then_inc(tile_read, 1)
                        if m >= 6:
                            dve.drain()
                            dve.tensor_tensor(z[:, t % 4, :], z[:, t % 4, :], const("sin", T), ALU.mult)
                            dve.tensor_tensor(qr[:, m - 6, :], qr[:, m - 6, :], const("cos", T), ALU.mult)
                            dve.drain()
                            dve.tensor_tensor(qr[:, m - 6, :], qr[:, m - 6, :], z[:, t % 4, :],
                                              ALU.add).then_inc(qrot_made, 1)
                    elif t < GB2:
                        m = t - UKV
                        to = kn[:, m, :] if m < 4 else z[:, m - 4, :]
                        dve.tensor_tensor(to, b, rlat[:, 1, :], ALU.mult).then_inc(tile_read, 1)
                    elif t < PA:
                        m = t - PR
                        if m == 0:
                            dve.wait_ge(act_took, (l + 1) * len(TAKEN))
                        dve.scalar_tensor_tensor(sgb[:, m, :], sgb[:, m, :], 1.0, b, ALU.add, ALU.mult
                                                 ).then_inc(tile_read, 1)
                    elif t < OUT:
                        m = t - PA
                        dve.scalar_tensor_tensor(sga[:, m, :], sga[:, m, :], 1.0, b, ALU.add, ALU.mult
                                                 ).then_inc(tile_read, 1)
                        dve.drain()
                        dve.tensor_tensor(sga[:, m, :], sga[:, m, :], sgb[:, m, :], ALU.add).then_inc(merged, 1)
                    else:
                        m = t - OUT
                        dve.scalar_tensor_tensor(h[:, m, :], b, 0.5, h[:, m, :], ALU.mult, ALU.add
                                                 ).then_inc(tile_read, 1)
                        x_lo(x + 1, m, 0)
                    for ch in chunks_ended(t):
                        split_lo(q + (ch + RING) // RING, ch % RING, CH8)

                def z_free(t):
                    before = Z_BEFORE.get(t)
                    if before in TAKEN:
                        dve.wait_ge(act_took, l * len(TAKEN) + taken(before))
                    if before is not None and CQ <= before < KPE:
                        dve.wait_ge(lat_z, l * 5 + before - CQ + 1)
                    if before is not None and UKV <= before < GB2:
                        dve.wait_ge(v2_turned, l * 3 + 3)

                def latent_lo(t):
                    dve.wait_ge(act_took, l * len(TAKEN) + taken(t))
                    dve.scalar_tensor_tensor(latlo[:, t - CQ, :], z[:, t % 4, :], small(l, t - CQ),
                                             lathi[:, t - CQ, :].bitcast(F32), ALU.mult, ALU.subtract
                                             ).then_inc(lat_lo, 1)

                def decay(hd):
                    dve.wait_ge(act_took, l * len(TAKEN) + hd + 1)
                    col = bass.ds(l * HG_HEADS + hd, 1)
                    dve.tensor_scalar(pre[:, hd, :], pre[:, hd, :], one_lb[:, col], lbs[:, col], ALU.mult, ALU.add)
                    dve.tensor_scalar(hk[:, hd, :], hk[:, hd, :], one_lb[:, col], None, ALU.mult)
                    dve.drain()
                    dve.tensor_scalar(pre[:, hd, :], pre[:, hd, :], F_MIN, None, ALU.max)
                    dve.drain()
                    dve.tensor_scalar(suf[:, hd, :], pre[:, hd, :], LN_SPLIT, 1.0 / LN_SPLIT - 1.0, ALU.is_lt, ALU.mult)
                    dve.drain()
                    last = dve.scalar_tensor_tensor(pre[:, hd, :], suf[:, hd, :], 1.0, pre[:, hd, :], ALU.add, ALU.mult)
                    if hd == HG_HEADS - 1:
                        last.then_inc(decay_made, 1)

                def log_decay():
                    dve.wait_ge(log_made, l + 1)
                    dve.scalar_tensor_tensor(flat(pre), flat(suf), -LN_SHIFT * LN_SPLIT, flat(pre), ALU.mult, ALU.add)
                    dve.drain()
                    dve.memset(suf[:, :, :], 0.0).then_inc(sums_ready, 1)

                def level(i):
                    qd = qds[i % 2]
                    if i == 0:
                        dve.wait_ge(act_took, l * len(TAKEN) + taken(HQ + 3))
                        dve.wait_ge(v_turned, l * 3 + 3)
                        dve.tensor_scalar(qd[:, :, :], hq[:, :, :], HG_SCALE, None, ALU.mult).then_inc(level_ready, 1)
                        return
                    dve.wait_ge(exp_made, l * (LEVELS - 1) + i)
                    dve.scalar_tensor_tensor(flat(qd), flat(qd), HG_SCALE, flat(hq), ALU.mult, ALU.mult
                                             ).then_inc(level_ready, 1)
                    if i < LEVELS - 1:
                        half = HALF[i]
                        if half <= 8:
                            cut = lambda b: flat(b).rearrange("p (b two m) -> p b two m", two=2, m=half)
                            first, second = (lambda v: v[:, :, 0, :]), (lambda v: v[:, :, 1, :])
                            end = lambda v, side: v[:, :, side, half - 1:half]
                        else:
                            cut = lambda b: b[:, :, 0:2 * P].rearrange("p h (b two m) -> p h b two m", two=2, m=half)
                            first, second = (lambda v: v[:, :, :, 0, :]), (lambda v: v[:, :, :, 1, :])
                            end = lambda v, side: v[:, :, :, side, half - 1:half]
                        vs, vp = cut(suf), cut(pre)
                        dve.tensor_tensor(first(vs), first(vs), end(vp, 1).to_broadcast(list(first(vs).shape)), ALU.add)
                        dve.drain()
                        dve.tensor_tensor(second(vp), second(vp), end(vp, 0).to_broadcast(list(second(vp).shape)),
                                          ALU.add).then_inc(sums_ready, 1)

                def take(i):
                    if i == 0:
                        dve.wait_ge(cleared, l + 1)
                    dve.wait_ge(level_done, l * LEVELS + i + 1)
                    dve.memset(idle[:, :], 0.0)
                    by_head = lambda b, size: bank[b][:, 0:4 * size].rearrange("p (h t) -> p h t", h=4)
                    if i < MASKED_LEVELS:
                        mask = masks[:, i, :].unsqueeze(1).to_broadcast([P, 4, P])
                        if HALF[i] <= 8:
                            dve.copy_predicated(dec2[0:16, :, :], masks[0:16, i, 0:16].unsqueeze(1).to_broadcast([16, 4, 16]),
                                                by_head(6, 16)[0:16])
                        dve.copy_predicated(dec0[:, :, 0:P], mask, by_head(4, P))
                        dve.copy_predicated(dec1[:, :, 0:P], mask, by_head(5, P)).then_inc(level_taken, 1)
                    elif HALF[i] == P:
                        dve.tensor_copy(dec0[:, :, P:2 * P], by_head(4, P)).then_inc(level_taken, 1)
                    else:
                        dve.tensor_copy(dec0[:, :, 2 * P:T], by_head(4, 16))
                        dve.tensor_copy(dec1[:, :, P:P + 16],
                                        bank[4][:, 64:128].rearrange("p (h t) -> p h t", h=4)).then_inc(level_taken, 1)

                def scores(hd):
                    p = hd % 2
                    dve.wait_ge(scores_done, l * HEADS + hd + 1)
                    if hd >= 2:
                        dve.wait_ge(probs_turned, l * HEADS + hd - 1)
                    dve.tensor_tensor(sc[:, p, :], bank[4 + p][:, 0:3 * P], const("causal", 3 * P), ALU.add)
                    dve.drain()
                    for e, (a0, a1) in enumerate(SCORE_ROWS):
                        last = dve.tensor_reduce(negmax[:, p, e:e + 1], sc[:, p, a0:a1], AX_X, ALU.max, negate=True)
                    last.then_inc(max_made, 1)

                def tail_scores(g):
                    dve.wait_ge(tail_done, l * 2 + g + 1)
                    dve.tensor_tensor(sct[:, g, :], bank[3][:, 0:T], const("causal_tail", T), ALU.add)
                    dve.drain()
                    dve.tensor_reduce(negmax[:, g, 2:3], sct[:, g, :], AX_X, ALU.max, negate=True).then_inc(tail_max, 1)

                def tail(g):
                    dve.wait_ge(tail_exp, l * 2 + g + 1)
                    dve.reciprocal(sums[:, g, 2:3], sums[:, g, 2:3])
                    dve.drain()
                    dve.tensor_scalar(sct[:, g, :], sct[:, g, :], sums[:, g, 2:3], None, ALU.mult
                                      ).then_inc(tail_normed, 1)

                def normalize(hd):
                    p = hd % 2
                    dve.wait_ge(probs_made, l * HEADS + hd + 1)
                    dve.reciprocal(sums[:, p, 0:2], sums[:, p, 0:2])
                    dve.drain()
                    for e, (a0, a1) in enumerate(SCORE_ROWS):
                        last = dve.tensor_scalar(sc[:, p, a0:a1], sc[:, p, a0:a1], sums[:, p, e:e + 1], None, ALU.mult)
                    last.then_inc(probs_normed, 1)
                    if hd % 2 == 0 and hd >= 2:
                        pair_lo(hd // 2 - 1)

                def pair_lo(pair):
                    dve.wait_ge(att_hi, l * 4 + pair + 1)
                    dve.tensor_tensor(attlo[:, pair, :], PAIR_BANKS[pair % 2][:, 0:T], atthi[:, pair, :].bitcast(F32),
                                      ALU.subtract).then_inc(att_lo, 1)

                for step, i in MIXER:
                    if step == "tile":
                        if i == PA:
                            pair_lo(3)
                        tile(i)
                    elif step == "decay":
                        decay(i)
                    elif step == "log_decay":
                        log_decay()
                    elif step == "level":
                        level(i)
                    elif step == "take":
                        take(i)
                    elif step == "rec_norm":
                        dve.wait_ge(rec_std, l * 4 + i + 1)
                        dve.reciprocal(kd0[:, i, :], kd0[:, i, :])
                        dve.drain()
                        dve.scalar_tensor_tensor(pre[:, i, :], pre[:, i, :], small(l, 5), kd0[:, i, :],
                                                 ALU.mult, ALU.mult)
                        dve.drain()
                        dve.tensor_tensor(pre[:, i, :], pre[:, i, :], gate[:, i, :], ALU.mult).then_inc(rec_f, 1)
                    elif step == "latent_norm":
                        norm_rstd(n + 1 + i, 0, rlat[:, i, :])
                    elif step == "scores":
                        scores(i)
                    elif step == "tail_scores":
                        tail_scores(i)
                    elif step == "tail":
                        tail(i)
                    elif step == "norm":
                        normalize(i)

            def flat(b):
                return b[:, :, :].rearrange("p h t -> p (h t)")

            def small(l, k):
                return vec[:, bass.ds(l * 6 + VEC["small"] + k, 1)]

            def update(n, post, weight, x=None, to=xlo, hi=xhi, c=N_META):
                def scaled(k):
                    dve.scalar_tensor_tensor(y[:, k, c:T], y[:, k, c:T], vcol(*post(k)), rstd[:, c:T],
                                             ALU.mult, ALU.mult)

                norm_rstd(n, c)
                scaled(0)
                for k in range(KD):
                    dve.drain()
                    dve.scalar_tensor_tensor(h[:, k, c:T], y[:, k, c:T], weight, h[:, k, c:T],
                                             ALU.mult, ALU.add).then_inc(h_made, 1)
                    if k + 1 < KD:
                        scaled(k + 1)
                    if x is not None and k >= 1:
                        x_lo(x, k - 1, c, to, hi)
                if x is not None:
                    x_lo(x, KD - 1, c, to, hi)

            def recurrent():
                q, j, x, n, c = (REC[k] for k in "qjxnc")

                def conv(m):
                    dve.wait_ge(conv_begun, m + 1)
                    for tap in range(3):
                        op = dve.scalar_tensor_tensor(cv[:, m, :], xb[:, m % 2, tap:tap + SEQ],
                                                      vcol("conv_w", 8 * tap + m), cv[:, m, :], ALU.mult, ALU.add)
                        if tap < 2:
                            dve.drain()
                    op.then_inc(conv_made, 1)

                dve.wait_ge(tile_done, j)
                dve.memset(xb[:, :, 0:3], 0.0).then_inc(xb_made, 1)
                first_splits(q)
                norm_rstd(n, c)
                for t in range(32):
                    dve.wait_ge(tile_done, j + t + 1)
                    if 4 <= t < 12:
                        dve.wait_ge(conv_begun, t - 3)
                    elif t >= 12:
                        dve.wait_ge(b_act_took, t - 11)
                    if t < 16:
                        dve.tensor_tensor(z[:, t % 4, c:T], bank[early_bank(t)][:, 0:SEQ], rstd[:, c:T],
                                          ALU.mult).then_inc(tile_read, 1)
                        if 1 <= t <= 8:
                            conv(t - 1)
                    else:
                        hd, u = (t - 16) // 4, (t - 16) % 4
                        dve.tensor_scalar(z[:, t % 4, c:T], bank[t % 4][:, 0:SEQ],
                                          vcol(("b_r", "b_i")[u // 2], 2 * hd + u % 2), None,
                                          ALU.add).then_inc(tile_read, 1)
                    if RING <= t < 16:
                        split_lo(q + 1 + t // RING, t % RING, CH8)
                    elif t >= 16 and (t - 16) % 4 == 3:
                        split_lo(q + 5, (t - 16) // 4, CH8)
                for m in range(KD):
                    dve.wait_ge(decay2_made, m + 1)
                    dve.tensor_tensor(q2[:, m, :], sr[:, m, :], sr[:, m, :], ALU.mult)
                    dve.drain()
                    dve.scalar_tensor_tensor(y[:, m, 0:SEQ], q2[:, m, :], 1.0, y[:, m, 0:SEQ],
                                             ALU.add, ALU.mult).then_inc(root_asked, 1)
                for m in range(KD):
                    dve.wait_ge(gated_made, m + 1)
                    dve.wait_ge(root_made, m + 1)
                    dve.tensor_tensor(si[:, m, :], si[:, m, :], y[:, m, 0:SEQ], ALU.mult)
                    dve.drain()
                    dve.tensor_tensor_scan(cv[:, m, :], sr[:, m, :], si[:, m, :], 0.0, ALU.mult, ALU.add
                                           ).then_inc(scan_made, 1)
                for m in range(KD):
                    dve.wait_ge(tile_done, j + 32 + m + 1)
                    dve.tensor_scalar(y[:, m, c:T], bank[early_bank(m)][:, 0:SEQ], vcol("b_out", m), None,
                                      ALU.add).then_inc(tile_read, 1)
                    split_lo(q + 6 + m // RING, m % RING, CH8)

            def keys_values():
                q, j, x, n, c = (KV[k] for k in "qjxnc")
                first_splits(q)
                norm_rstd(n, c)
                for t in range(16):
                    dve.wait_ge(tile_done, j + t + 1)
                    if t >= 12:
                        dve.wait_ge(kv_turned, t - 11)
                    to = k2[:, t, :] if t < 8 else z[:, t % 4, c:T]
                    dve.tensor_tensor(to, bank[early_bank(t)][:, 0:SEQ], rstd[:, c:T], ALU.mult).then_inc(tile_read, 1)
                    if t < 8:
                        x_lo(11, t, c)
                    if t >= RING:
                        split_lo(q + 1 + t // RING, t % RING, CH8)

            def attention():
                q, j, x, n, c = (ATT[k] for k in "qjxnc")
                first_splits(q)
                norm_rstd(n, c)
                for t in range(8):
                    dve.wait_ge(tile_done, j + t + 1)
                    dve.scalar_tensor_tensor(q2[:, t, :], bank[early_bank(t)][:, 0:SEQ], MOBA_SCALE, rstd[:, c:T],
                                             ALU.mult, ALU.mult).then_inc(tile_read, 1)
                    if t >= RING:
                        split_lo(q + 1 + t // RING, t % RING, CH8)

                def scores(hd):
                    p = hd % 2
                    dve.wait_ge(s2_done, hd + 1)
                    if hd >= 2:
                        dve.wait_ge(s2_turned, hd - 1)
                    dve.tensor_tensor(sc2[:, p, 0:P], bank[4 + p][:, 0:P], bias[:, hd, P:2 * P], ALU.add)
                    dve.tensor_tensor(sc2[:, p, P:3 * P], bank[4 + p][:, P:3 * P], bias[:, hd, 0:2 * P], ALU.add)
                    dve.drain()
                    dve.tensor_reduce(negmax[:, p, 0:1], sc2[:, p, 0:P], AX_X, ALU.max, negate=True)
                    dve.tensor_reduce(negmax[:, p, 1:2], sc2[:, p, P:3 * P], AX_X, ALU.max,
                                      negate=True).then_inc(s2_max, 1)

                dve.wait_ge(bias_in, 16)
                scores(0)
                scores(1)
                for hd in range(HEADS):
                    p = hd % 2
                    dve.wait_ge(s2_exp, hd + 1)
                    dve.reciprocal(sums[:, p, 0:2], sums[:, p, 0:2])
                    dve.drain()
                    dve.tensor_scalar(sc2[:, p, 0:P], sc2[:, p, 0:P], sums[:, p, 0:1], None, ALU.mult)
                    dve.tensor_scalar(sc2[:, p, P:3 * P], sc2[:, p, P:3 * P], sums[:, p, 1:2], None,
                                      ALU.mult).then_inc(s2_normed, 1)
                    if hd + 2 < HEADS:
                        scores(hd + 2)
                    if hd >= 1:
                        out_lo(hd - 1, c)
                out_lo(7, c)
                for m in range(KD):
                    dve.wait_ge(tile_done, j + 8 + m + 1)
                    dve.tensor_copy(y[:, m, c:T], bank[4 + m % 2][:, 0:SEQ]).then_inc(tile_read, 1)
                    split_lo(q + 3 + m // RING, m % RING, CH8)

            def out_lo(hd, c):
                dve.wait_ge(o2_hi, hd + 1)
                dve.tensor_tensor(midlo[:, hd, c:T], bank[hd % 2][:, 0:SEQ], midhi[:, hd, c:T].bitcast(F32),
                                  ALU.subtract).then_inc(o2_lo, 1)

            dve.wait_ge(vec_in, 16)
            for k in range(KD):
                if k % 4 == 0:
                    dve.wait_ge(h_in[k // 4], 16)
                x_lo(0, k, 0)
            for k in range(RING):
                split_lo(0, k, CH8)
            r0, r1 = vec[:, VEC["lb_raw"]:VEC["lb_raw"] + 4], vec[:, VEC["lb_raw"] + 4:VEC["lb_raw"] + 8]
            dve.tensor_tensor(lb[:, 3, 0:4], r0, r1, ALU.max)
            dve.drain()
            dve.tensor_tensor(lb[:, 2, 0:4], r0, lb[:, 3, 0:4], ALU.subtract)
            dve.tensor_tensor(lb[:, 2, 4:8], r1, lb[:, 3, 0:4], ALU.subtract).then_inc(lb_asked, 1)
            dve.wait_ge(lb_exp, 1)
            dve.tensor_tensor(lb[:, 3, 0:4], lb[:, 2, 0:4], lb[:, 2, 4:8], ALU.add)
            dve.drain()
            dve.reciprocal(lb[:, 3, 0:4], lb[:, 3, 0:4])
            dve.drain()
            for s in range(2):
                dve.tensor_tensor(lb[:, 2, 4 * s:4 * s + 4], lb[:, 2, 4 * s:4 * s + 4], lb[:, 3, 0:4], ALU.mult)
            dve.drain()
            dve.tensor_tensor(lbs[:, 0:4], lb[:, 2, 0:4], lb[:, 2, 0:4], ALU.subtract)
            dve.tensor_tensor(lb[:, 3, 0:4], lb[:, 2, 0:4], lb[:, 2, 4:8], ALU.add)
            dve.drain()
            dve.tensor_tensor(lbs[:, 4:8], lb[:, 3, 0:4], lb[:, 2, 0:4], ALU.subtract)
            dve.drain()
            dve.tensor_scalar(one_lb[:, :], lbs[:, :], -1.0, 1.0, ALU.mult, ALU.add)
            raw_lam = vec[:, VEC["lam"]:VEC["lam"] + KD]
            neg_abs, u1, ln_u, coef = lam[:, 1, :], lam[:, 2, :], lam[:, 3, :], lam[:, 0, :]
            dve.tensor_scalar(coef, raw_lam, -1.0, None, ALU.mult)
            dve.drain()
            dve.tensor_tensor(neg_abs, coef, raw_lam, ALU.min).then_inc(lam_asked, 1)
            dve.wait_ge(lam_step, 1)
            dve.tensor_scalar(u1, neg_abs, 1.0, None, ALU.add).then_inc(lam_asked, 1)
            dve.tensor_scalar(coef, coef, 0.0, None, ALU.max)
            dve.wait_ge(lam_step, 2)
            tmp, same = lb[:, 2, :], lb[:, 3, :]
            dve.drain()
            dve.tensor_scalar(tmp, u1, 1.0, TINY, ALU.subtract, ALU.max)
            dve.tensor_scalar(same, u1, 1.0, None, ALU.is_equal)
            dve.drain()
            dve.reciprocal(tmp, tmp)
            dve.tensor_tensor(same, same, neg_abs, ALU.mult)
            dve.tensor_tensor(ln_u, ln_u, neg_abs, ALU.mult)
            dve.drain()
            dve.tensor_tensor(ln_u, ln_u, tmp, ALU.mult)
            dve.tensor_tensor(coef, coef, same, ALU.add)
            dve.drain()
            dve.tensor_tensor(coef, coef, ln_u, ALU.add)
            dve.drain()
            dve.tensor_scalar(coef, coef, -LRU_C, None, ALU.mult).then_inc(coef_made, 1)
            dve.wait_ge(masks_in, 16)
            dve.tensor_copy(masks[:, :, :].rearrange("p l t -> p (l t)"), gate_flat)
            with dve.Fori(0, DEPTH) as l:
                ffn(**layer_stage(l, 0))
                ffn_down(**layer_stage(l, 0))
                mixer(l)
                ffn(**layer_stage(l, 2))
                ffn_down(**layer_stage(l, 2))
            c = N_META
            norm_rstd(10, 0)
            for k in range(KD):
                dve.scalar_tensor_tensor(h[:, k, c:T], h[:, k, c:T], norm_gain(6, k), rstd[:, c:T],
                                         ALU.mult, ALU.mult).then_inc(h_made, 1)
                if k >= 1:
                    x_lo(7, k - 1, c)
            x_lo(7, KD - 1, c)
            ffn(**F4)
            ffn_down(**F4)
            update(12, lambda k: ("ffn_post", k), 0.5, 8)
            recurrent()
            update(14, lambda k: ("mix_post", k), 1.0, 9)
            ffn(**F5)
            ffn_down(**F5)
            update(16, lambda k: ("ffn_post", 8 + k), 0.5, 10, midlo, midhi)
            keys_values()
            ffn(**F6, main_norm=False)
            ffn_down(**F6)
            update(18, lambda k: ("ffn_post", 16 + k), 0.5, 12)
            attention()
            update(20, lambda k: ("mix_post", 8 + k), 1.0, 13)
            ffn(**F7)
            ffn_down(**F7, tail=False)
            update(22, lambda k: ("ffn_post", 24 + k), 0.5)

        @block.gpsimd
        def _(pool):
            def squares_of(src, c, last_sum, ready):
                pool.wait_ge(sum_made, last_sum)
                for k in range(KD):
                    ready(k)
                    pool.tensor_tensor((sqt[:, k % 2, c:T] if k else acc[:, c:T]), src[:, k, c:T], src[:, k, c:T], ALU.mult)
                    pool.drain()
                    if k:
                        op = pool.tensor_tensor(acc[:, c:T], acc[:, c:T], sqt[:, k % 2, c:T], ALU.add)
                op.then_inc(sq_made, 1)

            def of_update(u, last_sum):
                squares_of(h, N_META, last_sum, lambda k: pool.wait_ge(h_made, 8 * (u - 7) + k + 1))

            def of_branch(j, last_sum):
                squares_of(y, N_META, last_sum, lambda k: pool.wait_ge(tile_read, j + k + 1))

            def ffn(q, j, x, n, f, c, main_norm=True):
                with pool.Fori(0, KF // 2) as b:
                    for p in range(2):
                        i = b * 2 + p
                        pool.wait_ge(silu_made, f * KF + i + 1)
                        pool.wait_ge(tile_read, b * RING + j + 2 * p + 2)
                        pool.tensor_tensor(z[:, 2 + p, c:T], sil[:, p, c:T], z[:, 2 + p, c:T],
                                           ALU.mult).then_inc(hid_made, 1)
                        pool.wait_ge(hid_hi_made, f * KF + i + 1)
                        at_i = bass.ds(i, 1)
                        pool.tensor_tensor(hidlo[:, at_i, c:T], z[:, 2 + p:3 + p, c:T],
                                           hidhi[:, at_i, c:T].bitcast(F32), ALU.subtract).then_inc(hid_lo_made, 1)

            def mixer(l):
                st = layer_stage(l, 1)
                j, n = st["j"], st["n"]
                for b in (dec0, dec1):
                    pool.memset(b[:, :, :], 0.0)
                pool.memset(dec2[:, :, :], 0.0).then_inc(cleared, 1)
                for step, i in MIXER:
                    if step == "tile" and CQ <= i < KPE:
                        which, first = (0, i == CQ) if i < CKV else (1, i == CKV)
                        pool.wait_ge(tile_read, j + i + 1)
                        dst = sil[:, which, :] if first else sqt[:, i % 2, :]
                        pool.tensor_tensor(dst, z[:, i % 4, :], z[:, i % 4, :], ALU.mult).then_inc(lat_z, 1)
                        pool.drain()
                        if not first:
                            op = pool.tensor_tensor(sil[:, which, :], sil[:, which, :], sqt[:, i % 2, :], ALU.add)
                            if i in (CKV - 1, KPE - 1):
                                op.then_inc(lat_sq, 1)
                    elif step == "level" and i >= 1:
                        pool.wait_ge(exp_made, l * (LEVELS - 1) + i)
                        kd = kds[i % 2]
                        pool.tensor_tensor(kd[:, :, :], kd[:, :, :], hk[:, :, :], ALU.mult).then_inc(kd_ready, 1)
                    elif step == "rec_norm":
                        pool.wait_ge(rec_hi, l * 4 + i + 1)
                        pool.tensor_tensor(reclo[:, i, :], pre[:, i, :], rechi[:, i, :].bitcast(F32),
                                           ALU.subtract).then_inc(rec_lo, 1)
                    elif step == "tile" and PA <= i < OUT:
                        m = i - PA
                        pool.wait_ge(mid_hi_made, l * 8 + m + 1)
                        pool.tensor_tensor(midlo[:, m, :], sga[:, m, :], midhi[:, m, :].bitcast(F32),
                                           ALU.subtract).then_inc(mid_lo_made, 1)
                squares_of(h, 0, n + 1, lambda k: pool.wait_ge(tile_read, j + OUT + k + 1))

            def of_layer(st):
                squares_of(h, 0, st["n"] + 1, lambda k: pool.wait_ge(tile_read, st["j"] + 2 * KF + k + 1))

            for k in range(KD):
                if k % 4 == 0:
                    pool.wait_ge(h_in[k // 4], 16)
                pool.tensor_tensor((sqt[:, k % 2, :] if k else acc[:, :]), h[:, k, :], h[:, k, :], ALU.mult)
                pool.drain()
                if k:
                    op = pool.tensor_tensor(acc[:, :], acc[:, :], sqt[:, k % 2, :], ALU.add)
            op.then_inc(sq_made, 1)
            with pool.Fori(0, DEPTH) as l:
                ffn(**layer_stage(l, 0))
                of_layer(layer_stage(l, 0))
                mixer(l)
                ffn(**layer_stage(l, 2))
                of_layer(layer_stage(l, 2))
            of_update(7, 11)
            ffn(**F4)
            of_branch(F4["j"] + 2 * KF, 12)
            of_update(8, 13)
            for m in range(KD):
                pool.wait_ge(cv_hi_made, m + 1)
                pool.tensor_tensor(cvlo[:, m, :], cv[:, m, :], cvhi[:, m, :].bitcast(F32),
                                   ALU.subtract).then_inc(cv_lo_made, 1)
            for m in range(KD):
                pool.wait_ge(b_act_took, 8 + 4 * (m // 2) + 3 + m % 2)
                pool.tensor_tensor(si[:, m, :], si[:, m, :], cv[:, m, :], ALU.mult).then_inc(gated_made, 1)

            def out_low(m):
                pool.wait_ge(out_hi_made, m + 1)
                pool.tensor_tensor(outlo[:, m, :], yg[:, m, :], outhi[:, m, :].bitcast(F32),
                                   ALU.subtract).then_inc(out_lo_made, 1)

            for m in range(KD):
                pool.wait_ge(scan_made, m + 1)
                pool.tensor_tensor(yg[:, m, :], yg[:, m, :], cv[:, m, :], ALU.mult).then_inc(out_f, 1)
                if m >= 1:
                    out_low(m - 1)
            out_low(KD - 1)
            of_branch(REC["j"] + 32, 14)
            of_update(9, 15)
            ffn(**F5)
            of_branch(F5["j"] + 2 * KF, 16)
            of_update(10, 17)
            ffn(**F6)
            of_branch(F6["j"] + 2 * KF, 18)
            of_update(11, 19)
            of_branch(ATT["j"] + 8, 20)
            of_update(12, 21)
            ffn(**F7)
            of_branch(F7["j"] + 2 * KF, 22)


def pad_to(a, width):
    return np.concatenate([a, np.zeros((a.shape[0], width - a.shape[1]), a.dtype)], 1)


def feature_columns(v):
    return v.reshape(-1, P).T


def mixer_weights(w_in, w_uq, w_ukv, w_pa, w_pr, w_out):
    sizes = (Q_LORA, KV_LORA, ROPE, 512, 512, 512, 512, D_MODEL, D_MODEL)
    cq, ckv, kpe, hq, hf, hi, hg, ga, gb = np.split(w_in, np.cumsum(sizes)[:-1], 1)
    swap = np.r_[ROPE // 2:ROPE, 0:ROPE // 2]
    first = np.concatenate([hf, hq, hi, hg, ga, cq, ckv, np.tile(kpe, (1, 4)), np.tile(kpe[:, swap], (1, 4)),
                            gb[:, :4 * P]], 1)
    q = w_uq.reshape(Q_LORA, HEADS, NOPE + ROPE)
    nope, rope = q[:, :, :NOPE], q[:, :, NOPE:]
    uq = np.concatenate([t.reshape(Q_LORA, -1) for t in (nope, rope, rope[:, :, swap])], 1)
    kv = w_ukv.reshape(KV_LORA, HEADS, NOPE + V_HEAD)
    ukv = np.concatenate([kv[:, :, :NOPE].reshape(KV_LORA, -1), kv[:, :, NOPE:].reshape(KV_LORA, -1)], 1)
    return np.concatenate([k8(first), k_few(uq), k_few(ukv), k8(gb[:, 4 * P:]), k_few(w_pr), k_few(w_pa), k8(w_out)])


def pairs(gate, up):
    d = gate.shape[0]
    return np.stack([gate.reshape(d, KF, P), up.reshape(d, KF, P)], 2).reshape(d, -1)


def lay_out(i):
    gu, down = [], []
    for l in range(DEPTH):
        for n in ("ffn1", "ffn2"):
            w = i[n + "_w_gu"][l]
            gu.append(k8(pairs(w[:, :D_FF], w[:, D_FF:])))
            down.append(down_chunks(i[n + "_w_down"][l]))
    for l in range(DEPTH):
        for n in ("ffn1", "ffn2"):
            gu.append(k8(pairs(i[n + "_w_gate_2"][l], i[n + "_w_up_2"][l])))
            down.append(down_chunks(i[n + "_w_down_2"][l]))
    x = np.concatenate([i["meta_tokens"], i["x"][0]], 0)
    norms = [i[n][l] for l in range(DEPTH) for n in ("ffn1_norm", "mix_norm", "ffn2_norm")] + [i["final_norm"]]
    small = [v for l in range(DEPTH) for v in (i["q_norm"][l], i["kv_norm"][l], i["hg_norm"][l])]
    by_ffn = lambda n: [i[f"{f}_{n}_2"][l] for l in range(DEPTH) for f in ("ffn1", "ffn2")]
    vectors = norms + small + [i["hg_lb_raw"]] + by_ffn("pre_g") + by_ffn("post_g") + [
        i["mix_pre_g_2"], i["mix_post_g_2"], i["kv_norm_g_2"], i["lru_b_in_2"][0], i["lru_conv_w_2"][0],
        i["lru_conv_b_2"][0], i["lru_b_r_2"][0], i["lru_b_i_2"][0], i["lru_lambda_2"][0], i["lru_b_out_2"][0]]
    consts, masks, bucket_rows = constants()
    heads = [k_few(np.concatenate([i["lru_w_r_2"][0, n], i["lru_w_i_2"][0, n]], 1)) for n in range(4)]
    return {
        "h0": np.ascontiguousarray(x.T.reshape(KD, P, T).transpose(1, 0, 2)),
        "vectors": np.ascontiguousarray(np.concatenate([feature_columns(v) for v in vectors], 1)),
        "consts": consts,
        "masks": masks,
        "bucket_rows": bucket_rows,
        "rel_rows": np.concatenate([i["rel_bias_2"].T, np.full((1, HEADS), NEG_BIG, np.float32)], 0),
        "ffn_gu": np.concatenate(gu),
        "ffn_down": np.concatenate(down),
        "mix": np.concatenate([mixer_weights(i["w_in"][l], i["w_uq"][l], i["w_ukv"][l], i["w_proj_attn"][l],
                                             i["w_proj_rec"][l], i["w_out"][l]) for l in range(DEPTH)]),
        "rec": np.concatenate([k8(i["lru_w_in_2"][0])] + heads + [k8(i["lru_w_out_2"][0])]),
        "kv": k8(i["w_kv_2"]),
        "att": np.concatenate([k8(i["attn_w_q_2"][0]), k8(i["attn_w_o_2"][0])]),
    }


def kernel(**inputs):
    import concourse.bacc as bacc
    from concourse.bass_utils import run_bass_kernel_spmd

    arrays = lay_out({n: np.asarray(v) for n, v in inputs.items()})
    nc = bacc.Bacc("TRN2", target_bir_lowering=False, num_devices=1)
    aps = {n: nc.dram_tensor(n, v.shape, mybir.dt.from_np(v.dtype), kind="ExternalInput").ap()
           for n, v in arrays.items()}
    aps["out"] = nc.dram_tensor("out", (P, KD, SEQ), F32, kind="ExternalOutput").ap()
    program(nc, aps)
    got = run_bass_kernel_spmd(nc, [arrays], core_ids=[0]).results[0]["out"]
    return np.ascontiguousarray(got.transpose(2, 1, 0)).reshape(1, SEQ, D_MODEL)
```
